# Optimizing a Trainium2 kernel written in Bass

```python
import math
import jax, jax.numpy as jnp
from jax import lax
import numpy as np

D_MODEL = 1024
BATCH = 1
SEQ = 2048
DEPTH = 1

CHUNK = 64
EPS = 1e-6
NEG = -1e30
A_HEADS = 8
A_KV_HEADS = 2
A_HEAD_DIM = 64
A_WINDOW = 128
A_WIN_CHUNKS = A_WINDOW // CHUNK
B_HEADS = 8
B_HEAD_DIM = 64
B_KV_RANK = 128
IDX_HEADS = 8
IDX_DIM = 64
TOPK_MAX = 256
Q_BLOCK = 128
REL_BUCKETS = 32
REL_MAX_DIST = 128
N_BIAS_HEADS = A_HEADS + B_HEADS
D_FF = ((-(-8 * D_MODEL // 3)) + 255) // 256 * 256

A_Q_W = A_HEADS * A_HEAD_DIM
A_KV_W = A_KV_HEADS * A_HEAD_DIM
B_Q_W = B_HEADS * B_HEAD_DIM
IDX_Q_W = IDX_HEADS * IDX_DIM
SPLITS = [A_Q_W, A_KV_W, A_KV_W, B_Q_W, B_KV_RANK, IDX_Q_W, IDX_DIM, IDX_HEADS, D_MODEL, D_MODEL]
D_IN = sum(SPLITS)

kernel_name = "hybrid_swa_sink_dsa_gated_trunk"

def _rmsnorm(x, g):
    x32 = x.astype(jnp.float32)
    y = x32 * lax.rsqrt(jnp.mean(x32 * x32, axis=-1, keepdims=True) + EPS)
    return y.astype(x.dtype) * g

def _t5_bucket(rel):
    nb = REL_BUCKETS // 2
    max_exact = nb // 2
    ret = jnp.where(rel > 0, nb, 0)
    n = jnp.abs(rel)
    nf = jnp.maximum(n, 1).astype(jnp.float32)
    large = max_exact + (jnp.log(nf / max_exact) / math.log(REL_MAX_DIST / max_exact)
                         * (nb - max_exact)).astype(jnp.int32)
    large = jnp.minimum(large, nb - 1)
    return (ret + jnp.where(n < max_exact, n, large)).astype(jnp.int32)

def _split_cols(p):
    offs = np.cumsum(SPLITS)[:-1].tolist()
    return jnp.split(p, offs, axis=-1)

def _mixer_a(q, k, v, sinks, rel_bias_a):
    b, s = q.shape[0], q.shape[1]
    nc = s // CHUNK
    g, r, d = A_KV_HEADS, A_HEADS // A_KV_HEADS, A_HEAD_DIM
    n_prev = A_WIN_CHUNKS - 1
    band = A_WIN_CHUNKS * CHUNK
    qc = q.reshape(b, nc, CHUNK, g, r, d)
    kc = k.reshape(b, nc, CHUNK, g, d)
    vc = v.reshape(b, nc, CHUNK, g, d)

    def shifted(t, p):
        return jnp.pad(t, ((0, 0), (p, 0), (0, 0), (0, 0), (0, 0)))[:, :nc]

    kb = jnp.concatenate([shifted(kc, p) for p in range(n_prev, 0, -1)] + [kc], axis=2)
    vb = jnp.concatenate([shifted(vc, p) for p in range(n_prev, 0, -1)] + [vc], axis=2)

    logits = jnp.einsum('bcqgrd,bckgd->bcgrqk', qc, kb).astype(jnp.float32) * (d ** -0.5)
    j = jnp.arange(band)
    i = jnp.arange(CHUNK)
    rel = (j[None, :] - n_prev * CHUNK) - i[:, None]
    bias = rel_bias_a[_t5_bucket(rel)].astype(jnp.float32)
    bias = jnp.transpose(bias, (2, 0, 1)).reshape(g, r, CHUNK, band)
    key_chunk_off = j // CHUNK - n_prev
    valid = (jnp.arange(nc)[:, None] + key_chunk_off[None, :]) >= 0
    logits = jnp.where(valid[None, :, None, None, None, :], logits + bias[None, None], NEG)
    sink = jnp.broadcast_to(sinks.astype(jnp.float32).reshape(1, 1, g, r, 1, 1),
                            logits.shape[:-1] + (1,))
    p = jax.nn.softmax(jnp.concatenate([logits, sink], axis=-1), axis=-1)[..., :-1]
    o = jnp.einsum('bcgrqk,bckgd->bcqgrd', p.astype(vb.dtype), vb)
    return o.reshape(b, s, A_HEADS * d)

def _mixer_b(q, k, v, q_idx, k_idx, w_idx, rel_bias_b):
    b, s = q.shape[0], q.shape[1]
    n_sel = min(TOPK_MAX, s // 4)
    nqb = s // Q_BLOCK
    kpos = jnp.arange(s)

    def to_blocks(t):
        return jnp.moveaxis(t.reshape((b, nqb, Q_BLOCK) + t.shape[2:]), 1, 0)

    def block(args):
        qb, qib, wb, start = args
        qpos = start + jnp.arange(Q_BLOCK)
        adm = (kpos[None, :] // CHUNK) <= (qpos[:, None] // CHUNK)
        isc = jnp.einsum('bqhd,bsd->bqhs', qib, k_idx).astype(jnp.float32) * (IDX_DIM ** -0.5)
        score = jnp.einsum('bqhs,bqh->bqs', jax.nn.relu(isc),
                           wb.astype(jnp.float32) * (IDX_HEADS ** -0.5))
        score = jnp.where(adm[None], score, NEG)
        _, idx = lax.top_k(score, n_sel)
        k_sel = jax.vmap(lambda kk, ii: kk[ii])(k, idx)
        v_sel = jax.vmap(lambda vv, ii: vv[ii])(v, idx)
        valid = (idx // CHUNK) <= (qpos[None, :, None] // CHUNK)
        bias = rel_bias_b[_t5_bucket(idx - qpos[None, :, None])]
        logits = jnp.einsum('bqhd,bqkd->bqhk', qb, k_sel).astype(jnp.float32) * (B_HEAD_DIM ** -0.5)
        logits = logits + jnp.transpose(bias, (0, 1, 3, 2)).astype(jnp.float32)
        logits = jnp.where(valid[:, :, None, :], logits, NEG)
        p = jax.nn.softmax(logits, axis=-1)
        return jnp.einsum('bqhk,bqkd->bqhd', p.astype(v_sel.dtype), v_sel)

    starts = jnp.arange(nqb, dtype=jnp.int32) * Q_BLOCK
    o = lax.map(block, (to_blocks(q), to_blocks(q_idx), to_blocks(w_idx), starts))
    return jnp.moveaxis(o, 0, 1).reshape(b, s, B_HEADS * B_HEAD_DIM)

def setup_inputs(seed: int = 0) -> dict:
    key = jax.random.key(seed)
    ks = jax.random.split(key, 20)
    f32 = jnp.float32

    def nrm(k, shape, scale):
        return jax.random.normal(k, shape, f32) * scale

    def gain(k, shape):
        return 1.0 + 0.02 * jax.random.normal(k, shape, f32)

    return {
        "x": jax.random.normal(ks[0], (BATCH, SEQ, D_MODEL), f32),
        "norm1_g": gain(ks[1], (DEPTH, D_MODEL)),
        "w_in": nrm(ks[2], (DEPTH, D_MODEL, D_IN), D_MODEL ** -0.5),
        "rel_bias": nrm(ks[3], (REL_BUCKETS, N_BIAS_HEADS), 0.5),
        "sinks": nrm(ks[4], (DEPTH, A_HEADS), 0.5),
        "kv_norm_g": gain(ks[5], (DEPTH, B_KV_RANK)),
        "w_uk": nrm(ks[6], (DEPTH, B_KV_RANK, B_HEAD_DIM), B_KV_RANK ** -0.5),
        "w_uv": nrm(ks[7], (DEPTH, B_KV_RANK, B_HEAD_DIM), B_KV_RANK ** -0.5),
        "w_branch_a": nrm(ks[8], (DEPTH, A_Q_W, D_MODEL), A_Q_W ** -0.5),
        "w_branch_b": nrm(ks[9], (DEPTH, B_Q_W, D_MODEL), B_Q_W ** -0.5),
        "w_out": nrm(ks[10], (DEPTH, D_MODEL, D_MODEL), D_MODEL ** -0.5),
        "norm2_g": gain(ks[11], (DEPTH, D_MODEL)),
        "w_ffn_gate": nrm(ks[12], (DEPTH, D_MODEL, D_FF), D_MODEL ** -0.5),
        "w_ffn_up": nrm(ks[13], (DEPTH, D_MODEL, D_FF), D_MODEL ** -0.5),
        "w_ffn_down": nrm(ks[14], (DEPTH, D_FF, D_MODEL), D_FF ** -0.5),
        "norm_f_g": gain(ks[15], (D_MODEL,)),
    }

def reference(x, norm1_g, w_in, rel_bias, sinks, kv_norm_g, w_uk, w_uv, w_branch_a, w_branch_b,
              w_out, norm2_g, w_ffn_gate, w_ffn_up, w_ffn_down, norm_f_g):
    b, s, _ = x.shape
    rel_bias_a = rel_bias[:, :A_HEADS]
    rel_bias_b = rel_bias[:, A_HEADS:]
    for layer in range(DEPTH):
        h = _rmsnorm(x, norm1_g[layer])
        proj = jnp.einsum('bsd,de->bse', h, w_in[layer])
        (a_q, a_k, a_v, b_q, b_lat, i_q, i_k, i_w, gate_a, gate_b) = _split_cols(proj)
        o_a = _mixer_a(a_q.reshape(b, s, A_HEADS, A_HEAD_DIM),
                       a_k.reshape(b, s, A_KV_HEADS, A_HEAD_DIM),
                       a_v.reshape(b, s, A_KV_HEADS, A_HEAD_DIM),
                       sinks[layer], rel_bias_a)
        lat = _rmsnorm(b_lat, kv_norm_g[layer])
        k_b = jnp.einsum('bsr,rd->bsd', lat, w_uk[layer])
        v_b = jnp.einsum('bsr,rd->bsd', lat, w_uv[layer])
        o_b = _mixer_b(b_q.reshape(b, s, B_HEADS, B_HEAD_DIM), k_b, v_b,
                       i_q.reshape(b, s, IDX_HEADS, IDX_DIM), i_k, i_w, rel_bias_b)
        merged = (jax.nn.sigmoid(gate_a) * jnp.einsum('bse,ed->bsd', o_a, w_branch_a[layer])
                  + jax.nn.sigmoid(gate_b) * jnp.einsum('bse,ed->bsd', o_b, w_branch_b[layer]))
        x = x + jnp.einsum('bsd,de->bse', merged, w_out[layer])
        h2 = _rmsnorm(x, norm2_g[layer])
        ff = jax.nn.silu(jnp.einsum('bsd,df->bsf', h2, w_ffn_gate[layer])) * jnp.einsum('bsd,df->bsf', h2, w_ffn_up[layer])
        x = x + jnp.einsum('bsf,fd->bsd', ff, w_ffn_down[layer])
    return _rmsnorm(x, norm_f_g)


_drawn_inputs = setup_inputs


def setup_inputs(seed=0):
    import zlib

    import numpy as np

    out = dict(_drawn_inputs(seed))
    spreads = {}
    factors = {'norm1_g': 5.125, 'sinks': 8.0, 'kv_norm_g': 8.0, 'norm2_g': 3.851, 'norm_f_g': 2.862}
    for name, (base, spread) in spreads.items():
        noise = np.random.default_rng([zlib.crc32(name.encode()), seed]).standard_normal(out[name].shape)
        drawn = base * np.exp(spread * noise) if base else spread * noise
        out[name] = __import__('jax').numpy.asarray(drawn.astype(out[name].dtype))
    for name, factor in factors.items():
        out[name] = (out[name] * factor).astype(out[name].dtype)
    return out
```

```python
import numpy as np
import concourse.bass as bass
from concourse import mybir
from contextlib import ExitStack

P = 128
ROWS = 512
JT = ROWS // P
HEADS, HD = 8, 64
KVH = 2
NEG = -1e30
EPS = 1e-6
LOWEST = -3e38
SLOTS = 8
LGW = 1024
BUCKETS, FAR_BUCKET = 32, 15
BAND = 2 * P
FTW = 384


class Count:

    def __init__(self, known):
        self.known, self.seen, self.now = known, {}, {}

    def made(self, sem, key, by=1):
        self.now[sem.name] = self.now.get(sem.name, 0) + by
        self.seen[(sem.name, key)] = self.now[sem.name]
        return by

    def n(self, sem, key):
        return self.known.get((sem.name, key), 1)


def trunk_program(nc, io, known):
    f32, f32r, bf16, i32 = mybir.dt.float32, mybir.dt.float32r, mybir.dt.bfloat16, mybir.dt.int32
    ACT, ALU = mybir.ActivationFunctionType, mybir.AluOpType
    x, out = io["x"], io["out"]
    SEQ, D = x.shape[1], x.shape[2]
    DFF = io["w_ffn_gate"].shape[2]
    NB = SEQ // ROWS
    KT = D // P
    ET = HEADS * HD // P
    FT = DFF // P
    TOPK = min(256, SEQ // 4)
    TK = TOPK // P
    PARTS = [range(a, min(a + SLOTS, FT)) for a in range(0, FT, SLOTS)]
    C = Count(known)
    n, made = C.n, C.made

    w_in = io["w_in"][0]
    COL = dict(aq=0, ak=512, av=640, bq=768, lat=1280, iq=1408, ikw=1920, gate=1992)

    with ExitStack() as ctx:
        top = (nc.sbuf_base + 63) // 64 * 64
        place = [top]

        def at(name, shape, dt, offset):
            return nc.alloc_sbuf_tensor_at(name, shape, dt, offset=offset)

        def new(name, shape, dt):
            size = int(np.prod(shape[1:])) * (2 if dt == bf16 else 4)
            offset = place[0]
            place[0] += (size + 31) // 32 * 32
            return at(name, shape, dt, offset)

        def region(size):
            offset = place[0]
            place[0] += size
            return offset

        KIhi, KIlo = new("KIhi", [P, SEQ], f32r), new("KIlo", [P, SEQ], f32r)
        KBhi, KBlo = new("KBhi", [P, SEQ], f32r), new("KBlo", [P, SEQ], f32r)
        VB = new("VB", [P, SEQ // P, P], f32r)
        AKhi, AKlo = (new(s, [P, KVH, (JT + 1) * P], f32r) for s in ("AKhi", "AKlo"))
        VA = new("VA", [P, JT + 1, KVH, P], f32r)
        TABA, TABB = new("TABA", [P, HEADS, BAND], f32), new("TABB", [P, HEADS, BAND], f32)
        IDENT, ONES = new("IDENT", [P, P], f32), new("ONES", [P, P], f32)
        WRAW = [new(f"WRAW{i}", [P, SLOTS, P], f32) for i in range(2)]
        WHI = [new(f"WHI{i}", [P, SLOTS, P], f32r) for i in range(2)]
        WLO = [new(f"WLO{i}", [P, SLOTS, P], f32r) for i in range(2)]
        WUKhi, WUKlo = new("WUKhi", [P, P], f32r), new("WUKlo", [P, P], f32r)
        WUVhi, WUVlo = new("WUVhi", [P, HD], f32r), new("WUVlo", [P, HD], f32r)
        G1, G2, GF = (new(s, [P, KT], f32) for s in ("G1", "G2", "GF"))
        GKV, SINK = new("GKV", [P, 1], f32), new("SINK", [P, HEADS], f32)
        IW = new("IW", [P, JT, HEADS], f32)
        CNT, NEED = new("CNT", [P, JT], f32), new("NEED", [P, JT], f32)
        PREF, SIGN, THR, TAKE = (new(s, [P, JT], i32) for s in ("PREF", "SIGN", "THR", "TAKE"))
        BIT = new("BIT", [P, 1], i32)
        MX, NM = new("MX", [P, 2, 2], f32), new("NM", [P, 2], f32)
        RS, ES, RR = new("RS", [P, 2, HEADS], f32), new("ES", [P, 2, HEADS], f32), new("RR", [P, 2, HEADS], f32)
        RV = new("RV", [P, ROWS], f32)
        rO, r1, rQ, rM, r3 = region(8192), region(32768), region(16384), region(16384), region(32768)
        assert place[0] <= nc.sbuf_usable_end, place[0] - nc.sbuf_usable_end
        OTA = at("OTA", [P, ET, ROWS], f32, rO)
        GS = at("GS", [P, 2, ROWS], f32, rO)
        IWT = at("IWT", [HEADS, ROWS], f32, rO)
        VAT = at("VAT", [P, ROWS], f32, rO + 4096)
        XN = at("XN", [P, JT, D], f32, r1)
        XT = at("XT", [P, KT, ROWS], f32, r1 + 16384)
        SC = at("SC", [P, JT, SEQ], f32, r1)
        LG = [at(f"LG{i}", [P, SEQ], f32, r1 + 8192 * i) for i in range(2)]
        PThi = [at(f"PThi{i}", [P, 4, P], f32r, r1 + 16384 + 2048 * i) for i in range(2)]
        PTlo = [at(f"PTlo{i}", [P, 4, P], f32r, r1 + 20480 + 2048 * i) for i in range(2)]
        ON = at("ON", [P, HEADS, HD], f32, r1 + 24576)
        OA, OB = at("OA", [P, 4, HD], f32, r1 + 26624), at("OB", [P, 4, HD], f32, r1 + 27648)
        OThi = [at(f"OThi{i}", [P, ET, ROWS], f32r, r1 + 8192 * i) for i in range(2)]
        OTlo = [at(f"OTlo{i}", [P, ET, ROWS], f32r, r1 + 16384 + 8192 * i) for i in range(2)]
        X1T = at("X1T", [P, KT, ROWS], f32, r1)
        XR = at("XR", [P, JT, D], f32, r1 + 16384)
        H2F = at("H2F", [P, KT, ROWS], f32, r1 + 16384)
        SL = at("SL", [P, 2, ROWS], f32, r1 + 16384)
        FF = at("FF", [P, 2, ROWS], f32, r1 + 16384 + 4096)
        OUTN = at("OUTN", [P, JT, D], f32, r1 + 16384)
        FTAB = at("FTAB", [P, 2 * HEADS, FTW], f32, r1)
        Q = at("Q", [P, HEADS, ROWS], f32r, rQ)
        JUNK = at("JUNK", [P, JT, SEQ], bf16, rQ)
        EQ, CS = at("EQ", [P, SEQ], f32, rQ), at("CS", [P, SEQ], f32, rQ + 8192)
        H2hi, H2lo = at("H2hi", [P, KT, ROWS], f32r, rQ), at("H2lo", [P, KT, ROWS], f32r, rM)
        SQ = at("SQ", [P, KT, ROWS], f32, rM)
        LT, LSQ = at("LT", [P, ROWS], f32, rM), at("LSQ", [P, ROWS], f32, rM + 2048)
        LThi, LTlo = at("LThi", [P, ROWS], f32r, rM + 4096), at("LTlo", [P, ROWS], f32r, rM + 6144)
        RB = at("RB", [P, 2, LGW], f32, rM)
        MASK = at("MASK", [P, JT, SEQ], bf16, rM)
        GL = at("GL", [P, 2, 2, ROWS], f32, rM)
        M1, M2 = at("M1", [P, 2, ROWS], f32, rM + 8192), at("M2", [P, 2, ROWS], f32, rM + 12288)
        HThi, HTlo = at("HThi", [P, KT, ROWS], f32r, r3), at("HTlo", [P, KT, ROWS], f32r, r3 + 16384)
        OTB = at("OTB", [P, ET, ROWS], f32, r3)
        MGhi, MGlo = at("MGhi", [P, KT, ROWS], f32r, r3), at("MGlo", [P, KT, ROWS], f32r, r3 + 16384)
        FFhi, FFlo = at("FFhi", [P, SLOTS, ROWS], f32r, r3), at("FFlo", [P, SLOTS, ROWS], f32r, r3 + 16384)
        HOT = at("HOT", [BUCKETS, 2 * FTW], f32, r3)
        RELB = at("RELB", [BUCKETS, 2 * HEADS], f32, r3 + 3072)
        BANDM = at("BANDM", [P, BAND], f32, r3 + 4096)
        WU = at("WU", [P, 2 * HD + HD], f32, r3 + 8192)

        BANK = [ctx.enter_context(nc.psum_tensor(f"BANK{i}", [P, ROWS], f32)) for i in range(2)]
        LP = [ctx.enter_context(nc.psum_tensor(f"LP{i}", [P, LGW], f32)) for i in range(2)]
        TP = [ctx.enter_context(nc.psum_tensor(f"TP{i}", [P, 4, P], f32)) for i in range(2)]

        def sem(name):
            return ctx.enter_context(nc.semaphore(name))

        const_in, ones_set = sem("const_in"), sem("ones_set")
        ftab_ready, ftab_out, taba_in, taba_ready = (sem(s) for s in ("ftab_ready", "ftab_out", "taba_in", "taba_ready"))
        wu_hi, wu_ready = sem("wu_hi"), sem("wu_ready")
        w_in_sem = [sem(f"w_loaded{i}") for i in range(2)]
        w_hi, w_split = sem("w_hi"), sem("w_split")
        bank_full, logits_full, trans_full = sem("bank_full"), sem("logits_full"), sem("trans_full")
        x_in = [sem(f"x_in{j}") for j in range(JT)]
        xr_in = [sem(f"xr_in{j}") for j in range(JT)]
        xt_ready, sq_ready = sem("xt_ready"), sem("sq_ready")
        var_ready, std_ready, rinv_ready = sem("var_ready"), sem("std_ready"), sem("rinv_ready")
        h_ready, h_hi, h_split = sem("h_ready"), sem("h_hi"), sem("h_split")
        q_hi, q_ready = sem("q_hi"), sem("q_ready")
        k_hi, k_ready, kw_ready, iw_ready = sem("k_hi"), sem("k_ready"), sem("kw_ready"), sem("iw_ready")
        lat_ready, lat_norm, lat_hi, lat_split = sem("lat_ready"), sem("lat_norm"), sem("lat_hi"), sem("lat_split")
        v_hi, v_ready, vat_ready, carried = sem("v_hi"), sem("v_ready"), sem("vat_ready"), sem("carried")
        relu_ready, score_added, score_ready = sem("relu_ready"), sem("score_added"), sem("score_ready")
        topk_step, mask_ready = sem("topk_step"), sem("mask_ready")
        gate_ready = sem("gate_ready")
        gate_out = [sem(f"gate_out{i}") for i in range(2)]
        gate_in = [sem(f"gate_in{i}") for i in range(2)]
        masked, negmax, probs, values_done = sem("masked"), sem("negmax"), sem("probs"), sem("values_done")
        pt_hi, pt_ready = sem("pt_hi"), sem("pt_ready")
        o_step, o_ready, ot_ready = sem("o_step"), sem("o_ready"), sem("ot_ready")
        oh_ready, os_ready = sem("oh_ready"), sem("os_ready")
        gated, merged, m_hi, m_split = sem("gated"), sem("merged"), sem("m_hi"), sem("m_split")
        x1_ready, x1_sq = sem("x1_ready"), sem("x1_sq")
        silu_ready, ff_ready, ff_hi, ff_split, added = (sem(s) for s in ("silu_ready", "ff_ready", "ff_hi", "ff_split", "added"))
        y_ready, outn_ready = sem("y_ready"), sem("outn_ready")
        out_done = [sem(f"out_done{j}") for j in range(JT)]

        def bank(key):
            return BANK[C.known.get(("bank use", key), 0) % 2]

        def logits(key):
            return LP[(n(logits_full, key) - 1) % 2]

        def trans(key):
            return TP[(n(trans_full, key) - 1) % 2]

        def weights(w, rows, c0, width=P):
            return w[rows[0] * P:(rows[-1] + 1) * P, c0:c0 + width].rearrange("(k p) c -> p k c", p=P)

        def proj_jobs(b, kind, tiles, width=P):
            return [((kind, b, m), weights(w_in, range(KT), COL[kind] + m * P, width)) for m in range(tiles)]

        def ffn_jobs(b, part):
            jobs = []
            for i in part:
                jobs.append((("fg", b, i), weights(io["w_ffn_gate"][0], range(KT), i * P)))
                jobs.append((("fu", b, i), weights(io["w_ffn_up"][0], range(KT), i * P)))
            for m in range(KT):
                jobs.append((("fd", b, part[0], m), weights(io["w_ffn_down"][0], part, m * P)))
            return jobs

        def jobs_of(b):
            jobs = proj_jobs(b, "iq", ET) + proj_jobs(b, "ikw", 1, HD + HEADS) + proj_jobs(b, "lat", 1)
            jobs += proj_jobs(b, "gate", 2 * KT) + proj_jobs(b, "aq", ET) + proj_jobs(b, "ak", 1)
            jobs += proj_jobs(b, "av", 1) + proj_jobs(b, "bq", ET)
            for m in range(KT):
                for s, w in enumerate(("w_branch_a", "w_branch_b")):
                    jobs.append((("br", b, m, s), weights(io[w][0], range(ET), m * P)))
            for m in range(KT):
                jobs.append((("wo", b, m), weights(io["w_out"][0], range(KT), m * P)))
            for part in PARTS:
                jobs += ffn_jobs(b, part)
            return jobs

        JOBS = [job for b in range(NB) for job in jobs_of(b)]

        def chunks(width):
            return [(c, min(LGW, width - c)) for c in range(0, width, LGW)]

        def halves(c, w):
            return [(a, min(ROWS, c + w - a)) for a in range(c, c + w, ROWS)]

        def groups(tiles):
            return [range(a, min(a + 4, tiles)) for a in range(0, tiles, 4)]

        def heads_of(b, kind):
            return [(b, kind, j, h) for j in range(JT) for h in range(HEADS)]

        def key_tiles(b, kind, j):
            t = b * JT + j
            if kind == "a":
                return (1, t) if t == 0 else (2, t - 1)
            return t + 1, 0

        def searched(b):
            return [j for j in range(JT) if b * JT + j >= TK]

        block = ctx.enter_context(nc.Block())

        @block.sync
        def _(sp):
            consts = [(IDENT[:, :], io["ident"]), (HOT[:, :], io["hot"]), (BANDM[:, :], io["band"]),
                      (RELB[:, :], io["rel_bias"]), (GKV[:, :], io["kv_norm_g"].rearrange("a p -> p a")),
                      (SINK[:, :], io["sinks"][0].partition_broadcast(P)), (WU[:, 2 * HD:3 * HD], io["w_uv"][0])]
            consts += [(WU[:, HD * i:HD * (i + 1)], io["w_uk"][0]) for i in range(2)]
            for g, name in ((G1, "norm1_g"), (G2, "norm2_g")):
                consts.append((g[:, :], io[name][0].rearrange("(k p) -> p k", p=P)))
            consts.append((GF[:, :], io["norm_f_g"].rearrange("(k p) -> p k", p=P)))
            for i, (dst, src) in enumerate(consts):
                made(const_in, i, 16)
                sp.dma_start(dst, src, allow_slow_non_contiguous=True).then_inc(const_in, 16)
            sp.wait_ge(ftab_ready, n(ftab_ready, 2 * HEADS - 1))
            ft = io["ft"]
            sp.dma_start(ft.rearrange("h p r -> p h r"), FTAB[:, :, :]).then_inc(ftab_out, 16)
            sp.wait_ge(ftab_out, 16)
            for s, tab in enumerate((TABA, TABB)):
                skew = bass.AP(ft.tensor, s * HEADS * P * FTW + P - 1, [[FTW - 1, P], [P * FTW, HEADS], [1, BAND]])
                sp.dma_start(tab[:, :, :], skew).then_inc(taba_in, 16)

            def load_x(b):
                for j in range(JT):
                    made(x_in[j], (b, 0), 16)
                    sp.dma_start(XN[:, j, :], x[0, b * ROWS + j * P:b * ROWS + (j + 1) * P, :]).then_inc(x_in[j], 16)

            load_x(0)
            for i, (key, src) in enumerate(JOBS):
                k, width = src.shape[1], src.shape[2]
                if i >= 2:
                    sp.wait_ge(w_split, i - 1)
                sp.dma_start(WRAW[i % 2][:, 0:k, 0:width], src).then_inc(w_in_sem[i % 2], 16)
                if key[0] == "iq" and key[1] and key[2] == 1:
                    b = key[1]
                    sp.wait_ge(bank_full, n(bank_full, ("yt", b - 1, JT - 1, D // ROWS - 1)))
                    load_x(b)
            for j in range(JT):
                sp.wait_ge(out_done[j], 16 * NB)

        @block.gpsimd
        def _(pool):
            for i, (key, src) in enumerate(JOBS):
                k, width = src.shape[1], src.shape[2]
                raw = WRAW[i % 2][:, 0:k, 0:width]
                hi, lo = WHI[i % 2][:, 0:k, 0:width], WLO[i % 2][:, 0:k, 0:width]
                pool.wait_ge(w_in_sem[i % 2], 16 * (i // 2 + 1))
                if i >= 2:
                    pool.wait_ge(bank_full, n(bank_full, JOBS[i - 2][0]))
                nc.gpsimd.tensor_scalar(hi, raw, 1.0, 1.0, ALU.mult, ALU.mult).then_inc(w_hi, 1)
                pool.wait_ge(w_hi, i + 1)
                nc.gpsimd.tensor_tensor(lo, raw, hi.bitcast(f32), ALU.subtract).then_inc(w_split, 1)

        @block.tensor
        def _(pe):
            releases = dict(bank=[], logits=[], trans=[])
            job_no = [0]

            def take(kind, sem_, key, use=None):
                uses = releases[kind]
                if len(uses) >= 2:
                    pe.wait_ge(uses[-2][0], n(*uses[-2]))
                C.seen[(kind + " use", use)] = len(uses)
                uses.append((sem_, key))
                return (BANK if kind == "bank" else LP if kind == "logits" else TP)[(len(uses) - 1) % 2]

            def three(dst, whi, wlo, mhi, mlo, first, last):
                nc.tensor.matmul(dst, whi, mhi, start=first, stop=False)
                nc.tensor.matmul(dst, whi, mlo, start=False, stop=False)
                return nc.tensor.matmul(dst, wlo, mhi, start=False, stop=last)

            def job(mhi, mlo, release, add=None):
                i = job_no[0]
                key, src = JOBS[i]
                job_no[0] += 1
                k, width = src.shape[1], src.shape[2]
                dst = take("bank", *release, key)[0:width, :]
                pe.wait_ge(w_split, i + 1)
                for s in range(k):
                    last = three(dst, WHI[i % 2][:, s, 0:width], WLO[i % 2][:, s, 0:width], mhi[:, s, :], mlo[:, s, :],
                                 s == 0, s == k - 1)
                if add is not None:
                    last = add(dst)
                last.then_inc(bank_full, made(bank_full, key))

            def square_sums(key, squares, release):
                dst = take("bank", *release, key)
                for k in range(squares.shape[1]):
                    last = nc.tensor.matmul(dst[:, :], ONES[:, :], squares[:, k, :], start=(k == 0),
                                            stop=(k == squares.shape[1] - 1))
                last.then_inc(bank_full, made(bank_full, key))

            pe.wait_ge(const_in, n(const_in, 11))
            for h in range(2 * HEADS):
                dst = take("bank", ftab_ready, h, ("ft", h))
                c = FTW * (h // HEADS)
                nc.tensor.matmul(dst[:, 0:FTW], RELB[:, h:h + 1].to_broadcast([BUCKETS, P]), HOT[:, c:c + FTW],
                                 start=True, stop=True).then_inc(bank_full, made(bank_full, ("ft", h)))
            pe.wait_ge(ones_set, 1)

            def attend(b, kind):
                items = heads_of(b, kind)
                outs_due = []

                def qk(item):
                    _, _, j, h = item
                    tiles, first = key_tiles(b, kind, j)
                    for c, w in chunks(tiles * P):
                        dst = take("logits", masked, (item, c))
                        for a, v in halves(c, w):
                            d = dst[:, a - c:a - c + v]
                            q = Q[:, h, j * P:(j + 1) * P]
                            if kind == "a":
                                s0 = (first - b * JT + 1) * P
                                khi, klo = (k[:, h // (HEADS // KVH), s0:s0 + v] for k in (AKhi, AKlo))
                            else:
                                khi, klo = KBhi[:, a:a + v], KBlo[:, a:a + v]
                            nc.tensor.matmul(d, q, khi, start=True, stop=False, skip_group_check=True)
                            near = []
                            if kind == "b":
                                for kt in range(max(0, tiles - 2), tiles):
                                    if a <= kt * P < a + v:
                                        near.append((kt * P - c, (kt - (tiles - 2)) * P))
                            last = nc.tensor.matmul(d, q, klo, start=False, stop=True, skip_group_check=True)
                            for at_, col in near:
                                last = nc.tensor.matmul(dst[:, at_:at_ + P], IDENT[:, :], TABB[:, h, col:col + P],
                                                        start=False, stop=True, skip_group_check=True)
                        last.then_inc(logits_full, made(logits_full, (item, c)))

                def transposes(item, grp):
                    i = items.index(item)
                    dst = take("trans", pt_ready, (item, grp[0]))
                    if grp[0] == 0:
                        pe.wait_ge(probs, n(probs, item))
                    for kt in grp:
                        last = nc.tensor.transpose(dst[:, kt - grp[0], :], LG[i % 2][:, kt * P:(kt + 1) * P], IDENT[:, :])
                    last.then_inc(trans_full, made(trans_full, (item, grp[0])))

                def pv(item, grp):
                    _, _, j, h = item
                    tiles, first = key_tiles(b, kind, j)
                    if h % 4 == 0 and grp[0] == 0:
                        pv.bank = take("bank", o_step, ("o", b, kind, j, h // 4, 2), ("o", b, kind, j, h // 4))
                    t = n(trans_full, (item, grp[0])) - 1
                    pe.wait_ge(pt_ready, n(pt_ready, (item, grp[0])))
                    dst = pv.bank[:, (h % 4) * P:(h % 4 + 1) * P]
                    for kt in grp:
                        v = VA[:, first + kt - b * JT + 1, h // (HEADS // KVH), :] if kind == "a" else VB[:, kt, :]
                        nc.tensor.matmul(dst, PThi[t % 2][:, kt - grp[0], :], v, start=(kt == 0), stop=False,
                                         skip_group_check=True)
                        last = nc.tensor.matmul(dst, PTlo[t % 2][:, kt - grp[0], :], v, start=False,
                                                stop=(kt == tiles - 1), skip_group_check=True)
                    last.then_inc(values_done, made(values_done, (item, grp[0])))

                def out_transposes(j):
                    dst = take("trans", ot_ready, (b, kind, j))
                    pe.wait_ge(o_ready, n(o_ready, (b, kind, j, 1)))
                    for e in range(ET):
                        last = nc.tensor.transpose(dst[:, e, :], ON[:, 2 * e:2 * e + 2, :].rearrange("p h d -> p (h d)"),
                                                   IDENT[:, :])
                    last.then_inc(trans_full, made(trans_full, ("on", b, kind, j)))

                qk(items[0])
                for i, item in enumerate(items):
                    if i + 1 < len(items):
                        qk(items[i + 1])
                    grps = groups(key_tiles(b, kind, item[2])[0])
                    transposes(item, grps[0])
                    for g, grp in enumerate(grps):
                        if g + 1 < len(grps):
                            transposes(item, grps[g + 1])
                        pv(item, grp)
                    if outs_due:
                        out_transposes(outs_due.pop())
                    if item[3] == HEADS - 1:
                        outs_due.append(item[2])
                out_transposes(outs_due.pop())

            for b in range(NB):
                for k in range(KT):
                    dst = take("bank", sq_ready, (b, 0, k), ("xt", b, k))
                    for j in range(JT):
                        if k == 0:
                            pe.wait_ge(x_in[j], n(x_in[j], (b, 0)))
                        last = nc.tensor.transpose(dst[:, j * P:(j + 1) * P], XN[:, j, k * P:(k + 1) * P], IDENT[:, :])
                    last.then_inc(bank_full, made(bank_full, ("xt", b, k)))
                pe.wait_ge(sq_ready, n(sq_ready, (b, 0, KT - 1)))
                square_sums(("ss", b, 0), SQ, (var_ready, (b, 0)))
                pe.wait_ge(h_split, n(h_split, (b, 0, KT - 1)))
                for m in range(ET):
                    job(HThi, HTlo, (q_ready, (b, "iq", m, 1)))
                job(HThi, HTlo, (kw_ready, b))
                job(HThi, HTlo, (lat_ready, (b, 1)))
                pe.wait_ge(lat_ready, n(lat_ready, (b, 1)))
                square_sums(("kvss", b), LSQ[:, :].rearrange("p (k r) -> p k r", k=1), (var_ready, (b, "kv")))
                pe.wait_ge(kw_ready, n(kw_ready, b))
                dst = take("bank", iw_ready, b, ("iwt", b))
                for j in range(JT):
                    last = nc.tensor.transpose(dst[:, j * HEADS:(j + 1) * HEADS], IWT[:, j * P:(j + 1) * P],
                                               IDENT[0:HEADS, 0:HEADS])
                last.then_inc(bank_full, made(bank_full, ("iwt", b)))
                pe.wait_ge(lat_split, n(lat_split, b))
                pe.wait_ge(wu_ready, 2)
                dst = take("bank", k_ready, (b, "kb", 0), ("kb", b))
                three(dst[:, :], WUKhi[:, :], WUKlo[:, :], LThi[:, :], LTlo[:, :], True, True
                      ).then_inc(bank_full, made(bank_full, ("kb", b)))
                dst = take("bank", v_ready, (b, "vb", 0), ("vb", b))
                for j in range(JT):
                    last = three(dst[:, j * HD:(j + 1) * HD], LThi[:, j * P:(j + 1) * P], LTlo[:, j * P:(j + 1) * P],
                                 WUVhi[:, :], WUVlo[:, :], True, True)
                last.then_inc(bank_full, made(bank_full, ("vb", b)))
                pe.wait_ge(q_ready, n(q_ready, (b, "iq", ET - 1, 1)))
                pe.wait_ge(k_ready, n(k_ready, (b, "ki", 1)))
                for j in searched(b):
                    for h in range(HEADS):
                        for c, w in chunks((b * JT + j + 1) * P):
                            dst = take("logits", relu_ready, (b, j, h, c))
                            for a, v in halves(c, w):
                                q = Q[:, h, j * P:(j + 1) * P]
                                nc.tensor.matmul(dst[:, a - c:a - c + v], q, KIhi[:, a:a + v], start=True, stop=False)
                                last = nc.tensor.matmul(dst[:, a - c:a - c + v], q, KIlo[:, a:a + v], start=False, stop=True)
                            last.then_inc(logits_full, made(logits_full, ("idx", b, j, h, c)))
                for m in range(2 * KT):
                    job(HThi, HTlo, (gate_ready, (b, m)))
                for m in range(ET):
                    job(HThi, HTlo, (q_ready, (b, "aq", m, 1)))
                job(HThi, HTlo, (k_ready, (b, "ak", 2 * KVH - 1)))
                job(HThi, HTlo, (vat_ready, b))
                pe.wait_ge(vat_ready, n(vat_ready, b))
                dst = take("bank", v_ready, (b, "va", 0), ("va", b))
                for j in range(JT):
                    last = nc.tensor.transpose(dst[:, j * P:(j + 1) * P], VAT[:, j * P:(j + 1) * P], IDENT[:, :])
                last.then_inc(bank_full, made(bank_full, ("va", b)))
                pe.wait_ge(q_ready, n(q_ready, (b, "aq", ET - 1, 1)))
                pe.wait_ge(k_ready, n(k_ready, (b, "ak", 2 * KVH - 1)))
                pe.wait_ge(v_ready, n(v_ready, (b, "va", 0)))
                attend(b, "a")
                for m in range(ET):
                    job(HThi, HTlo, (q_ready, (b, "bq", m, 1)))
                pe.wait_ge(q_ready, n(q_ready, (b, "bq", ET - 1, 1)))
                pe.wait_ge(k_ready, n(k_ready, (b, "kb", 0)))
                pe.wait_ge(v_ready, n(v_ready, (b, "vb", 0)))
                pe.wait_ge(taba_in, 32)
                attend(b, "b")
                pe.wait_ge(os_ready, n(os_ready, (b, 1)))
                for m in range(KT):
                    for s in range(2):
                        job(OThi[s], OTlo[s], (gated, (b, m, s)))
                pe.wait_ge(m_split, n(m_split, (b, KT - 1)))

                for m in range(KT):
                    def add_x(dst):
                        for j in range(JT):
                            if m == 0:
                                pe.wait_ge(xr_in[j], n(xr_in[j], b))
                            last = nc.tensor.matmul(dst[:, j * P:(j + 1) * P], XR[:, j, m * P:(m + 1) * P], IDENT[:, :],
                                                    start=False, stop=True, skip_group_check=True)
                        return last
                    job(MGhi, MGlo, (x1_sq, (b, m)), add_x)
                pe.wait_ge(x1_sq, n(x1_sq, (b, KT - 1)))
                square_sums(("ss", b, 1), SQ, (var_ready, (b, 1)))
                pe.wait_ge(h_split, n(h_split, (b, 1, KT - 1)))
                for part in PARTS:
                    for i in part:
                        job(H2hi, H2lo, (silu_ready, (b, i)))
                        job(H2hi, H2lo, (ff_ready, (b, i)))
                    pe.wait_ge(ff_split, n(ff_split, (b, part[-1])))
                    for m in range(KT):
                        job(FFhi, FFlo, (added, (b, part[0], m)))
                pe.wait_ge(sq_ready, n(sq_ready, (b, 2, KT - 1)))
                square_sums(("ss", b, 2), SQ, (var_ready, (b, 2)))
                for j in range(JT):
                    for half in range(D // ROWS):
                        dst = take("bank", outn_ready, (b, j, half), ("yt", b, j, half))
                        for k in range(4):
                            kk = half * 4 + k
                            if j == 0:
                                pe.wait_ge(y_ready, n(y_ready, (b, kk)))
                            last = nc.tensor.transpose(dst[:, k * P:(k + 1) * P], X1T[:, kk, j * P:(j + 1) * P], IDENT[:, :])
                        last.then_inc(bank_full, made(bank_full, ("yt", b, j, half)))

        @block.scalar
        def _(act):
            SCALE = HD ** -0.5

            def full(key):
                act.wait_ge(bank_full, n(bank_full, key))
                return bank(key)

            def root(which):
                act.wait_ge(var_ready, n(var_ready, which))
                nc.scalar.activation(RV[:, :], RV[:, :], ACT.Sqrt).then_inc(std_ready, made(std_ready, which))

            def round_h(b, s, src, dst):
                for k in range(KT):
                    act.wait_ge(h_ready, n(h_ready, (b, s, k)))
                    nc.scalar.copy(dst[:, k, :], src[:, k, :]).then_inc(h_hi, made(h_hi, (b, s, k)))

            def q_heads(b, kind, m):
                bk = full((kind, b, m))
                for s in range(2):
                    r = slice(s * HD, (s + 1) * HD)
                    nc.scalar.mul(Q[r, 2 * m + s, :], bk[r, :], SCALE).then_inc(q_hi, made(q_hi, (b, kind, m, s)))

            for h in range(2 * HEADS):
                bk = full(("ft", h))
                nc.scalar.copy(FTAB[:, h, :], bk[:, 0:FTW]).then_inc(ftab_ready, made(ftab_ready, h))
            act.wait_ge(const_in, n(const_in, 11))
            nc.scalar.copy(WUKhi[:, :], WU[:, 0:2 * HD]).then_inc(wu_hi, 1)
            nc.scalar.copy(WUVhi[:, :], WU[:, 2 * HD:3 * HD]).then_inc(wu_hi, 1)

            def attend(b, kind):
                items = heads_of(b, kind)
                ot = OTA if kind == "a" else OTB
                outs_due = []

                def exps(i):
                    item = items[i]
                    _, _, j, h = item
                    w = key_tiles(b, kind, j)[0] * P
                    act.wait_ge(negmax, n(negmax, item))
                    if kind == "a":
                        nc.scalar.activation(ES[:, j % 2, h:h + 1], SINK[:, h:h + 1], ACT.Exp, bias=NM[:, i % 2:i % 2 + 1])
                    nc.scalar.activation(LG[i % 2][:, 0:w], LG[i % 2][:, 0:w], ACT.Exp, bias=NM[:, i % 2:i % 2 + 1],
                                         accum_out=RS[:, j % 2, h:h + 1]).then_inc(probs, made(probs, item))

                exps(0)
                for i, item in enumerate(items):
                    for grp in groups(key_tiles(b, kind, item[2])[0]):
                        key = (item, grp[0])
                        t = n(trans_full, key) - 1
                        act.wait_ge(trans_full, t + 1)
                        if pt_last[t % 2] is not None:
                            act.wait_ge(values_done, n(values_done, pt_last[t % 2]))
                        pt_last[t % 2] = key
                        w = len(grp)
                        nc.scalar.copy(PThi[t % 2][:, 0:w, :], trans(key)[:, 0:w, :]).then_inc(pt_hi, made(pt_hi, key))
                    if outs_due:
                        j = outs_due.pop()
                        act.wait_ge(trans_full, n(trans_full, ("on", b, kind, j)))
                        nc.scalar.copy(ot[:, :, j * P:(j + 1) * P], trans(("on", b, kind, j))[:, :, :]
                                       ).then_inc(ot_ready, made(ot_ready, (b, kind, j)))
                    if item[3] == HEADS - 1:
                        outs_due.append(item[2])
                    if i + 1 < len(items):
                        exps(i + 1)
                j = outs_due.pop()
                act.wait_ge(trans_full, n(trans_full, ("on", b, kind, j)))
                nc.scalar.copy(ot[:, :, j * P:(j + 1) * P], trans(("on", b, kind, j))[:, :, :]
                               ).then_inc(ot_ready, made(ot_ready, (b, kind, j)))

            pt_last = [None, None]
            for b in range(NB):
                rows = slice(b * ROWS, (b + 1) * ROWS)
                if b:
                    for j in range(JT):
                        act.wait_ge(out_done[j], 16 * b)
                else:
                    act.wait_ge(ftab_out, 16)
                for k in range(KT):
                    bk = full(("xt", b, k))
                    nc.scalar.copy(XT[:, k, :], bk[:, :]).then_inc(xt_ready, made(xt_ready, (b, k)))
                    nc.scalar.activation(SQ[:, k, :], bk[:, :], ACT.Square).then_inc(sq_ready, made(sq_ready, (b, 0, k)))
                root((b, 0))
                round_h(b, 0, XT, HThi)
                for m in range(ET):
                    q_heads(b, "iq", m)
                bk = full(("ikw", b, 0))
                for s in range(2):
                    nc.scalar.copy(KIhi[s * HD:(s + 1) * HD, rows], bk[0:HD, :]).then_inc(k_hi, made(k_hi, (b, "ki", s)))
                act.wait_ge(k_ready, n(k_ready, (b, "ki", 1)))
                nc.scalar.mul(IWT[:, :], bk[HD:HD + HEADS, :], HEADS ** -0.5).then_inc(kw_ready, made(kw_ready, b))
                bk = full(("lat", b, 0))
                nc.scalar.copy(LT[:, :], bk[:, :]).then_inc(lat_ready, made(lat_ready, (b, 0)))
                nc.scalar.activation(LSQ[:, :], bk[:, :], ACT.Square).then_inc(lat_ready, made(lat_ready, (b, 1)))
                root((b, "kv"))
                act.wait_ge(lat_norm, n(lat_norm, b))
                nc.scalar.copy(LThi[:, :], LT[:, :]).then_inc(lat_hi, made(lat_hi, b))
                bk = full(("kb", b))
                nc.scalar.copy(KBhi[:, rows], bk[:, :]).then_inc(k_hi, made(k_hi, (b, "kb", 0)))
                bk = full(("vb", b))
                nc.scalar.copy(VB[:, b * JT:(b + 1) * JT, 0:HD], bk[:, 0:JT * HD].rearrange("p (j d) -> p j d", d=HD)
                               ).then_inc(v_hi, made(v_hi, (b, "vb", 0)))
                act.wait_ge(v_ready, n(v_ready, (b, "vb", 0)))
                for j in searched(b):
                    for h in range(HEADS):
                        for c, w in chunks((b * JT + j + 1) * P):
                            key = (b, j, h, c)
                            g = n(relu_ready, key) - 1
                            if g >= 2:
                                act.wait_ge(score_added, g - 1)
                            act.wait_ge(logits_full, n(logits_full, ("idx",) + key))
                            nc.scalar.activation(RB[:, g % 2, 0:w], logits(("idx",) + key)[:, 0:w], ACT.Relu
                                                 ).then_inc(relu_ready, made(relu_ready, key))
                for m in range(2 * KT):
                    bk = full(("gate", b, m))
                    g = b * KT + m // 2
                    if g >= 1:
                        act.wait_ge(gate_out[m % 2], 16 * g)
                    nc.scalar.activation(GS[:, m % 2, :], bk[:, :], ACT.Sigmoid).then_inc(gate_ready, made(gate_ready, (b, m)))
                    act.wait_ge(gate_ready, n(gate_ready, (b, m)))
                    act.dma_start(io["gates"][m], GS[:, m % 2, :]).then_inc(gate_out[m % 2], 16)
                if b:
                    nc.scalar.copy(AKhi[:, :, 0:P], AKhi[:, :, JT * P:(JT + 1) * P])
                    nc.scalar.copy(AKlo[:, :, 0:P], AKlo[:, :, JT * P:(JT + 1) * P])
                    nc.scalar.copy(VA[:, 0, :, :], VA[:, JT, :, :]).then_inc(carried, made(carried, b))
                    act.wait_ge(carried, n(carried, b))
                act.wait_ge(mask_ready, n(mask_ready, (b, JT - 1)))
                for m in range(ET):
                    q_heads(b, "aq", m)
                bk = full(("ak", b, 0))
                for g in range(KVH):
                    for s in range(2):
                        nc.scalar.copy(AKhi[s * HD:(s + 1) * HD, g, P:(JT + 1) * P], bk[g * HD:(g + 1) * HD, :]
                                       ).then_inc(k_hi, made(k_hi, (b, "ak", 2 * g + s)))
                bk = full(("av", b, 0))
                nc.scalar.copy(VAT[:, :], bk[:, :]).then_inc(vat_ready, made(vat_ready, b))
                bk = full(("va", b))
                nc.scalar.copy(VA[:, 1:JT + 1, :, 0:HD], bk[:, :].rearrange("p (j g d) -> p j g d", g=KVH, d=HD)
                               ).then_inc(v_hi, made(v_hi, (b, "va", 0)))
                for m in range(2):
                    act.wait_ge(gate_out[m], 16 * (b + 1) * KT)
                attend(b, "a")
                for m in range(ET):
                    q_heads(b, "bq", m)
                attend(b, "b")
                for s, ot in enumerate((OTA, OTB)):
                    act.wait_ge(ot_ready, n(ot_ready, (b, "b", JT - 1)))
                    nc.scalar.copy(OThi[s][:, :, :], ot[:, :, :]).then_inc(oh_ready, made(oh_ready, (b, s)))

                def load_gates(m):
                    if m >= 2:
                        act.wait_ge(gated, n(gated, (b, m - 2, 1)))
                    for s in range(2):
                        act.dma_start(GL[:, m % 2, s, :], io["gates"][s * KT + m]).then_inc(gate_in[m % 2], 16)
                        made(gate_in[m % 2], (b, m), 16)

                act.wait_ge(masked, n(masked, (heads_of(b, "b")[-1], chunks((b + 1) * ROWS)[-1][0])))
                load_gates(0)
                load_gates(1)
                for m in range(KT):
                    act.wait_ge(merged, n(merged, (b, m)))
                    nc.scalar.copy(MGhi[:, m, :], M1[:, m % 2, :]).then_inc(m_hi, made(m_hi, (b, m)))
                    if m + 2 < KT:
                        load_gates(m + 2)
                act.wait_ge(bank_full, n(bank_full, ("br", b, KT - 1, 1)))
                for j in range(JT):
                    made(xr_in[j], b, 16)
                    act.dma_start(XR[:, j, :], x[0, b * ROWS + j * P:b * ROWS + (j + 1) * P, :]).then_inc(xr_in[j], 16)
                act.wait_ge(m_split, n(m_split, (b, KT - 1)))
                for m in range(KT):
                    bk = full(("wo", b, m))
                    nc.scalar.copy(X1T[:, m, :], bk[:, :]).then_inc(x1_ready, made(x1_ready, (b, m)))
                    nc.scalar.activation(SQ[:, m, :], bk[:, :], ACT.Square).then_inc(x1_sq, made(x1_sq, (b, m)))
                root((b, 1))
                round_h(b, 1, H2F, H2hi)
                act.wait_ge(h_split, n(h_split, (b, 1, KT - 1)))
                for part in PARTS:
                    for i in part:
                        bk = full(("fg", b, i))
                        if i >= 2:
                            act.wait_ge(ff_ready, n(ff_ready, (b, i - 2)))
                        nc.scalar.activation(SL[:, i % 2, :], bk[:, :], ACT.Silu).then_inc(silu_ready, made(silu_ready, (b, i)))
                        act.wait_ge(ff_ready, n(ff_ready, (b, i)))
                        nc.scalar.copy(FFhi[:, i - part[0], :], FF[:, i % 2, :]).then_inc(ff_hi, made(ff_hi, (b, i)))
                for m in range(KT):
                    act.wait_ge(added, n(added, (b, PARTS[-1][0], m)))
                    nc.scalar.activation(SQ[:, m, :], X1T[:, m, :], ACT.Square).then_inc(sq_ready, made(sq_ready, (b, 2, m)))
                root((b, 2))
                for j in range(JT):
                    for half in range(D // ROWS):
                        bk = full(("yt", b, j, half))
                        nc.scalar.copy(OUTN[:, j, half * ROWS:(half + 1) * ROWS], bk[:, :]
                                       ).then_inc(outn_ready, made(outn_ready, (b, j, half)))
                    act.wait_ge(outn_ready, n(outn_ready, (b, j, D // ROWS - 1)))
                    act.dma_start(out[0, b * ROWS + j * P:b * ROWS + (j + 1) * P, :], OUTN[:, j, :]).then_inc(out_done[j], 16)

        @block.vector
        def _(dve):
            SCALE = HD ** -0.5

            def full(key):
                dve.wait_ge(bank_full, n(bank_full, key))
                return bank(key)

            def reciprocal_std(which, key, width):
                bk = full(key)
                nc.vector.tensor_scalar(RV[:, :], bk[:, :], 1.0 / width, EPS, ALU.mult, ALU.add
                                        ).then_inc(var_ready, made(var_ready, which))
                dve.wait_ge(std_ready, n(std_ready, which))
                nc.vector.reciprocal(RV[:, :], RV[:, :]).then_inc(rinv_ready, made(rinv_ready, which))
                dve.wait_ge(rinv_ready, n(rinv_ready, which))

            def normed(b, s, src, dst, gain, hi, lo):
                reciprocal_std((b, s), ("ss", b, s), D)
                for k in range(KT):
                    nc.vector.scalar_tensor_tensor(dst[:, k, :], src[:, k, :], gain[:, k:k + 1], RV[:, :], ALU.mult,
                                                   ALU.mult).then_inc(h_ready, made(h_ready, (b, s, k)))
                for k in range(KT):
                    dve.wait_ge(h_hi, n(h_hi, (b, s, k)))
                    nc.vector.tensor_tensor(lo[:, k, :], dst[:, k, :], hi[:, k, :].bitcast(f32), ALU.subtract
                                            ).then_inc(h_split, made(h_split, (b, s, k)))

            def q_heads(b, kind, m):
                bk = full((kind, b, m))
                for s in range(2):
                    r, o = slice(s * HD, (s + 1) * HD), slice((1 - s) * HD, (2 - s) * HD)
                    if s == 0:
                        dve.wait_ge(q_hi, n(q_hi, (b, kind, m, 1)))
                    nc.vector.scalar_tensor_tensor(Q[o, 2 * m + s, :], bk[r, :], SCALE, Q[r, 2 * m + s, :].bitcast(f32),
                                                   ALU.mult, ALU.subtract).then_inc(q_ready, made(q_ready, (b, kind, m, s)))

            nc.vector.memset(ONES[:, :], 1.0).then_inc(ones_set, 1)
            dve.wait_ge(const_in, n(const_in, 11))
            dve.wait_ge(wu_hi, 2)
            nc.vector.tensor_tensor(WUKlo[:, :], WU[:, 0:2 * HD], WUKhi[:, :].bitcast(f32), ALU.subtract).then_inc(wu_ready, 1)
            nc.vector.tensor_tensor(WUVlo[:, :], WU[:, 2 * HD:3 * HD], WUVhi[:, :].bitcast(f32), ALU.subtract
                                    ).then_inc(wu_ready, 1)
            dve.wait_ge(taba_in, 32)
            for h in range(HEADS):
                nc.vector.tensor_tensor(TABA[:, h, :], TABA[:, h, :], BANDM[:, :], ALU.add).then_inc(taba_ready, 1)

            step = [0]

            def topk(b):
                js = searched(b)
                col = slice(js[0], JT)

                def stepped(ins):
                    step[0] += 1
                    ins.then_inc(topk_step, 1)
                    return step[0]

                def count(threshold, op):
                    for j in js:
                        w = (b * JT + j + 1) * P
                        last = stepped(nc.vector.tensor_scalar(JUNK[:, j, 0:w], SC[:, j, 0:w], threshold(j), None,
                                                               op, ALU.add, accum_out=CNT[:, j:j + 1]))
                    dve.wait_ge(topk_step, last)

                count(lambda j: 0.0, ALU.is_ge)
                dve.wait_ge(topk_step, stepped(nc.vector.tensor_scalar(
                    TAKE[:, col], CNT[:, col], float(TOPK), -1.0, ALU.is_ge, ALU.add)))
                stepped(nc.vector.tensor_scalar(SIGN[:, col], TAKE[:, col], -2 ** 31, None, ALU.bitwise_or))
                stepped(nc.vector.tensor_scalar(PREF[:, col], TAKE[:, col], -1, -2 ** 31, ALU.bitwise_xor, ALU.bitwise_and))
                dve.wait_ge(topk_step, stepped(nc.vector.memset(BIT[:, :], 2 ** 30)))
                base, each = step[0], len(js) + 4
                with dve.Fori(0, 31) as it:
                    s0 = base + it * each
                    nc.vector.scalar_tensor_tensor(THR[:, col], PREF[:, col], BIT[:, 0:1], SIGN[:, col],
                                                   ALU.bitwise_or, ALU.bitwise_xor).then_inc(topk_step, 1)
                    dve.wait_ge(topk_step, s0 + 1)
                    for j in js:
                        w = (b * JT + j + 1) * P
                        nc.vector.tensor_scalar(JUNK[:, j, 0:w], SC[:, j, 0:w], THR[:, j:j + 1].bitcast(f32), None,
                                                ALU.is_ge, ALU.add, accum_out=CNT[:, j:j + 1]).then_inc(topk_step, 1)
                    dve.wait_ge(topk_step, s0 + 1 + len(js))
                    nc.vector.tensor_scalar(TAKE[:, col], CNT[:, col], float(TOPK), -1.0, ALU.is_ge, ALU.mult
                                            ).then_inc(topk_step, 1)
                    dve.wait_ge(topk_step, s0 + 2 + len(js))
                    nc.vector.scalar_tensor_tensor(PREF[:, col], TAKE[:, col], BIT[:, 0:1], PREF[:, col],
                                                   ALU.bitwise_and, ALU.bitwise_or).then_inc(topk_step, 1)
                    dve.wait_ge(topk_step, s0 + 3 + len(js))
                    nc.vector.tensor_scalar(BIT[:, :], BIT[:, :], 1, None, ALU.logical_shift_right).then_inc(topk_step, 1)
                    dve.wait_ge(topk_step, s0 + 4 + len(js))
                step[0] += 31 * each
                dve.wait_ge(topk_step, stepped(nc.vector.tensor_tensor(THR[:, col], PREF[:, col], SIGN[:, col], ALU.bitwise_xor)))
                count(lambda j: THR[:, j:j + 1].bitcast(f32), ALU.is_gt)
                dve.wait_ge(topk_step, stepped(nc.vector.tensor_scalar(
                    NEED[:, col], CNT[:, col], -1.0, float(TOPK), ALU.mult, ALU.add)))
                for j in js:
                    w = (b * JT + j + 1) * P
                    thr = THR[:, j:j + 1].bitcast(f32)
                    s, e, c = SC[:, j, 0:w], EQ[:, 0:w], CS[:, 0:w]
                    dve.wait_ge(topk_step, stepped(nc.vector.tensor_scalar(e, s, thr, None, ALU.is_equal)))
                    dve.wait_ge(topk_step, stepped(nc.vector.tensor_tensor_scan(c, e, e, 0.0, ALU.add, ALU.max)))
                    dve.wait_ge(topk_step, stepped(nc.vector.scalar_tensor_tensor(
                        e, c, NEED[:, j:j + 1], e, ALU.is_le, ALU.mult)))
                    dve.wait_ge(topk_step, stepped(nc.vector.scalar_tensor_tensor(s, s, thr, e, ALU.is_gt, ALU.add)))
                    nc.vector.tensor_scalar(MASK[:, j, 0:w], s, -1.0, -NEG, ALU.add, ALU.mult
                                            ).then_inc(mask_ready, made(mask_ready, (b, j)))

            def attend(b, kind):
                items = heads_of(b, kind)

                def mask_and_max(i):
                    item = items[i]
                    _, _, j, h = item
                    tiles, first = key_tiles(b, kind, j)
                    if i >= 2:
                        before = items[i - 2]
                        dve.wait_ge(trans_full, n(trans_full, (before, groups(key_tiles(b, kind, before[2])[0])[-1][0])))
                    for s, (c, w) in enumerate(chunks(tiles * P)):
                        if kind == "a":
                            add, start = TABA[:, h, BAND - w:BAND], SINK[:, h:h + 1]
                        else:
                            add, start = MASK[:, j, c:c + w], (MX[:, i % 2, 0:1] if s else LOWEST)
                        if s:
                            dve.wait_ge(masked, n(masked, (item, 0)))
                        dve.wait_ge(logits_full, n(logits_full, (item, c)))
                        nc.vector.tensor_tensor_reduce(
                            LG[i % 2][:, c:c + w], logits((item, c))[:, 0:w], add, 1.0, start, ALU.add, ALU.max,
                            MX[:, i % 2, s:s + 1]).then_inc(masked, made(masked, (item, c)))
                        end = (s, c)
                    dve.wait_ge(masked, n(masked, (item, end[1])))
                    nc.vector.tensor_scalar(NM[:, i % 2:i % 2 + 1], MX[:, i % 2, end[0]:end[0] + 1], -1.0, None, ALU.mult
                                            ).then_inc(negmax, made(negmax, item))

                mask_and_max(0)
                for i, item in enumerate(items):
                    _, _, j, h = item
                    if i + 1 < len(items):
                        mask_and_max(i + 1)
                    for grp in groups(key_tiles(b, kind, j)[0]):
                        key = (item, grp[0])
                        t, w = n(trans_full, key) - 1, len(grp)
                        dve.wait_ge(pt_hi, n(pt_hi, key))
                        nc.vector.tensor_tensor(PTlo[t % 2][:, 0:w, :], trans(key)[:, 0:w, :],
                                                PThi[t % 2][:, 0:w, :].bitcast(f32), ALU.subtract
                                                ).then_inc(pt_ready, made(pt_ready, key))
                    if h % 4 == 3:
                        g = h // 4
                        key = ("o", b, kind, j, g)
                        hs = slice(4 * g, 4 * g + 4)
                        p = j % 2
                        if kind == "a":
                            nc.vector.tensor_tensor(RS[:, p, hs], RS[:, p, hs], ES[:, p, hs], ALU.add
                                                    ).then_inc(o_step, made(o_step, key + (3,)))
                            dve.wait_ge(o_step, n(o_step, key + (3,)))
                        nc.vector.reciprocal(RR[:, p, hs], RS[:, p, hs]).then_inc(o_step, made(o_step, key + (0,)))
                        dve.wait_ge(o_step, n(o_step, key + (0,)))
                        dve.wait_ge(values_done, n(values_done, (item, groups(key_tiles(b, kind, j)[0])[-1][0])))
                        bk = bank(key)[:, :].rearrange("p (h d) -> p h d", h=4)
                        r = RR[:, p, hs].unsqueeze(2).to_broadcast([P, 4, HD])
                        nc.vector.tensor_tensor(OA[:, :, :], bk[:, :, 0:HD], r, ALU.mult).then_inc(o_step, made(o_step, key + (1,)))
                        nc.vector.tensor_tensor(OB[:, :, :], bk[:, :, HD:P], r, ALU.mult).then_inc(o_step, made(o_step, key + (2,)))
                        dve.wait_ge(o_step, n(o_step, key + (2,)))
                        if j >= 1:
                            dve.wait_ge(trans_full, n(trans_full, ("on", b, kind, j - 1)))
                        nc.vector.tensor_tensor(ON[:, hs, :], OA[:, :, :], OB[:, :, :], ALU.add
                                                ).then_inc(o_ready, made(o_ready, (b, kind, j, g)))
                        dve.wait_ge(o_ready, n(o_ready, (b, kind, j, g)))

            for b in range(NB):
                rows = slice(b * ROWS, (b + 1) * ROWS)
                normed(b, 0, XT, XT, G1, HThi, HTlo)
                for m in range(ET):
                    q_heads(b, "iq", m)
                bk = full(("ikw", b, 0))
                for s in range(2):
                    dve.wait_ge(k_hi, n(k_hi, (b, "ki", 1)))
                    nc.vector.tensor_tensor(KIlo[s * HD:(s + 1) * HD, rows], bk[0:HD, :], KIhi[0:HD, rows].bitcast(f32),
                                            ALU.subtract).then_inc(k_ready, made(k_ready, (b, "ki", s)))
                reciprocal_std((b, "kv"), ("kvss", b), P)
                nc.vector.scalar_tensor_tensor(LT[:, :], LT[:, :], GKV[:, 0:1], RV[:, :], ALU.mult, ALU.mult
                                               ).then_inc(lat_norm, made(lat_norm, b))
                bk = full(("iwt", b))
                nc.vector.tensor_copy(IW[:, :, :], bk[:, 0:JT * HEADS].rearrange("p (j h) -> p j h", h=HEADS)
                                      ).then_inc(iw_ready, made(iw_ready, b))
                dve.wait_ge(lat_hi, n(lat_hi, b))
                nc.vector.tensor_tensor(LTlo[:, :], LT[:, :], LThi[:, :].bitcast(f32), ALU.subtract
                                        ).then_inc(lat_split, made(lat_split, b))
                bk = full(("kb", b))
                dve.wait_ge(k_hi, n(k_hi, (b, "kb", 0)))
                nc.vector.tensor_tensor(KBlo[:, rows], bk[:, :], KBhi[:, rows].bitcast(f32), ALU.subtract
                                        ).then_inc(k_ready, made(k_ready, (b, "kb", 0)))
                bk = full(("vb", b))
                dve.wait_ge(v_hi, n(v_hi, (b, "vb", 0)))
                v = VB[:, b * JT:(b + 1) * JT, :]
                nc.vector.tensor_tensor(v[:, :, HD:P], bk[:, 0:JT * HD].rearrange("p (j d) -> p j d", d=HD),
                                        v[:, :, 0:HD].bitcast(f32), ALU.subtract).then_inc(v_ready, made(v_ready, (b, "vb", 0)))
                dve.wait_ge(iw_ready, n(iw_ready, b))
                for j in searched(b):
                    for h in range(HEADS):
                        for c, w in chunks((b * JT + j + 1) * P):
                            key = (b, j, h, c)
                            g = n(relu_ready, key) - 1
                            dve.wait_ge(relu_ready, g + 1)
                            r, s, iw = RB[:, g % 2, 0:w], SC[:, j, c:c + w], IW[:, j, h:h + 1]
                            if h == 0:
                                ins = nc.vector.tensor_scalar(s, r, iw, None, ALU.mult)
                            else:
                                dve.wait_ge(score_added, n(score_added, (b, j, h - 1, c)))
                                ins = nc.vector.scalar_tensor_tensor(s, r, iw, s, ALU.mult, ALU.add)
                            ins.then_inc(score_added, made(score_added, key))
                    w = (b * JT + j + 1) * P
                    dve.wait_ge(score_added, n(score_added, (b, j, HEADS - 1, chunks(w)[-1][0])))
                    nc.vector.memset(SC[0:HD, j, w - HD:w], NEG).then_inc(score_ready, made(score_ready, (b, j)))
                if searched(b):
                    dve.wait_ge(score_ready, n(score_ready, (b, searched(b)[-1])))
                    dve.wait_ge(logits_full, n(logits_full, ("idx", b, JT - 1, HEADS - 1, chunks((b + 1) * ROWS)[-1][0])))
                for j in range(JT):
                    if j not in searched(b):
                        w = (b * JT + j + 1) * P
                        step[0] += 1
                        nc.vector.memset(MASK[:, j, 0:w], 0.0).then_inc(topk_step, 1)
                        dve.wait_ge(topk_step, step[0])
                        nc.vector.memset(MASK[0:HD, j, w - HD:w], NEG).then_inc(mask_ready, made(mask_ready, (b, j)))
                if searched(b):
                    topk(b)
                for m in range(ET):
                    q_heads(b, "aq", m)
                bk = full(("ak", b, 0))
                for g in range(KVH):
                    for s in range(2):
                        dve.wait_ge(k_hi, n(k_hi, (b, "ak", 2 * KVH - 1)))
                        hi = AKhi[s * HD:(s + 1) * HD, g, P:(JT + 1) * P]
                        nc.vector.tensor_tensor(AKlo[s * HD:(s + 1) * HD, g, P:(JT + 1) * P], bk[g * HD:(g + 1) * HD, :],
                                                hi.bitcast(f32), ALU.subtract
                                                ).then_inc(k_ready, made(k_ready, (b, "ak", 2 * g + s)))
                bk = full(("va", b))
                dve.wait_ge(v_hi, n(v_hi, (b, "va", 0)))
                v = VA[:, 1:JT + 1, :, :]
                nc.vector.tensor_tensor(v[:, :, :, HD:P], bk[:, :].rearrange("p (j g d) -> p j g d", g=KVH, d=HD),
                                        v[:, :, :, 0:HD].bitcast(f32), ALU.subtract).then_inc(v_ready, made(v_ready, (b, "va", 0)))
                dve.wait_ge(taba_ready, HEADS)
                attend(b, "a")
                for m in range(ET):
                    q_heads(b, "bq", m)
                dve.wait_ge(mask_ready, n(mask_ready, (b, JT - 1)))
                attend(b, "b")
                for s, ot in enumerate((OTA, OTB)):
                    dve.wait_ge(oh_ready, n(oh_ready, (b, s)))
                    nc.vector.tensor_tensor(OTlo[s][:, :, :], ot[:, :, :], OThi[s][:, :, :].bitcast(f32), ALU.subtract
                                            ).then_inc(os_ready, made(os_ready, (b, s)))
                dve.wait_ge(os_ready, n(os_ready, (b, 1)))

                def split_m(m):
                    dve.wait_ge(m_hi, n(m_hi, (b, m)))
                    nc.vector.tensor_tensor(MGlo[:, m, :], M1[:, m % 2, :], MGhi[:, m, :].bitcast(f32), ALU.subtract
                                            ).then_inc(m_split, made(m_split, (b, m)))

                for m in range(KT):
                    dve.wait_ge(gate_in[m % 2], n(gate_in[m % 2], (b, m)))
                    if m >= 2:
                        dve.wait_ge(m_split, n(m_split, (b, m - 2)))
                    for s, dst in enumerate((M1, M2)):
                        bk = full(("br", b, m, s))
                        nc.vector.tensor_tensor(dst[:, m % 2, :], bk[:, :], GL[:, m % 2, s, :], ALU.mult
                                                ).then_inc(gated, made(gated, (b, m, s)))
                    dve.wait_ge(gated, n(gated, (b, m, 1)))
                    nc.vector.tensor_tensor(M1[:, m % 2, :], M1[:, m % 2, :], M2[:, m % 2, :], ALU.add
                                            ).then_inc(merged, made(merged, (b, m)))
                    if m:
                        split_m(m - 1)
                split_m(KT - 1)
                normed(b, 1, X1T, H2F, G2, H2hi, H2lo)
                for part in PARTS:
                    for i in part:
                        bk = full(("fu", b, i))
                        dve.wait_ge(silu_ready, n(silu_ready, (b, i)))
                        if i >= 2:
                            dve.wait_ge(ff_split, n(ff_split, (b, i - 2)))
                        nc.vector.tensor_tensor(FF[:, i % 2, :], bk[:, :], SL[:, i % 2, :], ALU.mult
                                                ).then_inc(ff_ready, made(ff_ready, (b, i)))
                        dve.wait_ge(ff_hi, n(ff_hi, (b, i)))
                        nc.vector.tensor_tensor(FFlo[:, i - part[0], :], FF[:, i % 2, :], FFhi[:, i - part[0], :].bitcast(f32),
                                                ALU.subtract).then_inc(ff_split, made(ff_split, (b, i)))
                    for m in range(KT):
                        bk = full(("fd", b, part[0], m))
                        if part[0]:
                            dve.wait_ge(added, n(added, (b, part[0] - SLOTS, m)))
                        nc.vector.tensor_tensor(X1T[:, m, :], bk[:, :], X1T[:, m, :], ALU.add
                                                ).then_inc(added, made(added, (b, part[0], m)))
                reciprocal_std((b, 2), ("ss", b, 2), D)
                for k in range(KT):
                    nc.vector.scalar_tensor_tensor(X1T[:, k, :], X1T[:, k, :], GF[:, k:k + 1], RV[:, :], ALU.mult,
                                                   ALU.mult).then_inc(y_ready, made(y_ready, (b, k)))

    return C.seen


def _bucket(rel):
    starts = [8, 12, 16, 23, 32, 46, 64, 91]
    near = np.abs(rel)
    large = 7 + sum((near >= s).astype(np.int64) for s in starts)
    return np.where(rel > 0, BUCKETS // 2, 0) + np.where(near < 8, near, large)


def _constants():
    hot = np.zeros((BUCKETS, 2 * FTW), np.float32)
    r = np.arange(FTW)
    bucket = _bucket(np.minimum(r - (BAND - 1), P - 1))
    hot[bucket, r] = 1.0
    hot[bucket, FTW + r] = 1.0
    hot[FAR_BUCKET, FTW:] -= 1.0
    band = np.zeros((P, BAND), np.float32)
    half = P // 2
    band[:half, :half] = NEG
    band[:half, 3 * half:] = NEG
    band[half:, :P] = NEG
    return {"hot": hot, "band": band, "ident": np.eye(P, dtype=np.float32)}


_INS = ["x", "norm1_g", "w_in", "rel_bias", "sinks", "kv_norm_g", "w_uk", "w_uv", "w_branch_a", "w_branch_b",
        "w_out", "norm2_g", "w_ffn_gate", "w_ffn_up", "w_ffn_down", "norm_f_g"]


def build(nc, shapes, known):
    f32 = mybir.dt.float32
    io = {name: nc.dram_tensor(f"in_{name}", shape, f32, kind="ExternalInput").ap() for name, shape in shapes.items()}
    io["out"] = nc.dram_tensor("out_0", shapes["x"], f32, kind="ExternalOutput").ap()
    io["ft"] = nc.dram_tensor("ft", (2 * HEADS, P, FTW), f32).ap()
    io["gates"] = nc.dram_tensor("gates", (2 * shapes["x"][2] // P, P, ROWS), f32).ap()
    return trunk_program(nc, io, known)


def kernel(**inputs):
    import concourse.bacc as bacc
    from concourse.bass_utils import run_bass_kernel_spmd

    arrays = {name: np.ascontiguousarray(inputs[name]) for name in _INS}
    arrays.update(_constants())
    shapes = {name: a.shape for name, a in arrays.items()}
    counts = build(bacc.Bacc("TRN2", target_bir_lowering=False, num_devices=1), shapes, {})
    nc = bacc.Bacc("TRN2", target_bir_lowering=False, num_devices=1)
    build(nc, shapes, counts)
    r = run_bass_kernel_spmd(nc, [{f"in_{name}": a for name, a in arrays.items()}], core_ids=[0])
    return r.results[0]["out_0"]
```

```python
import numpy as np
import concourse.bass as bass
from concourse import mybir
from contextlib import ExitStack

P = 128
ROWS = 512
JT = ROWS // P
HEADS, HD = 8, 64
KVH = 2
NEG = -1e30
EPS = 1e-6
LOWEST = -3e38
SLOTS = 8
LGW = 1024
BUCKETS, FAR_BUCKET = 32, 15
BAND = 2 * P
FTW = 384


class Count:

    def __init__(self, known):
        self.known, self.seen, self.now = known, {}, {}

    def made(self, sem, key, by=1):
        self.now[sem.name] = self.now.get(sem.name, 0) + by
        self.seen[(sem.name, key)] = self.now[sem.name]
        return by

    def n(self, sem, key):
        return self.known.get((sem.name, key), 1)


def trunk_program(nc, io, known):
    f32, f32r, bf16, i32 = mybir.dt.float32, mybir.dt.float32r, mybir.dt.bfloat16, mybir.dt.int32
    ACT, ALU = mybir.ActivationFunctionType, mybir.AluOpType
    x, out = io["x"], io["out"]
    SEQ, D = x.shape[1], x.shape[2]
    DFF = io["w_ffn_gate"].shape[2]
    NB = SEQ // ROWS
    KT = D // P
    ET = HEADS * HD // P
    FT = DFF // P
    TOPK = min(256, SEQ // 4)
    TK = TOPK // P
    PARTS = [range(a, min(a + SLOTS, FT)) for a in range(0, FT, SLOTS)]
    C = Count(known)
    n, made = C.n, C.made

    w_in = io["w_in"][0]
    COL = dict(aq=0, ak=512, av=640, bq=768, lat=1280, iq=1408, ikw=1920, gate=1992)

    with ExitStack() as ctx:
        top = (nc.sbuf_base + 63) // 64 * 64
        place = [top]

        def at(name, shape, dt, offset):
            return nc.alloc_sbuf_tensor_at(name, shape, dt, offset=offset)

        def new(name, shape, dt):
            size = int(np.prod(shape[1:])) * (2 if dt == bf16 else 4)
            offset = place[0]
            place[0] += (size + 31) // 32 * 32
            return at(name, shape, dt, offset)

        def region(size):
            offset = place[0]
            place[0] += size
            return offset

        KIhi, KIlo = new("KIhi", [P, SEQ], f32r), new("KIlo", [P, SEQ], f32r)
        KBhi, KBlo = new("KBhi", [P, SEQ], f32r), new("KBlo", [P, SEQ], f32r)
        VB = new("VB", [P, SEQ // P, P], f32r)
        AKhi, AKlo = (new(s, [P, KVH, (JT + 1) * P], f32r) for s in ("AKhi", "AKlo"))
        VA = new("VA", [P, JT + 1, KVH, P], f32r)
        TABA, TABB = new("TABA", [P, HEADS, BAND], f32), new("TABB", [P, HEADS, BAND], f32)
        IDENT, ONES = new("IDENT", [P, P], f32), new("ONES", [P, P], f32)
        WRAW = [new(f"WRAW{i}", [P, SLOTS, P], f32) for i in range(2)]
        WHI = [new(f"WHI{i}", [P, SLOTS, P], f32r) for i in range(2)]
        WLO = [new(f"WLO{i}", [P, SLOTS, P], f32r) for i in range(2)]
        WUKhi, WUKlo = new("WUKhi", [P, P], f32r), new("WUKlo", [P, P], f32r)
        WUVhi, WUVlo = new("WUVhi", [P, HD], f32r), new("WUVlo", [P, HD], f32r)
        G1, G2, GF = (new(s, [P, KT], f32) for s in ("G1", "G2", "GF"))
        GKV, SINK = new("GKV", [P, 1], f32), new("SINK", [P, HEADS], f32)
        IW = new("IW", [P, JT, HEADS], f32)
        CNT, NEED = new("CNT", [P, JT], f32), new("NEED", [P, JT], f32)
        PREF, SIGN, THR, TAKE = (new(s, [P, JT], i32) for s in ("PREF", "SIGN", "THR", "TAKE"))
        BIT = new("BIT", [P, 1], i32)
        MX, NM, SN = (new(s, [P, 4, 4], f32) for s in ("MX", "NM", "SN"))
        RS, ES, RR = new("RS", [P, 2, HEADS], f32), new("ES", [P, 2, HEADS], f32), new("RR", [P, 2, HEADS], f32)
        RV = new("RV", [P, ROWS], f32)
        rO, r1, rQ, rM, r3 = region(8192), region(32768), region(16384), region(16384), region(32768)
        assert place[0] <= nc.sbuf_usable_end, place[0] - nc.sbuf_usable_end
        OTA = at("OTA", [P, ET, ROWS], f32, rO)
        GS = at("GS", [P, 2, ROWS], f32, rO)
        IWT = at("IWT", [HEADS, ROWS], f32, rO)
        VAT = at("VAT", [P, ROWS], f32, rO + 4096)
        XN = at("XN", [P, JT, D], f32, r1)
        XT = at("XT", [P, KT, ROWS], f32, r1 + 16384)
        SC = at("SC", [P, JT, SEQ], f32, r1)
        LG = dict(a=[at(f"LGa{i}", [P, LGW], f32, r1 + 4096 * i) for i in range(4)],
                  b=[at(f"LGb{i}", [P, SEQ], f32, r1 + 8192 * i) for i in range(4)])
        r_pt, r_on = dict(a=r1 + 16384, b=r3 + 12288), dict(a=r1 + 24576, b=r3 + 8192)
        PThi = {k: [at(f"PThi{k}{i}", [P, 4, P], f32r, r + 2048 * i) for i in range(2)] for k, r in r_pt.items()}
        PTlo = {k: [at(f"PTlo{k}{i}", [P, 4, P], f32r, r + 4096 + 2048 * i) for i in range(2)] for k, r in r_pt.items()}
        ON = {k: at("ON" + k, [P, HEADS, HD], f32, r) for k, r in r_on.items()}
        OA = {k: at("OA" + k, [P, 4, HD], f32, r + 2048) for k, r in r_on.items()}
        OB = {k: at("OB" + k, [P, 4, HD], f32, r + 3072) for k, r in r_on.items()}
        OThi = [at(f"OThi{i}", [P, ET, ROWS], f32r, r1 + 8192 * i) for i in range(2)]
        OTlo = [at(f"OTlo{i}", [P, ET, ROWS], f32r, r1 + 16384 + 8192 * i) for i in range(2)]
        X1T = at("X1T", [P, KT, ROWS], f32, r1)
        XR = at("XR", [P, JT, D], f32, r1 + 16384)
        H2F = at("H2F", [P, KT, ROWS], f32, r1 + 16384)
        SL = at("SL", [P, 2, ROWS], f32, r1 + 16384)
        FF = at("FF", [P, 2, ROWS], f32, r1 + 16384 + 4096)
        OUTN = at("OUTN", [P, JT, D], f32, r1 + 16384)
        FTAB = at("FTAB", [P, 2 * HEADS, FTW], f32, r1)
        Q = at("Q", [P, HEADS, ROWS], f32r, rQ)
        JUNK = at("JUNK", [P, JT, SEQ], bf16, rQ)
        EQ, CS = at("EQ", [P, SEQ], f32, rQ), at("CS", [P, SEQ], f32, rQ + 8192)
        H2hi, H2lo = at("H2hi", [P, KT, ROWS], f32r, rQ), at("H2lo", [P, KT, ROWS], f32r, rM)
        SQ = at("SQ", [P, KT, ROWS], f32, rM)
        LT, LSQ = at("LT", [P, ROWS], f32, rM), at("LSQ", [P, ROWS], f32, rM + 2048)
        LThi, LTlo = at("LThi", [P, ROWS], f32r, rM + 4096), at("LTlo", [P, ROWS], f32r, rM + 6144)
        RB = at("RB", [P, 2, LGW], f32, rM)
        MASK = at("MASK", [P, JT, SEQ], bf16, rM)
        GL = at("GL", [P, 2, 2, ROWS], f32, rM)
        M1, M2 = at("M1", [P, 2, ROWS], f32, rM + 8192), at("M2", [P, 2, ROWS], f32, rM + 12288)
        HThi, HTlo = at("HThi", [P, KT, ROWS], f32r, r3), at("HTlo", [P, KT, ROWS], f32r, r3 + 16384)
        OTB = at("OTB", [P, ET, ROWS], f32, r3)
        MGhi, MGlo = at("MGhi", [P, KT, ROWS], f32r, r3), at("MGlo", [P, KT, ROWS], f32r, r3 + 16384)
        FFhi, FFlo = at("FFhi", [P, SLOTS, ROWS], f32r, r3), at("FFlo", [P, SLOTS, ROWS], f32r, r3 + 16384)
        HOT = at("HOT", [BUCKETS, 2 * FTW], f32, r3)
        RELB = at("RELB", [BUCKETS, 2 * HEADS], f32, r3 + 3072)
        BANDM = at("BANDM", [P, BAND], f32, r3 + 4096)
        WU = at("WU", [P, 2 * HD + HD], f32, r3 + 8192)

        BANK = [ctx.enter_context(nc.psum_tensor(f"BANK{i}", [P, ROWS], f32)) for i in range(2)]
        LP = [ctx.enter_context(nc.psum_tensor(f"LP{i}", [P, LGW], f32)) for i in range(2)]
        TP = [ctx.enter_context(nc.psum_tensor(f"TP{i}", [P, 4, P], f32)) for i in range(2)]

        def sem(name):
            return ctx.enter_context(nc.semaphore(name))

        const_in, ones_set = sem("const_in"), sem("ones_set")
        ftab_ready, ftab_out, taba_in, taba_ready = (sem(s) for s in ("ftab_ready", "ftab_out", "taba_in", "taba_ready"))
        wu_hi, wu_ready = sem("wu_hi"), sem("wu_ready")
        w_in_sem = [sem(f"w_loaded{i}") for i in range(2)]
        w_hi, w_split = sem("w_hi"), sem("w_split")
        bank_full, logits_full, trans_full = sem("bank_full"), sem("logits_full"), sem("trans_full")
        x_in = [sem(f"x_in{j}") for j in range(JT)]
        xr_in = [sem(f"xr_in{j}") for j in range(JT)]
        xt_ready, sq_ready = sem("xt_ready"), sem("sq_ready")
        var_ready, std_ready, rinv_ready = sem("var_ready"), sem("std_ready"), sem("rinv_ready")
        h_ready, h_hi, h_split = sem("h_ready"), sem("h_hi"), sem("h_split")
        q_hi, q_ready = sem("q_hi"), sem("q_ready")
        k_hi, k_ready, kw_ready, iw_ready = sem("k_hi"), sem("k_ready"), sem("kw_ready"), sem("iw_ready")
        lat_ready, lat_norm, lat_hi, lat_split = sem("lat_ready"), sem("lat_norm"), sem("lat_hi"), sem("lat_split")
        v_hi, v_ready, vat_ready, carried = sem("v_hi"), sem("v_ready"), sem("vat_ready"), sem("carried")
        relu_ready, score_added, score_ready = sem("relu_ready"), sem("score_added"), sem("score_ready")
        topk_step, mask_ready = sem("topk_step"), sem("mask_ready")
        gate_ready = sem("gate_ready")
        gate_out = [sem(f"gate_out{i}") for i in range(2)]
        gate_in = [sem(f"gate_in{i}") for i in range(2)]
        masked, negmax, probs, values_done = sem("masked"), sem("negmax"), sem("probs"), sem("values_done")
        pt_hi, pt_ready = sem("pt_hi"), sem("pt_ready")
        o_step, o_ready, ot_ready = sem("o_step"), sem("o_ready"), sem("ot_ready")
        oh_ready, os_ready = sem("oh_ready"), sem("os_ready")
        gated, merged, m_hi, m_split = sem("gated"), sem("merged"), sem("m_hi"), sem("m_split")
        x1_ready = sem("x1_ready")
        silu_ready, ff_ready, ff_hi, ff_split, added = (sem(s) for s in ("silu_ready", "ff_ready", "ff_hi", "ff_split", "added"))
        y_ready, outn_left, outn_right = sem("y_ready"), sem("outn_left"), sem("outn_right")
        out_done = [sem(f"out_done{j}") for j in range(JT)]

        def bank(key):
            return BANK[C.known.get(("bank use", key), 0) % 2]

        def logits(key):
            return LP[(n(logits_full, key) - 1) % 2]

        def trans(key):
            return TP[(n(trans_full, key) - 1) % 2]

        def weights(w, rows, c0, width=P):
            return w[rows[0] * P:(rows[-1] + 1) * P, c0:c0 + width].rearrange("(k p) c -> p k c", p=P)

        def proj_jobs(b, kind, tiles, width=P):
            return [((kind, b, m), weights(w_in, range(KT), COL[kind] + m * P, width)) for m in range(tiles)]

        def ffn_jobs(b, part):
            jobs = []
            for i in part:
                jobs.append((("fg", b, i), weights(io["w_ffn_gate"][0], range(KT), i * P)))
                jobs.append((("fu", b, i), weights(io["w_ffn_up"][0], range(KT), i * P)))
            for m in range(KT):
                jobs.append((("fd", b, part[0], m), weights(io["w_ffn_down"][0], part, m * P)))
            return jobs

        def jobs_of(b):
            jobs = proj_jobs(b, "iq", ET) + proj_jobs(b, "ikw", 1, HD + HEADS) + proj_jobs(b, "lat", 1)
            jobs += proj_jobs(b, "gate", 2 * KT) + proj_jobs(b, "aq", ET) + proj_jobs(b, "ak", 1)
            jobs += proj_jobs(b, "av", 1) + proj_jobs(b, "bq", ET)
            for m in range(KT):
                for s, w in enumerate(("w_branch_a", "w_branch_b")):
                    jobs.append((("br", b, m, s), weights(io[w][0], range(ET), m * P)))
            for m in range(KT):
                jobs.append((("wo", b, m), weights(io["w_out"][0], range(KT), m * P)))
            for part in PARTS:
                jobs += ffn_jobs(b, part)
            return jobs

        JOBS = [job for b in range(NB) for job in jobs_of(b)]

        def chunks(width):
            return [(c, min(LGW, width - c)) for c in range(0, width, LGW)]

        def halves(c, w):
            return [(a, min(ROWS, c + w - a)) for a in range(c, c + w, ROWS)]

        def units(b, kind):
            return [(b, kind, j, h) for j in range(JT) for h in range(0, HEADS, 4 if kind == "a" else 1)]

        def key_tiles(b, kind, j):
            t = b * JT + j
            if kind == "a":
                return (1, t) if t == 0 else (2, t - 1)
            return t + 1, 0

        def chunks_of(u):
            b, kind, j, _ = u
            return [(0, LGW)] if kind == "a" else chunks(key_tiles(b, kind, j)[0] * P)

        def groups(u):
            b, kind, j, h0 = u
            tiles = [(h0 + i, kt, i * BAND + kt * P) for i in range(4 if kind == "a" else 1)
                     for kt in range(key_tiles(b, kind, j)[0])]
            return [tiles[i:i + 4] for i in range(0, len(tiles), 4)]

        def searched(b):
            return [j for j in range(JT) if b * JT + j >= TK]

        block = ctx.enter_context(nc.Block())

        @block.sync
        def _(sp):
            consts = [(IDENT[:, :], io["ident"]), (HOT[:, :], io["hot"]), (BANDM[:, :], io["band"]),
                      (RELB[:, :], io["rel_bias"]), (GKV[:, :], io["kv_norm_g"].rearrange("a p -> p a")),
                      (SINK[:, :], io["sinks"][0].partition_broadcast(P)), (WU[:, 2 * HD:3 * HD], io["w_uv"][0])]
            consts += [(WU[:, HD * i:HD * (i + 1)], io["w_uk"][0]) for i in range(2)]
            for g, name in ((G1, "norm1_g"), (G2, "norm2_g")):
                consts.append((g[:, :], io[name][0].rearrange("(k p) -> p k", p=P)))
            consts.append((GF[:, :], io["norm_f_g"].rearrange("(k p) -> p k", p=P)))
            for i, (dst, src) in enumerate(consts):
                made(const_in, i, 16)
                sp.dma_start(dst, src, allow_slow_non_contiguous=True).then_inc(const_in, 16)
            sp.wait_ge(ftab_ready, n(ftab_ready, 2 * HEADS - 1))
            ft = io["ft"]
            sp.dma_start(ft.rearrange("h p r -> p h r"), FTAB[:, :, :]).then_inc(ftab_out, 16)
            sp.wait_ge(ftab_out, 16)
            for s, tab in enumerate((TABA, TABB)):
                skew = bass.AP(ft.tensor, s * HEADS * P * FTW + P - 1, [[FTW - 1, P], [P * FTW, HEADS], [1, BAND]])
                sp.dma_start(tab[:, :, :], skew).then_inc(taba_in, 16)

            def load_x(b):
                for j in range(JT):
                    made(x_in[j], (b, 0), 16)
                    sp.dma_start(XN[:, j, :], x[0, b * ROWS + j * P:b * ROWS + (j + 1) * P, :]).then_inc(x_in[j], 16)

            load_x(0)
            for i, (key, src) in enumerate(JOBS):
                k, width = src.shape[1], src.shape[2]
                if i >= 2:
                    sp.wait_ge(w_split, i - 1)
                sp.dma_start(WRAW[i % 2][:, 0:k, 0:width], src).then_inc(w_in_sem[i % 2], 16)
                if key[0] == "iq" and key[1] and key[2] == 1:
                    b = key[1]
                    sp.wait_ge(bank_full, n(bank_full, ("yt", b - 1, JT - 1, D // ROWS - 1)))
                    load_x(b)
            for j in range(JT):
                sp.wait_ge(out_done[j], 16 * NB)

        @block.gpsimd
        def _(pool):
            for i, (key, src) in enumerate(JOBS):
                k, width = src.shape[1], src.shape[2]
                raw = WRAW[i % 2][:, 0:k, 0:width]
                hi, lo = WHI[i % 2][:, 0:k, 0:width], WLO[i % 2][:, 0:k, 0:width]
                pool.wait_ge(w_in_sem[i % 2], 16 * (i // 2 + 1))
                if i >= 2:
                    pool.wait_ge(bank_full, n(bank_full, JOBS[i - 2][0]))
                nc.gpsimd.tensor_scalar(hi, raw, 1.0, 1.0, ALU.mult, ALU.mult).then_inc(w_hi, 1)
                pool.wait_ge(w_hi, i + 1)
                nc.gpsimd.tensor_tensor(lo, raw, hi.bitcast(f32), ALU.subtract).then_inc(w_split, 1)

        @block.tensor
        def _(pe):
            releases = dict(bank=[], logits=[], trans=[])
            job_no = [0]

            def take(kind, sem_, key, use=None):
                uses = releases[kind]
                if len(uses) >= 2:
                    pe.wait_ge(uses[-2][0], n(*uses[-2]))
                C.seen[(kind + " use", use)] = len(uses)
                uses.append((sem_, key))
                return (BANK if kind == "bank" else LP if kind == "logits" else TP)[(len(uses) - 1) % 2]

            def three(dst, whi, wlo, mhi, mlo, first, last):
                nc.tensor.matmul(dst, whi, mhi, start=first, stop=False)
                nc.tensor.matmul(dst, whi, mlo, start=False, stop=False)
                return nc.tensor.matmul(dst, wlo, mhi, start=False, stop=last)

            def job(mhi, mlo, release, add=None, ready=None):
                i = job_no[0]
                key, src = JOBS[i]
                job_no[0] += 1
                k, width = src.shape[1], src.shape[2]
                dst = take("bank", *release, key)[0:width, :]
                pe.wait_ge(w_split, i + 1)
                for s in range(k):
                    if ready is not None:
                        pe.wait_ge(h_split, n(h_split, (*ready, s)))
                    last = three(dst, WHI[i % 2][:, s, 0:width], WLO[i % 2][:, s, 0:width], mhi[:, s, :], mlo[:, s, :],
                                 s == 0, s == k - 1)
                if add is not None:
                    last = add(dst)
                last.then_inc(bank_full, made(bank_full, key))

            def square_sums(key, squares, ready, release):
                dst = take("logits", *release)[:, 0:ROWS]
                for k in range(squares.shape[1]):
                    yield
                    pe.wait_ge(ready, n(ready, (*key[1:], k)))
                    last = nc.tensor.matmul(dst, ONES[:, :], squares[:, k, :], start=(k == 0),
                                            stop=(k == squares.shape[1] - 1))
                last.then_inc(logits_full, made(logits_full, key))
                yield

            pe.wait_ge(const_in, n(const_in, 11))
            for h in range(2 * HEADS):
                dst = take("bank", ftab_ready, h, ("ft", h))
                c = FTW * (h // HEADS)
                nc.tensor.matmul(dst[:, 0:FTW], RELB[:, h:h + 1].to_broadcast([BUCKETS, P]), HOT[:, c:c + FTW],
                                 start=True, stop=True).then_inc(bank_full, made(bank_full, ("ft", h)))
            pe.wait_ge(ones_set, 1)

            def attend(b, kind):
                items = units(b, kind)
                outs_due = []

                def qk(u):
                    _, _, j, h0 = u
                    tiles, first = key_tiles(b, kind, j)
                    for c, w in chunks_of(u):
                        dst = take("logits", masked, (u, c))
                        if kind == "a":
                            v = tiles * P
                            s0 = (first - b * JT + 1) * P
                            g = h0 // (HEADS // KVH)
                            for i in range(4):
                                d, q = dst[:, i * BAND:i * BAND + v], Q[:, h0 + i, j * P:(j + 1) * P]
                                nc.tensor.matmul(d, q, AKhi[:, g, s0:s0 + v], start=True, stop=False)
                                last = nc.tensor.matmul(d, q, AKlo[:, g, s0:s0 + v], start=False, stop=True)
                                if i == 3:
                                    last.then_inc(logits_full, made(logits_full, (u, c)))
                                if i % 2:
                                    yield
                            continue
                        q = Q[:, h0, j * P:(j + 1) * P]
                        for a, v in halves(c, w):
                            d = dst[:, a - c:a - c + v]
                            nc.tensor.matmul(d, q, KBhi[:, a:a + v], start=True, stop=False, skip_group_check=True)
                            last = nc.tensor.matmul(d, q, KBlo[:, a:a + v], start=False, stop=True, skip_group_check=True)
                            for kt in range(max(0, tiles - 2), tiles):
                                if a <= kt * P < a + v:
                                    col = (kt - (tiles - 2)) * P
                                    last = nc.tensor.matmul(dst[:, kt * P - c:(kt + 1) * P - c], IDENT[:, :],
                                                            TABB[:, h0, col:col + P], start=False, stop=True,
                                                            skip_group_check=True)
                            if a + v == c + w:
                                last.then_inc(logits_full, made(logits_full, (u, c)))
                            yield

                def transposes(i, g):
                    u = items[i]
                    grp = groups(u)[g]
                    dst = take("trans", pt_ready, (u, g))
                    if g == 0:
                        pe.wait_ge(probs, n(probs, u))
                    for e, (_, _, col) in enumerate(grp):
                        last = nc.tensor.transpose(dst[:, e, :], LG[kind][i % 4][:, col:col + P], IDENT[:, :])
                    last.then_inc(trans_full, made(trans_full, (u, g)))

                def values(i, g):
                    u = items[i]
                    _, _, j, h0 = u
                    tiles, first = key_tiles(b, kind, j)
                    if h0 % 4 == 0 and g == 0:
                        values.bank = take("bank", o_step, ("o", b, kind, j, h0 // 4, 2), ("o", b, kind, j, h0 // 4))
                    t = n(trans_full, (u, g)) - 1
                    pe.wait_ge(pt_ready, n(pt_ready, (u, g)))
                    for e, (h, kt, _) in enumerate(groups(u)[g]):
                        dst = values.bank[:, (h % 4) * P:(h % 4 + 1) * P]
                        v = VA[:, first + kt - b * JT + 1, h // (HEADS // KVH), :] if kind == "a" else VB[:, kt, :]
                        nc.tensor.matmul(dst, PThi[kind][t % 2][:, e, :], v, start=(kt == 0), stop=False, skip_group_check=True)
                        last = nc.tensor.matmul(dst, PTlo[kind][t % 2][:, e, :], v, start=False, stop=(kt == tiles - 1),
                                                skip_group_check=True)
                    last.then_inc(values_done, made(values_done, (u, g)))

                def out_transposes(j):
                    dst = take("trans", ot_ready, (b, kind, j))
                    pe.wait_ge(o_ready, n(o_ready, (b, kind, j, 1)))
                    for e in range(ET):
                        last = nc.tensor.transpose(dst[:, e, :],
                                                   ON[kind][:, 2 * e:2 * e + 2, :].rearrange("p h d -> p (h d)"), IDENT[:, :])
                    last.then_inc(trans_full, made(trans_full, ("on", b, kind, j)))

                for u in items[:3]:
                    for _ in qk(u):
                        pass
                transposes(0, 0)
                for i, u in enumerate(items):
                    ahead = qk(items[i + 3]) if i + 3 < len(items) else iter(())
                    end = len(groups(u)) - 1
                    for g in range(end + 1):
                        if g < end:
                            transposes(i, g + 1)
                        elif i + 1 < len(items):
                            transposes(i + 1, 0)
                        next(ahead, None)
                        if g == end:
                            for _ in ahead:
                                pass
                        values(i, g)
                    if outs_due:
                        out_transposes(outs_due.pop())
                    if i + 1 == len(items) or items[i + 1][2] != u[2]:
                        outs_due.append(u[2])
                out_transposes(outs_due.pop())

            for b in range(NB):
                sums = square_sums(("ss", b, 0), SQ, sq_ready, (var_ready, (b, 0)))
                next(sums)
                for k in range(KT):
                    dst = take("bank", xt_ready, (b, k), ("xt", b, k))
                    for j in range(JT):
                        if k == 0:
                            pe.wait_ge(x_in[j], n(x_in[j], (b, 0)))
                        last = nc.tensor.transpose(dst[:, j * P:(j + 1) * P], XN[:, j, k * P:(k + 1) * P], IDENT[:, :])
                    last.then_inc(bank_full, made(bank_full, ("xt", b, k)))
                    if k >= 2:
                        next(sums)
                for _ in sums:
                    pass
                for m in range(ET):
                    job(HThi, HTlo, (q_ready, (b, "iq", m, 1)), ready=(b, 0) if m == 0 else None)
                job(HThi, HTlo, (kw_ready, b))
                job(HThi, HTlo, (sq_ready, (b, "kv", 0)))
                for _ in square_sums(("kvss", b, "kv"), LSQ[:, :].rearrange("p (k r) -> p k r", k=1), sq_ready,
                                     (var_ready, (b, "kv"))):
                    pass
                pe.wait_ge(kw_ready, n(kw_ready, b))
                dst = take("bank", iw_ready, b, ("iwt", b))
                for j in range(JT):
                    last = nc.tensor.transpose(dst[:, j * HEADS:(j + 1) * HEADS], IWT[:, j * P:(j + 1) * P],
                                               IDENT[0:HEADS, 0:HEADS])
                last.then_inc(bank_full, made(bank_full, ("iwt", b)))
                pe.wait_ge(lat_split, n(lat_split, b))
                pe.wait_ge(wu_ready, 2)
                dst = take("bank", k_ready, (b, "kb", 0), ("kb", b))
                three(dst[:, :], WUKhi[:, :], WUKlo[:, :], LThi[:, :], LTlo[:, :], True, True
                      ).then_inc(bank_full, made(bank_full, ("kb", b)))
                dst = take("bank", v_ready, (b, "vb", 0), ("vb", b))
                for j in range(JT):
                    last = three(dst[:, j * HD:(j + 1) * HD], LThi[:, j * P:(j + 1) * P], LTlo[:, j * P:(j + 1) * P],
                                 WUVhi[:, :], WUVlo[:, :], True, True)
                last.then_inc(bank_full, made(bank_full, ("vb", b)))
                pe.wait_ge(q_ready, n(q_ready, (b, "iq", ET - 1, 1)))
                pe.wait_ge(k_ready, n(k_ready, (b, "ki", 1)))
                for j in searched(b):
                    for h in range(HEADS):
                        for c, w in chunks((b * JT + j + 1) * P):
                            dst = take("logits", relu_ready, (b, j, h, c))
                            for a, v in halves(c, w):
                                q = Q[:, h, j * P:(j + 1) * P]
                                nc.tensor.matmul(dst[:, a - c:a - c + v], q, KIhi[:, a:a + v], start=True, stop=False)
                                last = nc.tensor.matmul(dst[:, a - c:a - c + v], q, KIlo[:, a:a + v], start=False, stop=True)
                            last.then_inc(logits_full, made(logits_full, ("idx", b, j, h, c)))
                for m in range(2 * KT):
                    job(HThi, HTlo, (gate_ready, (b, m)))
                for m in range(ET):
                    job(HThi, HTlo, (q_ready, (b, "aq", m, 1)))
                job(HThi, HTlo, (k_ready, (b, "ak", 2 * KVH - 1)))
                job(HThi, HTlo, (vat_ready, b))
                pe.wait_ge(vat_ready, n(vat_ready, b))
                dst = take("bank", v_ready, (b, "va", 0), ("va", b))
                for j in range(JT):
                    last = nc.tensor.transpose(dst[:, j * P:(j + 1) * P], VAT[:, j * P:(j + 1) * P], IDENT[:, :])
                last.then_inc(bank_full, made(bank_full, ("va", b)))
                pe.wait_ge(q_ready, n(q_ready, (b, "aq", ET - 1, 1)))
                pe.wait_ge(k_ready, n(k_ready, (b, "ak", 2 * KVH - 1)))
                pe.wait_ge(v_ready, n(v_ready, (b, "va", 0)))
                attend(b, "a")
                for m in range(ET):
                    job(HThi, HTlo, (q_ready, (b, "bq", m, 1)))
                pe.wait_ge(q_ready, n(q_ready, (b, "bq", ET - 1, 1)))
                pe.wait_ge(k_ready, n(k_ready, (b, "kb", 0)))
                pe.wait_ge(v_ready, n(v_ready, (b, "vb", 0)))
                pe.wait_ge(taba_in, 32)
                attend(b, "b")
                pe.wait_ge(os_ready, n(os_ready, (b, 1)))
                for m in range(KT):
                    for s in range(2):
                        job(OThi[s], OTlo[s], (gated, (b, m, s)))
                pe.wait_ge(m_split, n(m_split, (b, KT - 1)))
                sums = square_sums(("ss", b, 1), SQ, sq_ready, (var_ready, (b, 1)))
                next(sums)
                for m in range(KT):
                    def add_x(dst):
                        for j in range(JT):
                            if m == 0:
                                pe.wait_ge(xr_in[j], n(xr_in[j], b))
                            last = nc.tensor.matmul(dst[:, j * P:(j + 1) * P], XR[:, j, m * P:(m + 1) * P], IDENT[:, :],
                                                    start=False, stop=True, skip_group_check=True)
                        return last
                    job(MGhi, MGlo, (sq_ready, (b, 1, m)), add_x)
                    if m:
                        next(sums)
                for _ in sums:
                    pass
                for part in PARTS:
                    for i in part:
                        job(H2hi, H2lo, (silu_ready, (b, i)), ready=(b, 1) if i == 0 else None)
                        job(H2hi, H2lo, (ff_ready, (b, i)))
                    pe.wait_ge(ff_split, n(ff_split, (b, part[-1])))
                    if part is PARTS[-1]:
                        sums = square_sums(("ss", b, 2), SQ, sq_ready, (var_ready, (b, 2)))
                        next(sums)
                    for m in range(KT):
                        job(FFhi, FFlo, (added, (b, part[0], m)))
                        if part is PARTS[-1] and m >= 2:
                            next(sums)
                for _ in sums:
                    pass
                for j in range(JT):
                    for half in range(D // ROWS):
                        dst = take("bank", (outn_left, outn_right)[half], (b, j, half), ("yt", b, j, half))
                        for k in range(4):
                            kk = half * 4 + k
                            if j == 0:
                                pe.wait_ge(y_ready, n(y_ready, (b, kk)))
                            last = nc.tensor.transpose(dst[:, k * P:(k + 1) * P], X1T[:, kk, j * P:(j + 1) * P], IDENT[:, :])
                        last.then_inc(bank_full, made(bank_full, ("yt", b, j, half)))

        @block.scalar
        def _(act):
            SCALE = HD ** -0.5

            def full(key):
                act.wait_ge(bank_full, n(bank_full, key))
                return bank(key)

            def root(which):
                act.wait_ge(var_ready, n(var_ready, which))
                nc.scalar.activation(RV[:, :], RV[:, :], ACT.Sqrt).then_inc(std_ready, made(std_ready, which))

            def round_h(b, s, src, dst):
                for k in range(KT):
                    act.wait_ge(h_ready, n(h_ready, (b, s, k)))
                    nc.scalar.copy(dst[:, k, :], src[:, k, :]).then_inc(h_hi, made(h_hi, (b, s, k)))

            def q_heads(b, kind, m):
                bk = full((kind, b, m))
                for s in range(2):
                    r = slice(s * HD, (s + 1) * HD)
                    nc.scalar.mul(Q[r, 2 * m + s, :], bk[r, :], SCALE).then_inc(q_hi, made(q_hi, (b, kind, m, s)))

            for h in range(2 * HEADS):
                bk = full(("ft", h))
                nc.scalar.copy(FTAB[:, h, :], bk[:, 0:FTW]).then_inc(ftab_ready, made(ftab_ready, h))
            act.wait_ge(const_in, n(const_in, 11))
            nc.scalar.copy(WUKhi[:, :], WU[:, 0:2 * HD]).then_inc(wu_hi, 1)
            nc.scalar.copy(WUVhi[:, :], WU[:, 2 * HD:3 * HD]).then_inc(wu_hi, 1)

            def attend(b, kind):
                items = units(b, kind)
                ot = OTA if kind == "a" else OTB
                outs_due = []

                def exps(i):
                    u = items[i]
                    _, _, j, h0 = u
                    w = key_tiles(b, kind, j)[0] * P
                    act.wait_ge(negmax, n(negmax, u))
                    if kind == "a":
                        nc.scalar.activation(ES[:, j % 2, h0:h0 + 4], SN[:, i % 4, :], ACT.Exp)
                    for e in range(4 if kind == "a" else 1):
                        lg = LG[kind][i % 4][:, e * BAND:e * BAND + w]
                        last = nc.scalar.activation(lg, lg, ACT.Exp, bias=NM[:, i % 4, e:e + 1],
                                                    accum_out=RS[:, j % 2, h0 + e:h0 + e + 1])
                    last.then_inc(probs, made(probs, u))

                def out_copy(j):
                    act.wait_ge(trans_full, n(trans_full, ("on", b, kind, j)))
                    nc.scalar.copy(ot[:, :, j * P:(j + 1) * P], trans(("on", b, kind, j))[:, :, :]
                                   ).then_inc(ot_ready, made(ot_ready, (b, kind, j)))

                exps(0)
                exps(1)
                for i, u in enumerate(items):
                    grps = groups(u)
                    for g, grp in enumerate(grps):
                        key = (u, g)
                        t = n(trans_full, key) - 1
                        act.wait_ge(trans_full, t + 1)
                        if pt_last[t % 2] is not None:
                            act.wait_ge(values_done, n(values_done, pt_last[t % 2]))
                        pt_last[t % 2] = key
                        w = len(grp)
                        nc.scalar.copy(PThi[kind][t % 2][:, 0:w, :], trans(key)[:, 0:w, :]).then_inc(pt_hi, made(pt_hi, key))
                        if g == 0 and i + 2 < len(items):
                            exps(i + 2)
                    if outs_due:
                        out_copy(outs_due.pop())
                    if i + 1 == len(items) or items[i + 1][2] != u[2]:
                        outs_due.append(u[2])
                out_copy(outs_due.pop())

            pt_last = [None, None]
            for b in range(NB):
                rows = slice(b * ROWS, (b + 1) * ROWS)
                for k in range(KT):
                    act.wait_ge(xt_ready, n(xt_ready, (b, k)))
                    nc.scalar.activation(SQ[:, k, :], XT[:, k, :], ACT.Square).then_inc(sq_ready, made(sq_ready, (b, 0, k)))
                root((b, 0))
                round_h(b, 0, XT, HThi)
                for m in range(ET):
                    q_heads(b, "iq", m)
                bk = full(("ikw", b, 0))
                for s in range(2):
                    nc.scalar.copy(KIhi[s * HD:(s + 1) * HD, rows], bk[0:HD, :]).then_inc(k_hi, made(k_hi, (b, "ki", s)))
                act.wait_ge(k_ready, n(k_ready, (b, "ki", 1)))
                nc.scalar.mul(IWT[:, :], bk[HD:HD + HEADS, :], HEADS ** -0.5).then_inc(kw_ready, made(kw_ready, b))
                bk = full(("lat", b, 0))
                nc.scalar.copy(LT[:, :], bk[:, :]).then_inc(lat_ready, made(lat_ready, (b, 0)))
                nc.scalar.activation(LSQ[:, :], bk[:, :], ACT.Square).then_inc(sq_ready, made(sq_ready, (b, "kv", 0)))
                root((b, "kv"))
                act.wait_ge(lat_norm, n(lat_norm, b))
                nc.scalar.copy(LThi[:, :], LT[:, :]).then_inc(lat_hi, made(lat_hi, b))
                bk = full(("kb", b))
                nc.scalar.copy(KBhi[:, rows], bk[:, :]).then_inc(k_hi, made(k_hi, (b, "kb", 0)))
                bk = full(("vb", b))
                nc.scalar.copy(VB[:, b * JT:(b + 1) * JT, 0:HD], bk[:, 0:JT * HD].rearrange("p (j d) -> p j d", d=HD)
                               ).then_inc(v_hi, made(v_hi, (b, "vb", 0)))
                act.wait_ge(v_ready, n(v_ready, (b, "vb", 0)))
                for j in searched(b):
                    for h in range(HEADS):
                        for c, w in chunks((b * JT + j + 1) * P):
                            key = (b, j, h, c)
                            g = n(relu_ready, key) - 1
                            if g >= 2:
                                act.wait_ge(score_added, g - 1)
                            act.wait_ge(logits_full, n(logits_full, ("idx",) + key))
                            nc.scalar.activation(RB[:, g % 2, 0:w], logits(("idx",) + key)[:, 0:w], ACT.Relu
                                                 ).then_inc(relu_ready, made(relu_ready, key))
                for m in range(2 * KT):
                    bk = full(("gate", b, m))
                    g = b * KT + m // 2
                    if g >= 1:
                        act.wait_ge(gate_out[m % 2], 16 * g)
                    nc.scalar.activation(GS[:, m % 2, :], bk[:, :], ACT.Sigmoid).then_inc(gate_ready, made(gate_ready, (b, m)))
                    act.wait_ge(gate_ready, n(gate_ready, (b, m)))
                    act.dma_start(io["gates"][m], GS[:, m % 2, :]).then_inc(gate_out[m % 2], 16)
                if b:
                    nc.scalar.copy(AKhi[:, :, 0:P], AKhi[:, :, JT * P:(JT + 1) * P])
                    nc.scalar.copy(AKlo[:, :, 0:P], AKlo[:, :, JT * P:(JT + 1) * P])
                    nc.scalar.copy(VA[:, 0, :, :], VA[:, JT, :, :]).then_inc(carried, made(carried, b))
                    act.wait_ge(carried, n(carried, b))
                act.wait_ge(mask_ready, n(mask_ready, (b, JT - 1)))
                for m in range(ET):
                    q_heads(b, "aq", m)
                bk = full(("ak", b, 0))
                for g in range(KVH):
                    for s in range(2):
                        nc.scalar.copy(AKhi[s * HD:(s + 1) * HD, g, P:(JT + 1) * P], bk[g * HD:(g + 1) * HD, :]
                                       ).then_inc(k_hi, made(k_hi, (b, "ak", 2 * g + s)))
                bk = full(("av", b, 0))
                nc.scalar.copy(VAT[:, :], bk[:, :]).then_inc(vat_ready, made(vat_ready, b))
                bk = full(("va", b))
                nc.scalar.copy(VA[:, 1:JT + 1, :, 0:HD], bk[:, :].rearrange("p (j g d) -> p j g d", g=KVH, d=HD)
                               ).then_inc(v_hi, made(v_hi, (b, "va", 0)))
                for m in range(2):
                    act.wait_ge(gate_out[m], 16 * (b + 1) * KT)
                attend(b, "a")
                for m in range(ET):
                    q_heads(b, "bq", m)
                attend(b, "b")
                for s, ot in enumerate((OTA, OTB)):
                    act.wait_ge(ot_ready, n(ot_ready, (b, "b", JT - 1)))
                    nc.scalar.copy(OThi[s][:, :, :], ot[:, :, :]).then_inc(oh_ready, made(oh_ready, (b, s)))

                def load_gates(m):
                    if m >= 2:
                        act.wait_ge(gated, n(gated, (b, m - 2, 1)))
                    for s in range(2):
                        act.dma_start(GL[:, m % 2, s, :], io["gates"][s * KT + m]).then_inc(gate_in[m % 2], 16)
                        made(gate_in[m % 2], (b, m), 16)

                act.wait_ge(masked, n(masked, (units(b, "b")[-1], chunks_of(units(b, "b")[-1])[-1][0])))
                load_gates(0)
                load_gates(1)
                for m in range(KT):
                    act.wait_ge(merged, n(merged, (b, m)))
                    nc.scalar.copy(MGhi[:, m, :], M1[:, m % 2, :]).then_inc(m_hi, made(m_hi, (b, m)))
                    if m + 2 < KT:
                        load_gates(m + 2)
                act.wait_ge(bank_full, n(bank_full, ("br", b, KT - 1, 1)))
                for j in range(JT):
                    made(xr_in[j], b, 16)
                    act.dma_start(XR[:, j, :], x[0, b * ROWS + j * P:b * ROWS + (j + 1) * P, :]).then_inc(xr_in[j], 16)
                act.wait_ge(m_split, n(m_split, (b, KT - 1)))
                for m in range(KT):
                    bk = full(("wo", b, m))
                    nc.scalar.copy(X1T[:, m, :], bk[:, :]).then_inc(x1_ready, made(x1_ready, (b, m)))
                    nc.scalar.activation(SQ[:, m, :], bk[:, :], ACT.Square).then_inc(sq_ready, made(sq_ready, (b, 1, m)))
                root((b, 1))
                round_h(b, 1, H2F, H2hi)
                act.wait_ge(h_split, n(h_split, (b, 1, KT - 1)))
                for part in PARTS:
                    for i in part:
                        bk = full(("fg", b, i))
                        if i >= 2:
                            act.wait_ge(ff_ready, n(ff_ready, (b, i - 2)))
                        nc.scalar.activation(SL[:, i % 2, :], bk[:, :], ACT.Silu).then_inc(silu_ready, made(silu_ready, (b, i)))
                        act.wait_ge(ff_ready, n(ff_ready, (b, i)))
                        nc.scalar.copy(FFhi[:, i - part[0], :], FF[:, i % 2, :]).then_inc(ff_hi, made(ff_hi, (b, i)))
                for m in range(KT):
                    act.wait_ge(added, n(added, (b, PARTS[-1][0], m)))
                    nc.scalar.activation(SQ[:, m, :], X1T[:, m, :], ACT.Square).then_inc(sq_ready, made(sq_ready, (b, 2, m)))
                root((b, 2))
                for j in range(JT):
                    bk = full(("yt", b, j, 0))
                    nc.scalar.copy(OUTN[:, j, 0:ROWS], bk[:, :]).then_inc(outn_left, made(outn_left, (b, j, 0)))
                    act.wait_ge(outn_left, n(outn_left, (b, j, 0)))
                    act.wait_ge(outn_right, n(outn_right, (b, j, 1)))
                    act.dma_start(out[0, b * ROWS + j * P:b * ROWS + (j + 1) * P, :], OUTN[:, j, :]).then_inc(out_done[j], 16)

        @block.vector
        def _(dve):
            SCALE = HD ** -0.5

            def full(key):
                dve.wait_ge(bank_full, n(bank_full, key))
                return bank(key)

            def reciprocal_std(which, key, width):
                dve.wait_ge(logits_full, n(logits_full, key))
                bk = logits(key)[:, 0:ROWS]
                nc.vector.tensor_scalar(RV[:, :], bk, 1.0 / width, EPS, ALU.mult, ALU.add
                                        ).then_inc(var_ready, made(var_ready, which))
                dve.wait_ge(std_ready, n(std_ready, which))
                nc.vector.reciprocal(RV[:, :], RV[:, :]).then_inc(rinv_ready, made(rinv_ready, which))
                dve.wait_ge(rinv_ready, n(rinv_ready, which))

            def normed(b, s, src, dst, gain, hi, lo):
                reciprocal_std((b, s), ("ss", b, s), D)
                for k in range(KT + 2):
                    if k < KT:
                        nc.vector.scalar_tensor_tensor(dst[:, k, :], src[:, k, :], gain[:, k:k + 1], RV[:, :], ALU.mult,
                                                       ALU.mult).then_inc(h_ready, made(h_ready, (b, s, k)))
                    k -= 2
                    if k < 0:
                        continue
                    dve.wait_ge(h_hi, n(h_hi, (b, s, k)))
                    nc.vector.tensor_tensor(lo[:, k, :], dst[:, k, :], hi[:, k, :].bitcast(f32), ALU.subtract
                                            ).then_inc(h_split, made(h_split, (b, s, k)))

            def q_heads(b, kind, m):
                bk = full((kind, b, m))
                for s in range(2):
                    r, o = slice(s * HD, (s + 1) * HD), slice((1 - s) * HD, (2 - s) * HD)
                    if s == 0:
                        dve.wait_ge(q_hi, n(q_hi, (b, kind, m, 1)))
                    nc.vector.scalar_tensor_tensor(Q[o, 2 * m + s, :], bk[r, :], SCALE, Q[r, 2 * m + s, :].bitcast(f32),
                                                   ALU.mult, ALU.subtract).then_inc(q_ready, made(q_ready, (b, kind, m, s)))

            nc.vector.memset(ONES[:, :], 1.0).then_inc(ones_set, 1)
            dve.wait_ge(const_in, n(const_in, 11))
            dve.wait_ge(wu_hi, 2)
            nc.vector.tensor_tensor(WUKlo[:, :], WU[:, 0:2 * HD], WUKhi[:, :].bitcast(f32), ALU.subtract).then_inc(wu_ready, 1)
            nc.vector.tensor_tensor(WUVlo[:, :], WU[:, 2 * HD:3 * HD], WUVhi[:, :].bitcast(f32), ALU.subtract
                                    ).then_inc(wu_ready, 1)
            dve.wait_ge(taba_in, 32)
            for h in range(HEADS):
                nc.vector.tensor_tensor(TABA[:, h, :], TABA[:, h, :], BANDM[:, :], ALU.add).then_inc(taba_ready, 1)

            step = [0]

            def topk(b):
                js = searched(b)
                col = slice(js[0], JT)

                def stepped(ins):
                    step[0] += 1
                    ins.then_inc(topk_step, 1)
                    return step[0]

                def count(threshold, op):
                    for j in js:
                        w = (b * JT + j + 1) * P
                        last = stepped(nc.vector.tensor_scalar(JUNK[:, j, 0:w], SC[:, j, 0:w], threshold(j), None,
                                                               op, ALU.add, accum_out=CNT[:, j:j + 1]))
                    dve.wait_ge(topk_step, last)

                count(lambda j: 0.0, ALU.is_ge)
                dve.wait_ge(topk_step, stepped(nc.vector.tensor_scalar(
                    TAKE[:, col], CNT[:, col], float(TOPK), -1.0, ALU.is_ge, ALU.add)))
                stepped(nc.vector.tensor_scalar(SIGN[:, col], TAKE[:, col], -2 ** 31, None, ALU.bitwise_or))
                stepped(nc.vector.tensor_scalar(PREF[:, col], TAKE[:, col], -1, -2 ** 31, ALU.bitwise_xor, ALU.bitwise_and))
                dve.wait_ge(topk_step, stepped(nc.vector.memset(BIT[:, :], 2 ** 30)))
                base, each = step[0], len(js) + 4
                with dve.Fori(0, 31) as it:
                    s0 = base + it * each
                    nc.vector.scalar_tensor_tensor(THR[:, col], PREF[:, col], BIT[:, 0:1], SIGN[:, col],
                                                   ALU.bitwise_or, ALU.bitwise_xor).then_inc(topk_step, 1)
                    dve.wait_ge(topk_step, s0 + 1)
                    for j in js:
                        w = (b * JT + j + 1) * P
                        nc.vector.tensor_scalar(JUNK[:, j, 0:w], SC[:, j, 0:w], THR[:, j:j + 1].bitcast(f32), None,
                                                ALU.is_ge, ALU.add, accum_out=CNT[:, j:j + 1]).then_inc(topk_step, 1)
                    dve.wait_ge(topk_step, s0 + 1 + len(js))
                    nc.vector.tensor_scalar(TAKE[:, col], CNT[:, col], float(TOPK), -1.0, ALU.is_ge, ALU.mult
                                            ).then_inc(topk_step, 1)
                    dve.wait_ge(topk_step, s0 + 2 + len(js))
                    nc.vector.scalar_tensor_tensor(PREF[:, col], TAKE[:, col], BIT[:, 0:1], PREF[:, col],
                                                   ALU.bitwise_and, ALU.bitwise_or).then_inc(topk_step, 1)
                    dve.wait_ge(topk_step, s0 + 3 + len(js))
                    nc.vector.tensor_scalar(BIT[:, :], BIT[:, :], 1, None, ALU.logical_shift_right).then_inc(topk_step, 1)
                    dve.wait_ge(topk_step, s0 + 4 + len(js))
                step[0] += 31 * each
                dve.wait_ge(topk_step, stepped(nc.vector.tensor_tensor(THR[:, col], PREF[:, col], SIGN[:, col], ALU.bitwise_xor)))
                count(lambda j: THR[:, j:j + 1].bitcast(f32), ALU.is_gt)
                dve.wait_ge(topk_step, stepped(nc.vector.tensor_scalar(
                    NEED[:, col], CNT[:, col], -1.0, float(TOPK), ALU.mult, ALU.add)))
                for j in js:
                    w = (b * JT + j + 1) * P
                    thr = THR[:, j:j + 1].bitcast(f32)
                    s, e, c = SC[:, j, 0:w], EQ[:, 0:w], CS[:, 0:w]
                    dve.wait_ge(topk_step, stepped(nc.vector.tensor_scalar(e, s, thr, None, ALU.is_equal)))
                    dve.wait_ge(topk_step, stepped(nc.vector.tensor_tensor_scan(c, e, e, 0.0, ALU.add, ALU.max)))
                    dve.wait_ge(topk_step, stepped(nc.vector.scalar_tensor_tensor(
                        e, c, NEED[:, j:j + 1], e, ALU.is_le, ALU.mult)))
                    dve.wait_ge(topk_step, stepped(nc.vector.scalar_tensor_tensor(s, s, thr, e, ALU.is_gt, ALU.add)))
                    nc.vector.tensor_scalar(MASK[:, j, 0:w], s, -1.0, -NEG, ALU.add, ALU.mult
                                            ).then_inc(mask_ready, made(mask_ready, (b, j)))

            def attend(b, kind):
                items = units(b, kind)

                def mask_and_max(i):
                    u = items[i]
                    _, _, j, h0 = u
                    w = key_tiles(b, kind, j)[0] * P
                    if i >= 4:
                        before = items[i - 4]
                        dve.wait_ge(trans_full, n(trans_full, (before, len(groups(before)) - 1)))
                    for s, (c, cw) in enumerate(chunks_of(u)):
                        dve.wait_ge(logits_full, n(logits_full, (u, c)))
                        src = logits((u, c))
                        if kind == "a":
                            for e in range(4):
                                o = e * BAND
                                last = nc.vector.tensor_tensor_reduce(
                                    LG[kind][i % 4][:, o:o + w], src[:, o:o + w], TABA[:, h0 + e, BAND - w:BAND], 1.0,
                                    SINK[:, h0 + e:h0 + e + 1], ALU.add, ALU.max, MX[:, i % 4, e:e + 1])
                        else:
                            if s:
                                dve.wait_ge(masked, n(masked, (u, 0)))
                            last = nc.vector.tensor_tensor_reduce(
                                LG[kind][i % 4][:, c:c + cw], src[:, 0:cw], MASK[:, j, c:c + cw], 1.0,
                                MX[:, i % 4, 0:1] if s else LOWEST, ALU.add, ALU.max, MX[:, i % 4, s:s + 1])
                        last.then_inc(masked, made(masked, (u, c)))
                        if c + cw < chunks_of(u)[-1][0] + chunks_of(u)[-1][1]:
                            yield
                    dve.wait_ge(masked, n(masked, (u, c)))
                    e = slice(0, 4) if kind == "a" else slice(s, s + 1)
                    o = slice(0, 4) if kind == "a" else slice(0, 1)
                    last = nc.vector.tensor_scalar(NM[:, i % 4, o], MX[:, i % 4, e], -1.0, None, ALU.mult)
                    if kind == "a":
                        last.then_inc(o_step, made(o_step, ("nm", u)))
                        dve.wait_ge(o_step, n(o_step, ("nm", u)))
                        last = nc.vector.tensor_tensor(SN[:, i % 4, :], NM[:, i % 4, :], SINK[:, h0:h0 + 4], ALU.add)
                    last.then_inc(negmax, made(negmax, u))
                    yield

                def outputs(j, g, u):
                    key = ("o", b, kind, j, g)
                    hs = slice(4 * g, 4 * g + 4)
                    p = j % 2
                    dve.wait_ge(values_done, n(values_done, (u, len(groups(u)) - 1)))
                    if kind == "a":
                        nc.vector.tensor_tensor(RS[:, p, hs], RS[:, p, hs], ES[:, p, hs], ALU.add
                                                ).then_inc(o_step, made(o_step, key + (3,)))
                        dve.wait_ge(o_step, n(o_step, key + (3,)))
                    nc.vector.reciprocal(RR[:, p, hs], RS[:, p, hs]).then_inc(o_step, made(o_step, key + (0,)))
                    dve.wait_ge(o_step, n(o_step, key + (0,)))
                    bk = bank(key)[:, :].rearrange("p (h d) -> p h d", h=4)
                    r = RR[:, p, hs].unsqueeze(2).to_broadcast([P, 4, HD])
                    nc.vector.tensor_tensor(OA[kind][:, :, :], bk[:, :, 0:HD], r, ALU.mult
                                            ).then_inc(o_step, made(o_step, key + (1,)))
                    nc.vector.tensor_tensor(OB[kind][:, :, :], bk[:, :, HD:P], r, ALU.mult
                                            ).then_inc(o_step, made(o_step, key + (2,)))
                    dve.wait_ge(o_step, n(o_step, key + (2,)))
                    if j >= 1:
                        dve.wait_ge(trans_full, n(trans_full, ("on", b, kind, j - 1)))
                    nc.vector.tensor_tensor(ON[kind][:, hs, :], OA[kind][:, :, :], OB[kind][:, :, :], ALU.add
                                            ).then_inc(o_ready, made(o_ready, (b, kind, j, g)))
                    dve.wait_ge(o_ready, n(o_ready, (b, kind, j, g)))

                for i in range(3):
                    for _ in mask_and_max(i):
                        pass
                for i, u in enumerate(items):
                    _, _, j, h0 = u
                    ahead = mask_and_max(i + 3) if i + 3 < len(items) else iter(())
                    for g, grp in enumerate(groups(u)):
                        key = (u, g)
                        t, w = n(trans_full, key) - 1, len(grp)
                        dve.wait_ge(pt_hi, n(pt_hi, key))
                        nc.vector.tensor_tensor(PTlo[kind][t % 2][:, 0:w, :], trans(key)[:, 0:w, :],
                                                PThi[kind][t % 2][:, 0:w, :].bitcast(f32), ALU.subtract
                                                ).then_inc(pt_ready, made(pt_ready, key))
                        if g % 2:
                            next(ahead, None)
                    for _ in ahead:
                        pass
                    if kind == "a" or h0 % 4 == 3:
                        outputs(j, h0 // 4, u)

            for b in range(NB):
                rows = slice(b * ROWS, (b + 1) * ROWS)
                if b:
                    for j in range(JT):
                        dve.wait_ge(out_done[j], 16 * b)
                else:
                    dve.wait_ge(ftab_out, 16)
                for k in range(KT):
                    bk = full(("xt", b, k))
                    nc.vector.tensor_copy(XT[:, k, :], bk[:, :]).then_inc(xt_ready, made(xt_ready, (b, k)))
                normed(b, 0, XT, XT, G1, HThi, HTlo)
                for m in range(ET):
                    q_heads(b, "iq", m)
                bk = full(("ikw", b, 0))
                for s in range(2):
                    dve.wait_ge(k_hi, n(k_hi, (b, "ki", 1)))
                    nc.vector.tensor_tensor(KIlo[s * HD:(s + 1) * HD, rows], bk[0:HD, :], KIhi[0:HD, rows].bitcast(f32),
                                            ALU.subtract).then_inc(k_ready, made(k_ready, (b, "ki", s)))
                reciprocal_std((b, "kv"), ("kvss", b, "kv"), P)
                nc.vector.scalar_tensor_tensor(LT[:, :], LT[:, :], GKV[:, 0:1], RV[:, :], ALU.mult, ALU.mult
                                               ).then_inc(lat_norm, made(lat_norm, b))
                bk = full(("iwt", b))
                nc.vector.tensor_copy(IW[:, :, :], bk[:, 0:JT * HEADS].rearrange("p (j h) -> p j h", h=HEADS)
                                      ).then_inc(iw_ready, made(iw_ready, b))
                dve.wait_ge(lat_hi, n(lat_hi, b))
                nc.vector.tensor_tensor(LTlo[:, :], LT[:, :], LThi[:, :].bitcast(f32), ALU.subtract
                                        ).then_inc(lat_split, made(lat_split, b))
                bk = full(("kb", b))
                dve.wait_ge(k_hi, n(k_hi, (b, "kb", 0)))
                nc.vector.tensor_tensor(KBlo[:, rows], bk[:, :], KBhi[:, rows].bitcast(f32), ALU.subtract
                                        ).then_inc(k_ready, made(k_ready, (b, "kb", 0)))
                bk = full(("vb", b))
                dve.wait_ge(v_hi, n(v_hi, (b, "vb", 0)))
                v = VB[:, b * JT:(b + 1) * JT, :]
                nc.vector.tensor_tensor(v[:, :, HD:P], bk[:, 0:JT * HD].rearrange("p (j d) -> p j d", d=HD),
                                        v[:, :, 0:HD].bitcast(f32), ALU.subtract).then_inc(v_ready, made(v_ready, (b, "vb", 0)))
                dve.wait_ge(iw_ready, n(iw_ready, b))
                for j in searched(b):
                    for h in range(HEADS):
                        for c, w in chunks((b * JT + j + 1) * P):
                            key = (b, j, h, c)
                            g = n(relu_ready, key) - 1
                            dve.wait_ge(relu_ready, g + 1)
                            r, s, iw = RB[:, g % 2, 0:w], SC[:, j, c:c + w], IW[:, j, h:h + 1]
                            if h == 0:
                                ins = nc.vector.tensor_scalar(s, r, iw, None, ALU.mult)
                            else:
                                dve.wait_ge(score_added, n(score_added, (b, j, h - 1, c)))
                                ins = nc.vector.scalar_tensor_tensor(s, r, iw, s, ALU.mult, ALU.add)
                            ins.then_inc(score_added, made(score_added, key))
                    w = (b * JT + j + 1) * P
                    dve.wait_ge(score_added, n(score_added, (b, j, HEADS - 1, chunks(w)[-1][0])))
                    nc.vector.memset(SC[0:HD, j, w - HD:w], NEG).then_inc(score_ready, made(score_ready, (b, j)))
                if searched(b):
                    dve.wait_ge(score_ready, n(score_ready, (b, searched(b)[-1])))
                    dve.wait_ge(logits_full, n(logits_full, ("idx", b, JT - 1, HEADS - 1, chunks((b + 1) * ROWS)[-1][0])))
                for j in range(JT):
                    if j not in searched(b):
                        w = (b * JT + j + 1) * P
                        step[0] += 1
                        nc.vector.memset(MASK[:, j, 0:w], 0.0).then_inc(topk_step, 1)
                        dve.wait_ge(topk_step, step[0])
                        nc.vector.memset(MASK[0:HD, j, w - HD:w], NEG).then_inc(mask_ready, made(mask_ready, (b, j)))
                if searched(b):
                    topk(b)
                for m in range(ET):
                    q_heads(b, "aq", m)
                bk = full(("ak", b, 0))
                for g in range(KVH):
                    for s in range(2):
                        dve.wait_ge(k_hi, n(k_hi, (b, "ak", 2 * KVH - 1)))
                        hi = AKhi[s * HD:(s + 1) * HD, g, P:(JT + 1) * P]
                        nc.vector.tensor_tensor(AKlo[s * HD:(s + 1) * HD, g, P:(JT + 1) * P], bk[g * HD:(g + 1) * HD, :],
                                                hi.bitcast(f32), ALU.subtract
                                                ).then_inc(k_ready, made(k_ready, (b, "ak", 2 * g + s)))
                bk = full(("va", b))
                dve.wait_ge(v_hi, n(v_hi, (b, "va", 0)))
                v = VA[:, 1:JT + 1, :, :]
                nc.vector.tensor_tensor(v[:, :, :, HD:P], bk[:, :].rearrange("p (j g d) -> p j g d", g=KVH, d=HD),
                                        v[:, :, :, 0:HD].bitcast(f32), ALU.subtract).then_inc(v_ready, made(v_ready, (b, "va", 0)))
                dve.wait_ge(taba_ready, HEADS)
                attend(b, "a")
                for m in range(ET):
                    q_heads(b, "bq", m)
                dve.wait_ge(mask_ready, n(mask_ready, (b, JT - 1)))
                attend(b, "b")
                for s, ot in enumerate((OTA, OTB)):
                    dve.wait_ge(oh_ready, n(oh_ready, (b, s)))
                    nc.vector.tensor_tensor(OTlo[s][:, :, :], ot[:, :, :], OThi[s][:, :, :].bitcast(f32), ALU.subtract
                                            ).then_inc(os_ready, made(os_ready, (b, s)))
                dve.wait_ge(os_ready, n(os_ready, (b, 1)))

                def split_m(m):
                    dve.wait_ge(m_hi, n(m_hi, (b, m)))
                    nc.vector.tensor_tensor(MGlo[:, m, :], M1[:, m % 2, :], MGhi[:, m, :].bitcast(f32), ALU.subtract
                                            ).then_inc(m_split, made(m_split, (b, m)))

                for m in range(KT):
                    dve.wait_ge(gate_in[m % 2], n(gate_in[m % 2], (b, m)))
                    if m >= 2:
                        dve.wait_ge(m_split, n(m_split, (b, m - 2)))
                    for s, dst in enumerate((M1, M2)):
                        bk = full(("br", b, m, s))
                        nc.vector.tensor_tensor(dst[:, m % 2, :], bk[:, :], GL[:, m % 2, s, :], ALU.mult
                                                ).then_inc(gated, made(gated, (b, m, s)))
                    dve.wait_ge(gated, n(gated, (b, m, 1)))
                    nc.vector.tensor_tensor(M1[:, m % 2, :], M1[:, m % 2, :], M2[:, m % 2, :], ALU.add
                                            ).then_inc(merged, made(merged, (b, m)))
                    if m:
                        split_m(m - 1)
                split_m(KT - 1)
                normed(b, 1, X1T, H2F, G2, H2hi, H2lo)
                for part in PARTS:
                    for i in part:
                        bk = full(("fu", b, i))
                        dve.wait_ge(silu_ready, n(silu_ready, (b, i)))
                        if i >= 2:
                            dve.wait_ge(ff_split, n(ff_split, (b, i - 2)))
                        nc.vector.tensor_tensor(FF[:, i % 2, :], bk[:, :], SL[:, i % 2, :], ALU.mult
                                                ).then_inc(ff_ready, made(ff_ready, (b, i)))
                        dve.wait_ge(ff_hi, n(ff_hi, (b, i)))
                        nc.vector.tensor_tensor(FFlo[:, i - part[0], :], FF[:, i % 2, :], FFhi[:, i - part[0], :].bitcast(f32),
                                                ALU.subtract).then_inc(ff_split, made(ff_split, (b, i)))
                    for m in range(KT):
                        bk = full(("fd", b, part[0], m))
                        if part[0]:
                            dve.wait_ge(added, n(added, (b, part[0] - SLOTS, m)))
                        nc.vector.tensor_tensor(X1T[:, m, :], bk[:, :], X1T[:, m, :], ALU.add
                                                ).then_inc(added, made(added, (b, part[0], m)))
                reciprocal_std((b, 2), ("ss", b, 2), D)
                for k in range(KT):
                    nc.vector.scalar_tensor_tensor(X1T[:, k, :], X1T[:, k, :], GF[:, k:k + 1], RV[:, :], ALU.mult,
                                                   ALU.mult).then_inc(y_ready, made(y_ready, (b, k)))
                for j in range(JT):
                    bk = full(("yt", b, j, 1))
                    nc.vector.tensor_copy(OUTN[:, j, ROWS:2 * ROWS], bk[:, :]).then_inc(outn_right, made(outn_right, (b, j, 1)))

    return C.seen


def _bucket(rel):
    starts = [8, 12, 16, 23, 32, 46, 64, 91]
    near = np.abs(rel)
    large = 7 + sum((near >= s).astype(np.int64) for s in starts)
    return np.where(rel > 0, BUCKETS // 2, 0) + np.where(near < 8, near, large)


def _constants():
    hot = np.zeros((BUCKETS, 2 * FTW), np.float32)
    r = np.arange(FTW)
    bucket = _bucket(np.minimum(r - (BAND - 1), P - 1))
    hot[bucket, r] = 1.0
    hot[bucket, FTW + r] = 1.0
    hot[FAR_BUCKET, FTW:] -= 1.0
    band = np.zeros((P, BAND), np.float32)
    half = P // 2
    band[:half, :half] = NEG
    band[:half, 3 * half:] = NEG
    band[half:, :P] = NEG
    return {"hot": hot, "band": band, "ident": np.eye(P, dtype=np.float32)}


_INS = ["x", "norm1_g", "w_in", "rel_bias", "sinks", "kv_norm_g", "w_uk", "w_uv", "w_branch_a", "w_branch_b",
        "w_out", "norm2_g", "w_ffn_gate", "w_ffn_up", "w_ffn_down", "norm_f_g"]


def build(nc, shapes, known):
    f32 = mybir.dt.float32
    io = {name: nc.dram_tensor(f"in_{name}", shape, f32, kind="ExternalInput").ap() for name, shape in shapes.items()}
    io["out"] = nc.dram_tensor("out_0", shapes["x"], f32, kind="ExternalOutput").ap()
    io["ft"] = nc.dram_tensor("ft", (2 * HEADS, P, FTW), f32).ap()
    io["gates"] = nc.dram_tensor("gates", (2 * shapes["x"][2] // P, P, ROWS), f32).ap()
    return trunk_program(nc, io, known)


def kernel(**inputs):
    import concourse.bacc as bacc
    from concourse.bass_utils import run_bass_kernel_spmd

    arrays = {name: np.ascontiguousarray(inputs[name]) for name in _INS}
    arrays.update(_constants())
    shapes = {name: a.shape for name, a in arrays.items()}
    counts = build(bacc.Bacc("TRN2", target_bir_lowering=False, num_devices=1), shapes, {})
    nc = bacc.Bacc("TRN2", target_bir_lowering=False, num_devices=1)
    build(nc, shapes, counts)
    r = run_bass_kernel_spmd(nc, [{f"in_{name}": a for name, a in arrays.items()}], core_ids=[0])
    return r.results[0]["out_0"]
```

```python
import numpy as np
import concourse.bass as bass
from concourse import mybir
from contextlib import ExitStack

P = 128
ROWS = 512
JT = ROWS // P
HEADS, HD = 8, 64
KVH = 2
NEG = -1e30
EPS = 1e-6
LOWEST = -3e38
SLOTS = 8
LGW = 1024
BUCKETS, FAR_BUCKET = 32, 15
BAND = 2 * P
FTW = 384


class Count:

    def __init__(self, known):
        self.known, self.seen, self.now = known, {}, {}

    def made(self, sem, key, by=1):
        self.now[sem.name] = self.now.get(sem.name, 0) + by
        self.seen[(sem.name, key)] = self.now[sem.name]
        return by

    def n(self, sem, key):
        return self.known.get((sem.name, key), 1)


def trunk_program(nc, io, known):
    f32, f32r, bf16, i32 = mybir.dt.float32, mybir.dt.float32r, mybir.dt.bfloat16, mybir.dt.int32
    ACT, ALU = mybir.ActivationFunctionType, mybir.AluOpType
    x, out = io["x"], io["out"]
    SEQ, D = x.shape[1], x.shape[2]
    DFF = io["w_ffn_gate"].shape[2]
    NB = SEQ // ROWS
    KT = D // P
    ET = HEADS * HD // P
    FT = DFF // P
    TOPK = min(256, SEQ // 4)
    TK = TOPK // P
    PARTS = [range(a, min(a + SLOTS, FT)) for a in range(0, FT, SLOTS)]
    C = Count(known)
    n, made = C.n, C.made

    w_in = io["w_in"][0]
    COL = dict(aq=0, ak=512, av=640, bq=768, lat=1280, iq=1408, ikw=1920, gate=1992)

    with ExitStack() as ctx:
        top = (nc.sbuf_base + 63) // 64 * 64
        place = [top]

        def at(name, shape, dt, offset):
            return nc.alloc_sbuf_tensor_at(name, shape, dt, offset=offset)

        def new(name, shape, dt):
            size = int(np.prod(shape[1:])) * (2 if dt == bf16 else 4)
            offset = place[0]
            place[0] += (size + 31) // 32 * 32
            return at(name, shape, dt, offset)

        def region(size):
            offset = place[0]
            place[0] += size
            return offset

        KIhi, KIlo = new("KIhi", [P, SEQ], f32r), new("KIlo", [P, SEQ], f32r)
        KBhi, KBlo = new("KBhi", [P, SEQ], f32r), new("KBlo", [P, SEQ], f32r)
        VB = new("VB", [P, SEQ // P, P], f32r)
        AKhi, AKlo = (new(s, [P, KVH, (JT + 1) * P], f32r) for s in ("AKhi", "AKlo"))
        VA = new("VA", [P, JT + 1, KVH, P], f32r)
        TABA, TABB = new("TABA", [P, HEADS, BAND], f32), new("TABB", [P, HEADS, BAND], f32)
        IDENT, ONES = new("IDENT", [P, P], f32), new("ONES", [P, P], f32)
        WRAW = [new(f"WRAW{i}", [P, SLOTS, P], f32) for i in range(2)]
        WHI = [new(f"WHI{i}", [P, SLOTS, P], f32r) for i in range(2)]
        WLO = [new(f"WLO{i}", [P, SLOTS, P], f32r) for i in range(2)]
        WUKhi, WUKlo = new("WUKhi", [P, P], f32r), new("WUKlo", [P, P], f32r)
        WUVhi, WUVlo = new("WUVhi", [P, HD], f32r), new("WUVlo", [P, HD], f32r)
        G1, G2, GF = (new(s, [P, KT], f32) for s in ("G1", "G2", "GF"))
        GKV, SINK = new("GKV", [P, 1], f32), new("SINK", [P, HEADS], f32)
        IW = new("IW", [P, JT, HEADS], f32)
        CNT, NEED, SHIFT = (new(s, [P, JT], f32) for s in ("CNT", "NEED", "SHIFT"))
        PREF, SIGN, THR, TAKE = (new(s, [P, JT], i32) for s in ("PREF", "SIGN", "THR", "TAKE"))
        BIT = [new(f"BIT{i}", [P, 1], i32) for i in range(2)]
        MORE, LOW, CARRY = (new(s, [P, JT], i32) for s in ("MORE", "LOW", "CARRY"))
        MX, NM, SN = (new(s, [P, 4, 4], f32) for s in ("MX", "NM", "SN"))
        RS, ES, RR = new("RS", [P, 2, HEADS], f32), new("ES", [P, 2, HEADS], f32), new("RR", [P, 2, HEADS], f32)
        RV = new("RV", [P, ROWS], f32)
        rO, r1, rQ, rM, r3 = region(8192), region(32768), region(16384), region(16384), region(32768)
        assert place[0] <= nc.sbuf_usable_end, place[0] - nc.sbuf_usable_end
        OTA = at("OTA", [P, ET, ROWS], f32, rO)
        GS = at("GS", [P, 2, ROWS], f32, rO)
        IWT = at("IWT", [HEADS, ROWS], f32, rO)
        QAT = at("QAT", [P, 2, ROWS], f32, rO)
        VAT, KAT = at("VAT", [P, ROWS], f32, rO + 4096), at("KAT", [P, ROWS], f32, rO + 6144)
        XN = at("XN", [P, JT, D], f32, r1)
        XT = at("XT", [P, KT, ROWS], f32, r1 + 16384)
        SC = at("SC", [P, JT, SEQ], f32, r1)
        LG = dict(a=[at(f"LGa{i}", [P, LGW], f32, r1 + 4096 * i) for i in range(4)],
                  b=[at(f"LGb{i}", [P, SEQ], f32, r1 + 8192 * i) for i in range(4)])
        r_pt, r_on = dict(a=r1 + 16384, b=r3 + 12288), dict(a=r1 + 24576, b=r3 + 8192)
        PThi = {k: [at(f"PThi{k}{i}", [P, 4, P], f32r, r + 2048 * i) for i in range(2)] for k, r in r_pt.items()}
        PTlo = {k: [at(f"PTlo{k}{i}", [P, 4, P], f32r, r + 4096 + 2048 * i) for i in range(2)] for k, r in r_pt.items()}
        ON = {k: [at(f"ON{k}{i}", [P, HEADS, HD], f32, r + 12288 * i if k == "b" else r + 4096 * i) for i in range(2)]
              for k, r in r_on.items()}
        OA = {k: at("OA" + k, [P, 4, HD], f32, r + 2048) for k, r in r_on.items()}
        OB = {k: at("OB" + k, [P, 4, HD], f32, r + 3072) for k, r in r_on.items()}
        OThi = [at(f"OThi{i}", [P, ET, ROWS], f32r, r1 + 8192 * i) for i in range(2)]
        OTlo = [at(f"OTlo{i}", [P, ET, ROWS], f32r, r1 + 16384 + 8192 * i) for i in range(2)]
        X1T = at("X1T", [P, KT, ROWS], f32, r1)
        XR = at("XR", [P, JT, D], f32, r1 + 16384)
        H2F = at("H2F", [P, KT, ROWS], f32, r1 + 16384)
        SL = at("SL", [P, 2, ROWS], f32, r1 + 16384)
        FF = at("FF", [P, 2, ROWS], f32, r1 + 16384 + 4096)
        OUTN = at("OUTN", [P, JT, D], f32, r1 + 16384)
        FTAB = at("FTAB", [P, 2 * HEADS, FTW], f32, r1)
        Q = at("Q", [P, HEADS, ROWS], f32r, rQ)
        JUNK = at("JUNK", [P, JT, SEQ], bf16, rQ)
        EQ, CS = at("EQ", [P, SEQ], f32, rQ), at("CS", [P, SEQ], f32, rQ + 8192)
        H2hi, H2lo = at("H2hi", [P, KT, ROWS], f32r, rQ), at("H2lo", [P, KT, ROWS], f32r, rM)
        SQ = at("SQ", [P, KT, ROWS], f32, rM)
        LT, LSQ = at("LT", [P, ROWS], f32, rM), at("LSQ", [P, ROWS], f32, rM + 2048)
        LThi, LTlo = at("LThi", [P, ROWS], f32r, rM + 4096), at("LTlo", [P, ROWS], f32r, rM + 6144)
        RB = at("RB", [P, 2, LGW], f32, rM)
        MASK = at("MASK", [P, JT, SEQ], bf16, rM)
        GL = at("GL", [P, 2, 2, ROWS], f32, rM)
        M1, M2 = at("M1", [P, 2, ROWS], f32, rM + 8192), at("M2", [P, 2, ROWS], f32, rM + 12288)
        HThi, HTlo = at("HThi", [P, KT, ROWS], f32r, r3), at("HTlo", [P, KT, ROWS], f32r, r3 + 16384)
        OTB = at("OTB", [P, ET, ROWS], f32, r3)
        MGhi, MGlo = at("MGhi", [P, KT, ROWS], f32r, r3), at("MGlo", [P, KT, ROWS], f32r, r3 + 16384)
        FFhi, FFlo = at("FFhi", [P, SLOTS, ROWS], f32r, r3), at("FFlo", [P, SLOTS, ROWS], f32r, r3 + 16384)
        HOT = at("HOT", [BUCKETS, 2 * FTW], f32, r3)
        RELB = at("RELB", [BUCKETS, 2 * HEADS], f32, r3 + 3072)
        BANDM = at("BANDM", [P, BAND], f32, r3 + 4096)
        WU = at("WU", [P, 2 * HD + HD], f32, r3 + 8192)

        BANK = [ctx.enter_context(nc.psum_tensor(f"BANK{i}", [P, ROWS], f32)) for i in range(2)]
        LP = [ctx.enter_context(nc.psum_tensor(f"LP{i}", [P, LGW], f32)) for i in range(2)]
        TP = [ctx.enter_context(nc.psum_tensor(f"TP{i}", [P, 4, P], f32)) for i in range(2)]

        def sem(name):
            return ctx.enter_context(nc.semaphore(name))

        const_in, ones_set = sem("const_in"), sem("ones_set")
        ftab_ready, ftab_out, taba_in, taba_ready = (sem(s) for s in ("ftab_ready", "ftab_out", "taba_in", "taba_ready"))
        wu_hi, wu_ready = sem("wu_hi"), sem("wu_ready")
        w_in_sem = [sem(f"w_loaded{i}") for i in range(2)]
        w_hi, w_split = sem("w_hi"), sem("w_split")
        bank_full, logits_full, trans_full = sem("bank_full"), sem("logits_full"), sem("trans_full")
        x_in = [sem(f"x_in{j}") for j in range(JT)]
        xr_in = [sem(f"xr_in{j}") for j in range(JT)]
        xt_ready, sq_ready = sem("xt_ready"), sem("sq_ready")
        var_ready, std_ready, rinv_ready = sem("var_ready"), sem("std_ready"), sem("rinv_ready")
        h_ready, h_hi, h_split = sem("h_ready"), sem("h_hi"), sem("h_split")
        q_hi, q_ready = sem("q_hi"), sem("q_ready")
        k_hi, k_ready, kw_ready, iw_ready = sem("k_hi"), sem("k_ready"), sem("kw_ready"), sem("iw_ready")
        lat_ready, lat_norm, lat_hi, lat_split = sem("lat_ready"), sem("lat_norm"), sem("lat_hi"), sem("lat_split")
        v_hi, v_ready, vat_ready, carried = sem("v_hi"), sem("v_ready"), sem("vat_ready"), sem("carried")
        kat_ready, qat_ready = sem("kat_ready"), sem("qat_ready")
        relu_ready, score_added, score_ready = sem("relu_ready"), sem("score_added"), sem("score_ready")
        topk_step, dropped, mask_ready = sem("topk_step"), sem("dropped"), sem("mask_ready")
        threshold_set, tiles_counted = sem("threshold_set"), sem("tiles_counted")
        gate_ready = sem("gate_ready")
        gate_out = [sem(f"gate_out{i}") for i in range(2)]
        gate_in = [sem(f"gate_in{i}") for i in range(2)]
        masked, negmax, probs, values_done = sem("masked"), sem("negmax"), sem("probs"), sem("values_done")
        pt_hi, pt_ready = sem("pt_hi"), sem("pt_ready")
        o_step, o_ready, ot_ready = sem("o_step"), sem("o_ready"), sem("ot_ready")
        oh_ready, os_ready = sem("oh_ready"), sem("os_ready")
        gated, merged, m_hi, m_split = sem("gated"), sem("merged"), sem("m_hi"), sem("m_split")
        x1_ready = sem("x1_ready")
        silu_ready, ff_ready, ff_hi, ff_split, added = (sem(s) for s in ("silu_ready", "ff_ready", "ff_hi", "ff_split", "added"))
        y_ready, outn_left, outn_right = sem("y_ready"), sem("outn_left"), sem("outn_right")
        out_done = [sem(f"out_done{j}") for j in range(JT)]

        def bank(key):
            return BANK[C.known.get(("bank use", key), 0) % 2]

        def logits(key):
            return LP[(n(logits_full, key) - 1) % 2]

        def trans(key):
            return TP[(n(trans_full, key) - 1) % 2]

        def weights(w, rows, c0, width=P):
            return w[rows[0] * P:(rows[-1] + 1) * P, c0:c0 + width].rearrange("(k p) c -> p k c", p=P)

        def proj_jobs(b, kind, tiles, width=P):
            return [((kind, b, m), weights(w_in, range(KT), COL[kind] + m * P, width)) for m in range(tiles)]

        def ffn_jobs(b, part):
            jobs = []
            for i in part:
                jobs.append((("fg", b, i), weights(io["w_ffn_gate"][0], range(KT), i * P)))
                jobs.append((("fu", b, i), weights(io["w_ffn_up"][0], range(KT), i * P)))
            for m in range(KT):
                jobs.append((("fd", b, part[0], m), weights(io["w_ffn_down"][0], part, m * P)))
            return jobs

        def jobs_of(b):
            jobs = proj_jobs(b, "iq", ET) + proj_jobs(b, "ikw", 1, HD + HEADS) + proj_jobs(b, "lat", 1)
            jobs += proj_jobs(b, "gate", 2 * KT) + proj_jobs(b, "av", 1) + proj_jobs(b, "ak", 1)
            jobs += proj_jobs(b, "aq", ET) + proj_jobs(b, "bq", ET)
            for m in range(KT):
                for s, w in enumerate(("w_branch_a", "w_branch_b")):
                    jobs.append((("br", b, m, s), weights(io[w][0], range(ET), m * P)))
            for m in range(KT):
                jobs.append((("wo", b, m), weights(io["w_out"][0], range(KT), m * P)))
            for part in PARTS:
                jobs += ffn_jobs(b, part)
            return jobs

        JOBS = [job for b in range(NB) for job in jobs_of(b)]

        def chunks(width):
            return [(c, min(LGW, width - c)) for c in range(0, width, LGW)]

        def halves(c, w):
            return [(a, min(ROWS, c + w - a)) for a in range(c, c + w, ROWS)]

        def units(b, kind):
            return [(b, kind, j, h) for j in range(JT) for h in range(0, HEADS, 4 if kind == "a" else 1)]

        def key_tiles(b, kind, j):
            t = b * JT + j
            if kind == "a":
                return (1, t) if t == 0 else (2, t - 1)
            return t + 1, 0

        def chunks_of(u):
            b, kind, j, _ = u
            return [(0, LGW)] if kind == "a" else chunks(key_tiles(b, kind, j)[0] * P)

        def beside(b, kind, i):
            m = i - (len(units(b, kind)) - ET)
            return m if kind == "a" and m >= 0 else None

        def pieces(u):
            return 2 if u[1] == "a" else len(chunks_of(u))

        def piece_of(u, tile):
            return (tile[0] % 4) // 2 if u[1] == "a" else tile[2] // LGW

        def last_of_rows(b, kind):
            items = units(b, kind)
            return [i for i, u in enumerate(items) if i + 1 == len(items) or items[i + 1][2] != u[2]]

        def groups(u):
            b, kind, j, h0 = u
            tiles = [(h0 + i, kt, i * BAND + kt * P) for i in range(4 if kind == "a" else 1)
                     for kt in range(key_tiles(b, kind, j)[0])]
            return [tiles[i:i + 4] for i in range(0, len(tiles), 4)]

        def searched(b):
            return [j for j in range(JT) if b * JT + j >= TK]

        def search_halves(b):
            js = searched(b)
            return js[:len(js) // 2], js[len(js) // 2:]

        STEPS, TURN = 31, 6
        first_step = [0]
        first_count = [0]
        for b in range(NB):
            steps = STEPS if searched(b) else 0
            first_step.append(first_step[-1] + steps)
            first_count.append(first_count[-1] + steps * len(search_halves(b)[1]))

        block = ctx.enter_context(nc.Block())

        @block.sync
        def _(sp):
            consts = [(IDENT[:, :], io["ident"]), (HOT[:, :], io["hot"]), (BANDM[:, :], io["band"]),
                      (RELB[:, :], io["rel_bias"]), (GKV[:, :], io["kv_norm_g"].rearrange("a p -> p a")),
                      (SINK[:, :], io["sinks"][0].partition_broadcast(P)), (WU[:, 2 * HD:3 * HD], io["w_uv"][0])]
            consts += [(WU[:, HD * i:HD * (i + 1)], io["w_uk"][0]) for i in range(2)]
            for g, name in ((G1, "norm1_g"), (G2, "norm2_g")):
                consts.append((g[:, :], io[name][0].rearrange("(k p) -> p k", p=P)))
            consts.append((GF[:, :], io["norm_f_g"].rearrange("(k p) -> p k", p=P)))
            for i, (dst, src) in enumerate(consts):
                made(const_in, i, 16)
                sp.dma_start(dst, src, allow_slow_non_contiguous=True).then_inc(const_in, 16)
            sp.wait_ge(ftab_ready, n(ftab_ready, 2 * HEADS - 1))
            ft = io["ft"]
            sp.dma_start(ft.rearrange("h p r -> p h r"), FTAB[:, :, :]).then_inc(ftab_out, 16)
            sp.wait_ge(ftab_out, 16)
            for s, tab in enumerate((TABA, TABB)):
                skew = bass.AP(ft.tensor, s * HEADS * P * FTW + P - 1, [[FTW - 1, P], [P * FTW, HEADS], [1, BAND]])
                sp.dma_start(tab[:, :, :], skew).then_inc(taba_in, 16)

            def load_x(b):
                for j in range(JT):
                    made(x_in[j], (b, 0), 16)
                    sp.dma_start(XN[:, j, :], x[0, b * ROWS + j * P:b * ROWS + (j + 1) * P, :]).then_inc(x_in[j], 16)

            load_x(0)
            for i, (key, src) in enumerate(JOBS):
                k, width = src.shape[1], src.shape[2]
                if i >= 2:
                    sp.wait_ge(w_split, i - 1)
                sp.dma_start(WRAW[i % 2][:, 0:k, 0:width], src).then_inc(w_in_sem[i % 2], 16)
                if key[0] == "iq" and key[1] and key[2] == 1:
                    b = key[1]
                    sp.wait_ge(bank_full, n(bank_full, ("yt", b - 1, JT - 1, D // ROWS - 1)))
                    load_x(b)
            for j in range(JT):
                sp.wait_ge(out_done[j], 16 * NB)

        @block.gpsimd
        def _(pool):
            for i, (key, src) in enumerate(JOBS):
                k, width = src.shape[1], src.shape[2]
                raw = WRAW[i % 2][:, 0:k, 0:width]
                hi, lo = WHI[i % 2][:, 0:k, 0:width], WLO[i % 2][:, 0:k, 0:width]
                pool.wait_ge(w_in_sem[i % 2], 16 * (i // 2 + 1))
                if i >= 2:
                    pool.wait_ge(bank_full, n(bank_full, JOBS[i - 2][0]))
                nc.gpsimd.tensor_scalar(hi, raw, 1.0, 1.0, ALU.mult, ALU.mult).then_inc(w_hi, 1)
                pool.wait_ge(w_hi, i + 1)
                nc.gpsimd.tensor_tensor(lo, raw, hi.bitcast(f32), ALU.subtract).then_inc(w_split, 1)

        @block.tensor
        def _(pe):
            releases = dict(bank=[], logits=[], trans=[])
            job_no = [0]

            def take(kind, sem_, key, use=None):
                uses = releases[kind]
                if len(uses) >= 2:
                    pe.wait_ge(uses[-2][0], n(*uses[-2]))
                C.seen[(kind + " use", use)] = len(uses)
                uses.append((sem_, key))
                return (BANK if kind == "bank" else LP if kind == "logits" else TP)[(len(uses) - 1) % 2]

            def three(dst, whi, wlo, mhi, mlo, first, last):
                nc.tensor.matmul(dst, whi, mhi, start=first, stop=False)
                nc.tensor.matmul(dst, whi, mlo, start=False, stop=False)
                return nc.tensor.matmul(dst, wlo, mhi, start=False, stop=last)

            def job(mhi, mlo, release, add=None, ready=None):
                i = job_no[0]
                key, src = JOBS[i]
                job_no[0] += 1
                k, width = src.shape[1], src.shape[2]
                dst = take("bank", *release, key)[0:width, :]
                pe.wait_ge(w_split, i + 1)
                for s in range(k):
                    if ready is not None:
                        pe.wait_ge(h_split, n(h_split, (*ready, s)))
                    last = three(dst, WHI[i % 2][:, s, 0:width], WLO[i % 2][:, s, 0:width], mhi[:, s, :], mlo[:, s, :],
                                 s == 0, s == k - 1)
                if add is not None:
                    last = add(dst)
                last.then_inc(bank_full, made(bank_full, key))

            def square_sums(key, squares, ready, release):
                dst = take("logits", *release)[:, 0:ROWS]
                for k in range(squares.shape[1]):
                    yield
                    pe.wait_ge(ready, n(ready, (*key[1:], k)))
                    last = nc.tensor.matmul(dst, ONES[:, :], squares[:, k, :], start=(k == 0),
                                            stop=(k == squares.shape[1] - 1))
                last.then_inc(logits_full, made(logits_full, key))
                yield

            pe.wait_ge(const_in, n(const_in, 11))
            for h in range(2 * HEADS):
                dst = take("bank", ftab_ready, h, ("ft", h))
                c = FTW * (h // HEADS)
                nc.tensor.matmul(dst[:, 0:FTW], RELB[:, h:h + 1].to_broadcast([BUCKETS, P]), HOT[:, c:c + FTW],
                                 start=True, stop=True).then_inc(bank_full, made(bank_full, ("ft", h)))
            pe.wait_ge(ones_set, 1)

            def attend(b, kind):
                items = units(b, kind)
                ends = last_of_rows(b, kind)

                def qk(u):
                    _, _, j, h0 = u
                    tiles, first = key_tiles(b, kind, j)
                    for c, w in chunks_of(u):
                        dst = take("logits", masked, (u, c))
                        if kind == "a":
                            v = tiles * P
                            s0 = (first - b * JT + 1) * P
                            g = h0 // (HEADS // KVH)
                            for i in range(4):
                                d, q = dst[:, i * BAND:i * BAND + v], Q[:, h0 + i, j * P:(j + 1) * P]
                                nc.tensor.matmul(d, q, AKhi[:, g, s0:s0 + v], start=True, stop=False)
                                last = nc.tensor.matmul(d, q, AKlo[:, g, s0:s0 + v], start=False, stop=True)
                                if i == 3:
                                    last.then_inc(logits_full, made(logits_full, (u, c)))
                                if i % 2:
                                    yield
                            continue
                        q = Q[:, h0, j * P:(j + 1) * P]
                        for a, v in halves(c, w):
                            d = dst[:, a - c:a - c + v]
                            nc.tensor.matmul(d, q, KBhi[:, a:a + v], start=True, stop=False, skip_group_check=True)
                            last = nc.tensor.matmul(d, q, KBlo[:, a:a + v], start=False, stop=True, skip_group_check=True)
                            for kt in range(max(0, tiles - 2), tiles):
                                if a <= kt * P < a + v:
                                    col = (kt - (tiles - 2)) * P
                                    last = nc.tensor.matmul(dst[:, kt * P - c:(kt + 1) * P - c], IDENT[:, :],
                                                            TABB[:, h0, col:col + P], start=False, stop=True,
                                                            skip_group_check=True)
                            if a + v == c + w:
                                last.then_inc(logits_full, made(logits_full, (u, c)))
                            yield

                def transposes(i, g):
                    u = items[i]
                    grp = groups(u)[g]
                    dst = take("trans", pt_ready, (u, g))
                    s = piece_of(u, grp[-1])
                    if g == 0 or s != piece_of(u, groups(u)[g - 1][-1]):
                        pe.wait_ge(probs, n(probs, (u, s)))
                    for e, (_, _, col) in enumerate(grp):
                        last = nc.tensor.transpose(dst[:, e, :], LG[kind][i % 4][:, col:col + P], IDENT[:, :])
                    last.then_inc(trans_full, made(trans_full, (u, g)))

                def values(i, g):
                    u = items[i]
                    _, _, j, h0 = u
                    tiles, first = key_tiles(b, kind, j)
                    if h0 % 4 == 0 and g == 0:
                        values.bank = take("bank", o_step, ("o", b, kind, j, h0 // 4, 2), ("o", b, kind, j, h0 // 4))
                    t = n(pt_hi, (u, g)) - 1
                    pe.wait_ge(pt_ready, n(pt_ready, (u, g)))
                    for e, (h, kt, _) in enumerate(groups(u)[g]):
                        dst = values.bank[:, (h % 4) * P:(h % 4 + 1) * P]
                        v = VA[:, first + kt - b * JT + 1, h // (HEADS // KVH), :] if kind == "a" else VB[:, kt, :]
                        nc.tensor.matmul(dst, PThi[kind][t % 2][:, e, :], v, start=(kt == 0), stop=False, skip_group_check=True)
                        last = nc.tensor.matmul(dst, PTlo[kind][t % 2][:, e, :], v, start=False, stop=(kt == tiles - 1),
                                                skip_group_check=True)
                    last.then_inc(values_done, made(values_done, (u, g)))

                def out_transposes(j):
                    dst = take("trans", ot_ready, (b, kind, j))
                    pe.wait_ge(o_ready, n(o_ready, (b, kind, j, 1)))
                    for e in range(ET):
                        last = nc.tensor.transpose(dst[:, e, :],
                                                   ON[kind][j % 2][:, 2 * e:2 * e + 2, :].rearrange("p h d -> p (h d)"), IDENT[:, :])
                    last.then_inc(trans_full, made(trans_full, ("on", b, kind, j)))

                for u in items[:3]:
                    for _ in qk(u):
                        pass
                transposes(0, 0)
                for i, u in enumerate(items):
                    ahead = qk(items[i + 3]) if i + 3 < len(items) else iter(())
                    end = len(groups(u)) - 1
                    for g in range(end + 1):
                        if g < end:
                            transposes(i, g + 1)
                        elif i + 1 < len(items):
                            transposes(i + 1, 0)
                        next(ahead, None)
                        if g == end or kind == "b" and len(chunks_of(u)) == 1:
                            for _ in ahead:
                                pass
                        if g == 0 and beside(b, kind, i) is not None:
                            job(HThi, HTlo, (q_ready, (b, "bq", beside(b, kind, i), 1)))
                        values(i, g)
                    if i - 2 in ends:
                        out_transposes(items[i - 2][2])
                for i in ends:
                    if i + 2 >= len(items):
                        out_transposes(items[i][2])

            for b in range(NB):
                sums = square_sums(("ss", b, 0), SQ, sq_ready, (var_ready, (b, 0)))
                next(sums)
                for k in range(KT):
                    dst = take("bank", xt_ready, (b, k), ("xt", b, k))
                    for j in range(JT):
                        if k == 0:
                            pe.wait_ge(x_in[j], n(x_in[j], (b, 0)))
                        last = nc.tensor.transpose(dst[:, j * P:(j + 1) * P], XN[:, j, k * P:(k + 1) * P], IDENT[:, :])
                    last.then_inc(bank_full, made(bank_full, ("xt", b, k)))
                    if k >= 2:
                        next(sums)
                for _ in sums:
                    pass
                for m in range(ET):
                    job(HThi, HTlo, (q_ready, (b, "iq", m, 1)), ready=(b, 0) if m == 0 else None)
                job(HThi, HTlo, (kw_ready, b))
                job(HThi, HTlo, (sq_ready, (b, "kv", 0)))
                for _ in square_sums(("kvss", b, "kv"), LSQ[:, :].rearrange("p (k r) -> p k r", k=1), sq_ready,
                                     (var_ready, (b, "kv"))):
                    pass
                pe.wait_ge(kw_ready, n(kw_ready, b))
                dst = take("bank", iw_ready, b, ("iwt", b))
                for j in range(JT):
                    last = nc.tensor.transpose(dst[:, j * HEADS:(j + 1) * HEADS], IWT[:, j * P:(j + 1) * P],
                                               IDENT[0:HEADS, 0:HEADS])
                last.then_inc(bank_full, made(bank_full, ("iwt", b)))
                pe.wait_ge(lat_split, n(lat_split, b))
                pe.wait_ge(wu_ready, 2)
                dst = take("bank", k_ready, (b, "kb", 0), ("kb", b))
                three(dst[:, :], WUKhi[:, :], WUKlo[:, :], LThi[:, :], LTlo[:, :], True, True
                      ).then_inc(bank_full, made(bank_full, ("kb", b)))
                dst = take("bank", v_ready, (b, "vb", 0), ("vb", b))
                for j in range(JT):
                    last = three(dst[:, j * HD:(j + 1) * HD], LThi[:, j * P:(j + 1) * P], LTlo[:, j * P:(j + 1) * P],
                                 WUVhi[:, :], WUVlo[:, :], True, True)
                last.then_inc(bank_full, made(bank_full, ("vb", b)))
                pe.wait_ge(q_ready, n(q_ready, (b, "iq", ET - 1, 1)))
                pe.wait_ge(k_ready, n(k_ready, (b, "ki", 1)))
                for j in searched(b):
                    for h in range(HEADS):
                        for c, w in chunks((b * JT + j + 1) * P):
                            dst = take("logits", relu_ready, (b, j, h, c))
                            for a, v in halves(c, w):
                                q = Q[:, h, j * P:(j + 1) * P]
                                nc.tensor.matmul(dst[:, a - c:a - c + v], q, KIhi[:, a:a + v], start=True, stop=False)
                                last = nc.tensor.matmul(dst[:, a - c:a - c + v], q, KIlo[:, a:a + v], start=False, stop=True)
                            last.then_inc(logits_full, made(logits_full, ("idx", b, j, h, c)))
                for m in range(2 * KT):
                    job(HThi, HTlo, (gate_ready, (b, m)))
                job(HThi, HTlo, (vat_ready, b))
                job(HThi, HTlo, (kat_ready, b))
                for m in range(ET):
                    job(HThi, HTlo, (qat_ready, (b, m)) if m < 2 else (q_ready, (b, "aq", m, 1)))
                pe.wait_ge(vat_ready, n(vat_ready, b))
                dst = take("bank", v_ready, (b, "va", 0), ("va", b))
                for j in range(JT):
                    last = nc.tensor.transpose(dst[:, j * P:(j + 1) * P], VAT[:, j * P:(j + 1) * P], IDENT[:, :])
                last.then_inc(bank_full, made(bank_full, ("va", b)))
                pe.wait_ge(q_ready, n(q_ready, (b, "aq", ET - 1, 1)))
                pe.wait_ge(k_ready, n(k_ready, (b, "ak", 2 * KVH - 1)))
                pe.wait_ge(v_ready, n(v_ready, (b, "va", 0)))
                attend(b, "a")
                pe.wait_ge(q_ready, n(q_ready, (b, "bq", ET - 1, 1)))
                pe.wait_ge(k_ready, n(k_ready, (b, "kb", 0)))
                pe.wait_ge(v_ready, n(v_ready, (b, "vb", 0)))
                pe.wait_ge(taba_in, 32)
                attend(b, "b")
                pe.wait_ge(os_ready, n(os_ready, (b, 1)))
                for m in range(KT):
                    for s in range(2):
                        job(OThi[s], OTlo[s], (gated, (b, m, s)))
                pe.wait_ge(m_split, n(m_split, (b, KT - 1)))
                sums = square_sums(("ss", b, 1), SQ, sq_ready, (var_ready, (b, 1)))
                next(sums)
                for m in range(KT):
                    def add_x(dst):
                        for j in range(JT):
                            if m == 0:
                                pe.wait_ge(xr_in[j], n(xr_in[j], b))
                            last = nc.tensor.matmul(dst[:, j * P:(j + 1) * P], XR[:, j, m * P:(m + 1) * P], IDENT[:, :],
                                                    start=False, stop=True, skip_group_check=True)
                        return last
                    job(MGhi, MGlo, (sq_ready, (b, 1, m)), add_x)
                    if m:
                        next(sums)
                for _ in sums:
                    pass
                for part in PARTS:
                    for i in part:
                        job(H2hi, H2lo, (silu_ready, (b, i)), ready=(b, 1) if i == 0 else None)
                        job(H2hi, H2lo, (ff_ready, (b, i)))
                    pe.wait_ge(ff_split, n(ff_split, (b, part[-1])))
                    if part is PARTS[-1]:
                        sums = square_sums(("ss", b, 2), SQ, sq_ready, (var_ready, (b, 2)))
                        next(sums)
                    for m in range(KT):
                        job(FFhi, FFlo, (added, (b, part[0], m)))
                        if part is PARTS[-1] and m >= 2:
                            next(sums)
                for _ in sums:
                    pass
                for j in range(JT):
                    for half in range(D // ROWS):
                        dst = take("bank", (outn_left, outn_right)[half], (b, j, half), ("yt", b, j, half))
                        for k in range(4):
                            kk = half * 4 + k
                            if j == 0:
                                pe.wait_ge(y_ready, n(y_ready, (b, kk)))
                            last = nc.tensor.transpose(dst[:, k * P:(k + 1) * P], X1T[:, kk, j * P:(j + 1) * P], IDENT[:, :])
                        last.then_inc(bank_full, made(bank_full, ("yt", b, j, half)))

        @block.scalar
        def _(act):
            SCALE = HD ** -0.5

            def full(key):
                act.wait_ge(bank_full, n(bank_full, key))
                return bank(key)

            def root(which):
                act.wait_ge(var_ready, n(var_ready, which))
                nc.scalar.activation(RV[:, :], RV[:, :], ACT.Sqrt).then_inc(std_ready, made(std_ready, which))

            def round_h(b, s, src, dst):
                for k in range(KT):
                    act.wait_ge(h_ready, n(h_ready, (b, s, k)))
                    nc.scalar.copy(dst[:, k, :], src[:, k, :]).then_inc(h_hi, made(h_hi, (b, s, k)))

            def q_heads(b, kind, m):
                bk = QAT[:, m, :] if kind == "aq" and m < 2 else full((kind, b, m))
                for s in range(2):
                    r = slice(s * HD, (s + 1) * HD)
                    nc.scalar.mul(Q[r, 2 * m + s, :], bk[r, :], SCALE).then_inc(q_hi, made(q_hi, (b, kind, m, s)))

            for h in range(2 * HEADS):
                bk = full(("ft", h))
                nc.scalar.copy(FTAB[:, h, :], bk[:, 0:FTW]).then_inc(ftab_ready, made(ftab_ready, h))
            act.wait_ge(const_in, n(const_in, 11))
            nc.scalar.copy(WUKhi[:, :], WU[:, 0:2 * HD]).then_inc(wu_hi, 1)
            nc.scalar.copy(WUVhi[:, :], WU[:, 2 * HD:3 * HD]).then_inc(wu_hi, 1)

            def attend(b, kind):
                items = units(b, kind)
                ot = OTA if kind == "a" else OTB
                ends = last_of_rows(b, kind)

                def exps(i, s):
                    if i >= len(items) or s >= pieces(items[i]):
                        return
                    u = items[i]
                    _, _, j, h0 = u
                    w = key_tiles(b, kind, j)[0] * P
                    if s == 0:
                        act.wait_ge(negmax, n(negmax, u))
                    if kind == "b":
                        c, cw = chunks_of(u)[s]
                        lg = LG[kind][i % 4][:, c:c + cw]
                        last = nc.scalar.activation(lg, lg, ACT.Exp, bias=NM[:, i % 4, 0:1],
                                                    accum_out=(ES if s else RS)[:, j % 2, h0:h0 + 1])
                    else:
                        if s == 0:
                            nc.scalar.activation(ES[:, j % 2, h0:h0 + 4], SN[:, i % 4, :], ACT.Exp)
                        for e in (2 * s, 2 * s + 1):
                            lg = LG[kind][i % 4][:, e * BAND:e * BAND + w]
                            last = nc.scalar.activation(lg, lg, ACT.Exp, bias=NM[:, i % 4, e:e + 1],
                                                        accum_out=RS[:, j % 2, h0 + e:h0 + e + 1])
                    last.then_inc(probs, made(probs, (u, s)))

                def out_copy(j):
                    act.wait_ge(trans_full, n(trans_full, ("on", b, kind, j)))
                    nc.scalar.copy(ot[:, :, j * P:(j + 1) * P], trans(("on", b, kind, j))[:, :, :]
                                   ).then_inc(ot_ready, made(ot_ready, (b, kind, j)))

                exps(0, 0)
                exps(0, 1)
                exps(1, 0)
                for i, u in enumerate(items):
                    grps = groups(u)
                    for g, grp in enumerate(grps):
                        key = (u, g)
                        t = n(pt_hi, key) - 1
                        act.wait_ge(trans_full, n(trans_full, key))
                        if pt_last[t % 2] is not None:
                            act.wait_ge(values_done, n(values_done, pt_last[t % 2]))
                        pt_last[t % 2] = key
                        w = len(grp)
                        nc.scalar.copy(PThi[kind][t % 2][:, 0:w, :], trans(key)[:, 0:w, :]).then_inc(pt_hi, made(pt_hi, key))
                        if g == 0:
                            exps(i + 1, 1)
                            if i - 3 in ends:
                                out_copy(items[i - 3][2])
                        if g == min(2, len(grps) - 1):
                            exps(i + 2, 0)
                    if beside(b, kind, i) is not None:
                        q_heads(b, "bq", beside(b, kind, i))
                for i in ends:
                    if i + 3 >= len(items):
                        out_copy(items[i][2])

            pt_last = [None, None]
            for b in range(NB):
                rows = slice(b * ROWS, (b + 1) * ROWS)
                for k in range(KT):
                    act.wait_ge(xt_ready, n(xt_ready, (b, k)))
                    nc.scalar.activation(SQ[:, k, :], XT[:, k, :], ACT.Square).then_inc(sq_ready, made(sq_ready, (b, 0, k)))
                root((b, 0))
                round_h(b, 0, XT, HThi)
                for m in range(ET):
                    q_heads(b, "iq", m)
                bk = full(("ikw", b, 0))
                for s in range(2):
                    nc.scalar.copy(KIhi[s * HD:(s + 1) * HD, rows], bk[0:HD, :]).then_inc(k_hi, made(k_hi, (b, "ki", s)))
                act.wait_ge(k_ready, n(k_ready, (b, "ki", 1)))
                nc.scalar.mul(IWT[:, :], bk[HD:HD + HEADS, :], HEADS ** -0.5).then_inc(kw_ready, made(kw_ready, b))
                bk = full(("lat", b, 0))
                nc.scalar.copy(LT[:, :], bk[:, :]).then_inc(lat_ready, made(lat_ready, (b, 0)))
                nc.scalar.activation(LSQ[:, :], bk[:, :], ACT.Square).then_inc(sq_ready, made(sq_ready, (b, "kv", 0)))
                root((b, "kv"))
                act.wait_ge(lat_norm, n(lat_norm, b))
                nc.scalar.copy(LThi[:, :], LT[:, :]).then_inc(lat_hi, made(lat_hi, b))
                bk = full(("kb", b))
                nc.scalar.copy(KBhi[:, rows], bk[:, :]).then_inc(k_hi, made(k_hi, (b, "kb", 0)))
                bk = full(("vb", b))
                nc.scalar.copy(VB[:, b * JT:(b + 1) * JT, 0:HD], bk[:, 0:JT * HD].rearrange("p (j d) -> p j d", d=HD)
                               ).then_inc(v_hi, made(v_hi, (b, "vb", 0)))
                act.wait_ge(v_ready, n(v_ready, (b, "vb", 0)))
                for j in searched(b):
                    for h in range(HEADS):
                        for c, w in chunks((b * JT + j + 1) * P):
                            key = (b, j, h, c)
                            g = n(relu_ready, key) - 1
                            if g >= 2:
                                act.wait_ge(score_added, g - 1)
                            act.wait_ge(logits_full, n(logits_full, ("idx",) + key))
                            nc.scalar.activation(RB[:, g % 2, 0:w], logits(("idx",) + key)[:, 0:w], ACT.Relu
                                                 ).then_inc(relu_ready, made(relu_ready, key))
                def count_tiles(it):
                    act.wait_ge(threshold_set, first_step[b] + it + 1)
                    for j in search_halves(b)[1]:
                        w = (b * JT + j + 1) * P
                        nc.scalar.activation(JUNK[:, j, 0:w], SC[:, j, 0:w], ACT.Sign, bias=THR[:, j:j + 1].bitcast(f32),
                                             accum_out=CNT[:, j:j + 1]).then_inc(tiles_counted, 1)

                steps = first_step[b + 1] - first_step[b]
                for m in range(2 * KT):
                    bk = full(("gate", b, m))
                    g = b * KT + m // 2
                    if g >= 1:
                        act.wait_ge(gate_out[m % 2], 16 * g)
                    nc.scalar.activation(GS[:, m % 2, :], bk[:, :], ACT.Sigmoid).then_inc(gate_ready, made(gate_ready, (b, m)))
                    act.wait_ge(gate_ready, n(gate_ready, (b, m)))
                    act.dma_start(io["gates"][m], GS[:, m % 2, :]).then_inc(gate_out[m % 2], 16)
                    for it in range(steps * max(0, m - 2) // (2 * KT - 2), steps * max(0, m - 1) // (2 * KT - 2)):
                        count_tiles(it)
                if b:
                    nc.scalar.copy(AKhi[:, :, 0:P], AKhi[:, :, JT * P:(JT + 1) * P])
                    nc.scalar.copy(AKlo[:, :, 0:P], AKlo[:, :, JT * P:(JT + 1) * P])
                    nc.scalar.copy(VA[:, 0, :, :], VA[:, JT, :, :]).then_inc(carried, made(carried, b))
                    act.wait_ge(carried, n(carried, b))
                bk = full(("av", b, 0))
                nc.scalar.copy(VAT[:, :], bk[:, :]).then_inc(vat_ready, made(vat_ready, b))
                bk = full(("ak", b, 0))
                nc.scalar.copy(KAT[:, :], bk[:, :]).then_inc(kat_ready, made(kat_ready, b))
                act.wait_ge(kat_ready, n(kat_ready, b))
                for g in range(KVH):
                    for s in range(2):
                        nc.scalar.copy(AKhi[s * HD:(s + 1) * HD, g, P:(JT + 1) * P], KAT[g * HD:(g + 1) * HD, :]
                                       ).then_inc(k_hi, made(k_hi, (b, "ak", 2 * g + s)))
                for m in range(2):
                    act.wait_ge(gate_out[m], 16 * (b + 1) * KT)
                    bk = full(("aq", b, m))
                    nc.scalar.copy(QAT[:, m, :], bk[:, :]).then_inc(qat_ready, made(qat_ready, (b, m)))
                act.wait_ge(qat_ready, n(qat_ready, (b, 1)))
                for j in searched(b):
                    w = (b * JT + j + 1) * P
                    act.wait_ge(dropped, n(dropped, (b, j)))
                    nc.scalar.mul(MASK[:, j, 0:w], SC[:, j, 0:w], NEG).then_inc(mask_ready, made(mask_ready, (b, j)))
                for m in range(ET):
                    q_heads(b, "aq", m)
                bk = full(("va", b))
                nc.scalar.copy(VA[:, 1:JT + 1, :, 0:HD], bk[:, :].rearrange("p (j g d) -> p j g d", g=KVH, d=HD)
                               ).then_inc(v_hi, made(v_hi, (b, "va", 0)))
                attend(b, "a")
                attend(b, "b")
                for s, ot in enumerate((OTA, OTB)):
                    act.wait_ge(ot_ready, n(ot_ready, (b, "b", JT - 1)))
                    nc.scalar.copy(OThi[s][:, :, :], ot[:, :, :]).then_inc(oh_ready, made(oh_ready, (b, s)))

                def load_gates(m):
                    if m >= 2:
                        act.wait_ge(gated, n(gated, (b, m - 2, 1)))
                    for s in range(2):
                        act.dma_start(GL[:, m % 2, s, :], io["gates"][s * KT + m]).then_inc(gate_in[m % 2], 16)
                        made(gate_in[m % 2], (b, m), 16)

                act.wait_ge(masked, n(masked, (units(b, "b")[-1], chunks_of(units(b, "b")[-1])[-1][0])))
                load_gates(0)
                load_gates(1)
                for m in range(KT):
                    act.wait_ge(merged, n(merged, (b, m)))
                    nc.scalar.copy(MGhi[:, m, :], M1[:, m % 2, :]).then_inc(m_hi, made(m_hi, (b, m)))
                    if m + 2 < KT:
                        load_gates(m + 2)
                act.wait_ge(bank_full, n(bank_full, ("br", b, KT - 1, 1)))
                for j in range(JT):
                    made(xr_in[j], b, 16)
                    act.dma_start(XR[:, j, :], x[0, b * ROWS + j * P:b * ROWS + (j + 1) * P, :]).then_inc(xr_in[j], 16)
                act.wait_ge(m_split, n(m_split, (b, KT - 1)))
                for m in range(KT):
                    bk = full(("wo", b, m))
                    nc.scalar.copy(X1T[:, m, :], bk[:, :]).then_inc(x1_ready, made(x1_ready, (b, m)))
                    nc.scalar.activation(SQ[:, m, :], bk[:, :], ACT.Square).then_inc(sq_ready, made(sq_ready, (b, 1, m)))
                root((b, 1))
                round_h(b, 1, H2F, H2hi)
                act.wait_ge(h_split, n(h_split, (b, 1, KT - 1)))
                for part in PARTS:
                    for i in part:
                        bk = full(("fg", b, i))
                        if i >= 2:
                            act.wait_ge(ff_ready, n(ff_ready, (b, i - 2)))
                        nc.scalar.activation(SL[:, i % 2, :], bk[:, :], ACT.Silu).then_inc(silu_ready, made(silu_ready, (b, i)))
                        act.wait_ge(ff_ready, n(ff_ready, (b, i)))
                        nc.scalar.copy(FFhi[:, i - part[0], :], FF[:, i % 2, :]).then_inc(ff_hi, made(ff_hi, (b, i)))
                for m in range(KT):
                    act.wait_ge(added, n(added, (b, PARTS[-1][0], m)))
                    nc.scalar.activation(SQ[:, m, :], X1T[:, m, :], ACT.Square).then_inc(sq_ready, made(sq_ready, (b, 2, m)))
                root((b, 2))
                for j in range(JT):
                    bk = full(("yt", b, j, 0))
                    nc.scalar.copy(OUTN[:, j, 0:ROWS], bk[:, :]).then_inc(outn_left, made(outn_left, (b, j, 0)))
                    act.wait_ge(outn_left, n(outn_left, (b, j, 0)))
                    act.wait_ge(outn_right, n(outn_right, (b, j, 1)))
                    act.dma_start(out[0, b * ROWS + j * P:b * ROWS + (j + 1) * P, :], OUTN[:, j, :]).then_inc(out_done[j], 16)

        @block.vector
        def _(dve):
            SCALE = HD ** -0.5

            def full(key):
                dve.wait_ge(bank_full, n(bank_full, key))
                return bank(key)

            def reciprocal_std(which, key, width):
                dve.wait_ge(logits_full, n(logits_full, key))
                bk = logits(key)[:, 0:ROWS]
                nc.vector.tensor_scalar(RV[:, :], bk, 1.0 / width, EPS, ALU.mult, ALU.add
                                        ).then_inc(var_ready, made(var_ready, which))
                dve.wait_ge(std_ready, n(std_ready, which))
                nc.vector.reciprocal(RV[:, :], RV[:, :]).then_inc(rinv_ready, made(rinv_ready, which))
                dve.wait_ge(rinv_ready, n(rinv_ready, which))

            def normed(b, s, src, dst, gain, hi, lo):
                reciprocal_std((b, s), ("ss", b, s), D)
                for k in range(KT + 2):
                    if k < KT:
                        nc.vector.scalar_tensor_tensor(dst[:, k, :], src[:, k, :], gain[:, k:k + 1], RV[:, :], ALU.mult,
                                                       ALU.mult).then_inc(h_ready, made(h_ready, (b, s, k)))
                    k -= 2
                    if k < 0:
                        continue
                    dve.wait_ge(h_hi, n(h_hi, (b, s, k)))
                    nc.vector.tensor_tensor(lo[:, k, :], dst[:, k, :], hi[:, k, :].bitcast(f32), ALU.subtract
                                            ).then_inc(h_split, made(h_split, (b, s, k)))

            def q_heads(b, kind, m):
                bk = QAT[:, m, :] if kind == "aq" and m < 2 else full((kind, b, m))
                for s in range(2):
                    r, o = slice(s * HD, (s + 1) * HD), slice((1 - s) * HD, (2 - s) * HD)
                    if s == 0:
                        dve.wait_ge(q_hi, n(q_hi, (b, kind, m, 1)))
                    nc.vector.scalar_tensor_tensor(Q[o, 2 * m + s, :], bk[r, :], SCALE, Q[r, 2 * m + s, :].bitcast(f32),
                                                   ALU.mult, ALU.subtract).then_inc(q_ready, made(q_ready, (b, kind, m, s)))

            nc.vector.memset(ONES[:, :], 1.0).then_inc(ones_set, 1)
            dve.wait_ge(const_in, n(const_in, 11))
            dve.wait_ge(wu_hi, 2)
            nc.vector.tensor_tensor(WUKlo[:, :], WU[:, 0:2 * HD], WUKhi[:, :].bitcast(f32), ALU.subtract).then_inc(wu_ready, 1)
            nc.vector.tensor_tensor(WUVlo[:, :], WU[:, 2 * HD:3 * HD], WUVhi[:, :].bitcast(f32), ALU.subtract
                                    ).then_inc(wu_ready, 1)
            dve.wait_ge(taba_in, 32)
            for h in range(HEADS):
                nc.vector.tensor_tensor(TABA[:, h, :], TABA[:, h, :], BANDM[:, :], ALU.add).then_inc(taba_ready, 1)

            step = [0]

            def topk(b):
                js = searched(b)
                own, others = search_halves(b)
                col, own_col, others_col = slice(js[0], JT), slice(own[0], own[-1] + 1), slice(others[0], JT)

                def stepped(ins):
                    step[0] += 1
                    ins.then_inc(topk_step, 1)
                    return step[0]

                def done(ins):
                    dve.wait_ge(topk_step, stepped(ins))

                def count(threshold, op):
                    for j in js:
                        w = (b * JT + j + 1) * P
                        last = stepped(nc.vector.tensor_scalar(JUNK[:, j, 0:w], SC[:, j, 0:w], threshold(j), None,
                                                               op, ALU.add, accum_out=CNT[:, j:j + 1]))
                    dve.wait_ge(topk_step, last)

                count(lambda j: 0.0, ALU.is_ge)
                done(nc.vector.tensor_scalar(TAKE[:, col], CNT[:, col], float(TOPK), -1.0, ALU.is_ge, ALU.add))
                done(nc.vector.tensor_scalar(SIGN[:, col], TAKE[:, col], -2 ** 31, None, ALU.bitwise_or))
                done(nc.vector.tensor_scalar(SIGN[:, others_col], SIGN[:, others_col], -2 ** 31, None, ALU.bitwise_xor))
                stepped(nc.vector.tensor_scalar(PREF[:, col], TAKE[:, col], -1, -2 ** 31, ALU.bitwise_xor, ALU.bitwise_and))
                done(nc.vector.memset(BIT[0][:, :], 2 ** 30))
                each = len(own) + 4 + len(others)

                def search(s0, counted, bit, next_bit):
                    nc.vector.scalar_tensor_tensor(THR[:, others_col], PREF[:, others_col], bit[:, 0:1], SIGN[:, others_col],
                                                   ALU.bitwise_or, ALU.bitwise_xor).then_inc(threshold_set, 1)
                    nc.vector.scalar_tensor_tensor(THR[:, own_col], PREF[:, own_col], bit[:, 0:1], SIGN[:, own_col],
                                                   ALU.bitwise_or, ALU.bitwise_xor).then_inc(topk_step, 1)
                    nc.vector.tensor_scalar(next_bit[:, :], bit[:, :], 1, None, ALU.logical_shift_right
                                            ).then_inc(topk_step, 1)
                    dve.wait_ge(topk_step, s0 + 1)
                    for j in own:
                        w = (b * JT + j + 1) * P
                        nc.vector.tensor_scalar(JUNK[:, j, 0:w], SC[:, j, 0:w], THR[:, j:j + 1].bitcast(f32), None,
                                                ALU.is_ge, ALU.add, accum_out=CNT[:, j:j + 1]).then_inc(topk_step, 1)
                    dve.wait_ge(topk_step, s0 + 2 + len(own))
                    nc.vector.tensor_scalar(TAKE[:, own_col], CNT[:, own_col], float(TOPK), -1.0, ALU.is_ge, ALU.mult
                                            ).then_inc(topk_step, 1)
                    dve.wait_ge(tiles_counted, counted)
                    for j in others:
                        w = (b * JT + j + 1) * P
                        nc.vector.tensor_scalar(TAKE[:, j:j + 1], CNT[:, j:j + 1], float(2 * TOPK - w), -1.0,
                                                ALU.is_ge, ALU.mult).then_inc(topk_step, 1)
                    dve.wait_ge(topk_step, s0 + each - 1)
                    nc.vector.scalar_tensor_tensor(PREF[:, col], TAKE[:, col], bit[:, 0:1], PREF[:, col],
                                                   ALU.bitwise_and, ALU.bitwise_or).then_inc(topk_step, 1)
                    dve.wait_ge(topk_step, s0 + each)

                base = step[0]
                search(base, first_count[b] + len(others), BIT[0], BIT[1])
                with dve.Fori(0, STEPS // TURN) as turn:
                    for i in range(TURN):
                        it = turn * TURN + (1 + i)
                        search(base + it * each, first_count[b] + (it + 1) * len(others), BIT[1 - i % 2], BIT[i % 2])
                step[0] += STEPS * each
                done(nc.vector.tensor_scalar(SIGN[:, others_col], SIGN[:, others_col], -2 ** 31, None, ALU.bitwise_xor))
                done(nc.vector.tensor_tensor(THR[:, col], PREF[:, col], SIGN[:, col], ALU.bitwise_xor))
                count(lambda j: THR[:, j:j + 1].bitcast(f32), ALU.is_gt)
                stepped(nc.vector.tensor_scalar(MORE[:, col], CNT[:, col], float(TOPK), None, ALU.is_ge))
                stepped(nc.vector.tensor_scalar(SHIFT[:, col], CNT[:, col], float(TOPK), None, ALU.is_ge))
                stepped(nc.vector.tensor_scalar(NEED[:, col], CNT[:, col], -1.0, float(TOPK), ALU.mult, ALU.add))
                stepped(nc.vector.tensor_scalar(LOW[:, col], PREF[:, col], 65535, None, ALU.bitwise_and))
                done(nc.vector.tensor_scalar(PREF[:, col], PREF[:, col], 16, None, ALU.logical_shift_right))
                done(nc.vector.tensor_tensor(LOW[:, col], LOW[:, col], MORE[:, col], ALU.add))
                done(nc.vector.tensor_scalar(CARRY[:, col], LOW[:, col], 16, None, ALU.logical_shift_right))
                stepped(nc.vector.tensor_scalar(LOW[:, col], LOW[:, col], 65535, None, ALU.bitwise_and))
                done(nc.vector.tensor_tensor(PREF[:, col], PREF[:, col], CARRY[:, col], ALU.add))
                done(nc.vector.tensor_scalar(PREF[:, col], PREF[:, col], 16, None, ALU.logical_shift_left))
                done(nc.vector.tensor_tensor(PREF[:, col], PREF[:, col], LOW[:, col], ALU.bitwise_or))
                done(nc.vector.tensor_tensor(THR[:, col], PREF[:, col], SIGN[:, col], ALU.bitwise_xor))
                for j in js:
                    w = (b * JT + j + 1) * P
                    thr = THR[:, j:j + 1].bitcast(f32)
                    s, e, c = SC[:, j, 0:w], EQ[:, 0:w], CS[:, 0:w]
                    if j > js[0]:
                        dve.wait_ge(dropped, n(dropped, (b, j - 1)))
                    done(nc.vector.tensor_scalar(e, s, thr, None, ALU.is_equal))
                    done(nc.vector.tensor_tensor_scan(c, e, e, 0.0, ALU.add, ALU.max))
                    if j in others:
                        done(nc.vector.scalar_tensor_tensor(NEED[:, j:j + 1], CS[:, w - 1:w], SHIFT[:, j:j + 1],
                                                            NEED[:, j:j + 1], ALU.mult, ALU.add))
                    done(nc.vector.scalar_tensor_tensor(e, c, NEED[:, j:j + 1], e, ALU.is_le, ALU.mult))
                    nc.vector.scalar_tensor_tensor(s, s, thr, e, ALU.is_le, ALU.subtract
                                                   ).then_inc(dropped, made(dropped, (b, j)))

            def attend(b, kind):
                items = units(b, kind)

                def masks(i, s):
                    if i >= len(items) or s >= pieces(items[i]):
                        return
                    u = items[i]
                    _, _, j, h0 = u
                    w = key_tiles(b, kind, j)[0] * P
                    if s == 0 and i >= 4:
                        before = items[i - 4]
                        dve.wait_ge(trans_full, n(trans_full, (before, len(groups(before)) - 1)))
                    c, cw = chunks_of(u)[0 if kind == "a" else s]
                    dve.wait_ge(logits_full, n(logits_full, (u, c)))
                    src = logits((u, c))
                    if kind == "a":
                        for e in (2 * s, 2 * s + 1):
                            o = e * BAND
                            last = nc.vector.tensor_tensor_reduce(
                                LG[kind][i % 4][:, o:o + w], src[:, o:o + w], TABA[:, h0 + e, BAND - w:BAND], 1.0,
                                SINK[:, h0 + e:h0 + e + 1], ALU.add, ALU.max, MX[:, i % 4, e:e + 1])
                        if s == 0:
                            return
                    else:
                        if s:
                            dve.wait_ge(masked, n(masked, (u, 0)))
                        last = nc.vector.tensor_tensor_reduce(
                            LG[kind][i % 4][:, c:c + cw], src[:, 0:cw], MASK[:, j, c:c + cw], 1.0,
                            MX[:, i % 4, 0:1] if s else LOWEST, ALU.add, ALU.max, MX[:, i % 4, s:s + 1])
                    last.then_inc(masked, made(masked, (u, c)))

                def maxima(i):
                    if i >= len(items):
                        return
                    u = items[i]
                    h0 = u[3]
                    dve.wait_ge(masked, n(masked, (u, chunks_of(u)[-1][0])))
                    if kind == "a":
                        nc.vector.tensor_scalar(NM[:, i % 4, :], MX[:, i % 4, :], -1.0, None, ALU.mult
                                                ).then_inc(o_step, made(o_step, ("nm", u)))
                        last = nc.vector.tensor_tensor(SN[:, i % 4, :], SINK[:, h0:h0 + 4], MX[:, i % 4, :], ALU.subtract)
                    else:
                        s = pieces(u) - 1
                        last = nc.vector.tensor_scalar(NM[:, i % 4, 0:1], MX[:, i % 4, s:s + 1], -1.0, None, ALU.mult)
                    last.then_inc(negmax, made(negmax, u))

                def outputs(j, g, u):
                    key = ("o", b, kind, j, g)
                    hs = slice(4 * g, 4 * g + 4)
                    p = j % 2
                    dve.wait_ge(values_done, n(values_done, (u, len(groups(u)) - 1)))
                    if pieces(u) > 1:
                        nc.vector.tensor_tensor(RS[:, p, hs], RS[:, p, hs], ES[:, p, hs], ALU.add
                                                ).then_inc(o_step, made(o_step, key + (3,)))
                        yield
                        dve.wait_ge(o_step, n(o_step, key + (3,)))
                    nc.vector.reciprocal(RR[:, p, hs], RS[:, p, hs]).then_inc(o_step, made(o_step, key + (0,)))
                    yield
                    dve.wait_ge(o_step, n(o_step, key + (0,)))
                    bk = bank(key)[:, :].rearrange("p (h d) -> p h d", h=4)
                    r = RR[:, p, hs].unsqueeze(2).to_broadcast([P, 4, HD])
                    nc.vector.tensor_tensor(OA[kind][:, :, :], bk[:, :, 0:HD], r, ALU.mult
                                            ).then_inc(o_step, made(o_step, key + (1,)))
                    nc.vector.tensor_tensor(OB[kind][:, :, :], bk[:, :, HD:P], r, ALU.mult
                                            ).then_inc(o_step, made(o_step, key + (2,)))
                    yield
                    dve.wait_ge(o_step, n(o_step, key + (2,)))
                    if j >= 2:
                        dve.wait_ge(trans_full, n(trans_full, ("on", b, kind, j - 2)))
                    nc.vector.tensor_tensor(ON[kind][p][:, hs, :], OA[kind][:, :, :], OB[kind][:, :, :], ALU.add
                                            ).then_inc(o_ready, made(o_ready, (b, kind, j, g)))
                    yield
                    dve.wait_ge(o_ready, n(o_ready, (b, kind, j, g)))

                masks(0, 0)
                masks(0, 1)
                maxima(0)
                masks(1, 0)
                masks(1, 1)
                maxima(1)
                masks(2, 0)
                due = iter(())
                for i, u in enumerate(items):
                    _, _, j, h0 = u
                    for g, grp in enumerate(groups(u)):
                        key = (u, g)
                        t, w = n(pt_hi, key) - 1, len(grp)
                        dve.wait_ge(pt_hi, n(pt_hi, key))
                        nc.vector.tensor_tensor(PTlo[kind][t % 2][:, 0:w, :], trans(key)[:, 0:w, :],
                                                PThi[kind][t % 2][:, 0:w, :].bitcast(f32), ALU.subtract
                                                ).then_inc(pt_ready, made(pt_ready, key))
                        if g == 0:
                            masks(i + 2, 1)
                            next(due, None)
                            maxima(i + 2)
                        if g == min(2, len(groups(u)) - 1):
                            next(due, None)
                            masks(i + 3, 0)
                        next(due, None)
                    for _ in due:
                        pass
                    if beside(b, kind, i) is not None:
                        q_heads(b, "bq", beside(b, kind, i))
                    if kind == "a" or h0 % 4 == 3:
                        due = outputs(j, h0 // 4, u)
                for _ in due:
                    pass

            for b in range(NB):
                rows = slice(b * ROWS, (b + 1) * ROWS)
                if b:
                    for j in range(JT):
                        dve.wait_ge(out_done[j], 16 * b)
                else:
                    dve.wait_ge(ftab_out, 16)
                for k in range(KT):
                    bk = full(("xt", b, k))
                    nc.vector.tensor_copy(XT[:, k, :], bk[:, :]).then_inc(xt_ready, made(xt_ready, (b, k)))
                normed(b, 0, XT, XT, G1, HThi, HTlo)
                for m in range(ET):
                    q_heads(b, "iq", m)
                bk = full(("ikw", b, 0))
                for s in range(2):
                    dve.wait_ge(k_hi, n(k_hi, (b, "ki", 1)))
                    nc.vector.tensor_tensor(KIlo[s * HD:(s + 1) * HD, rows], bk[0:HD, :], KIhi[0:HD, rows].bitcast(f32),
                                            ALU.subtract).then_inc(k_ready, made(k_ready, (b, "ki", s)))
                reciprocal_std((b, "kv"), ("kvss", b, "kv"), P)
                nc.vector.scalar_tensor_tensor(LT[:, :], LT[:, :], GKV[:, 0:1], RV[:, :], ALU.mult, ALU.mult
                                               ).then_inc(lat_norm, made(lat_norm, b))
                bk = full(("iwt", b))
                nc.vector.tensor_copy(IW[:, :, :], bk[:, 0:JT * HEADS].rearrange("p (j h) -> p j h", h=HEADS)
                                      ).then_inc(iw_ready, made(iw_ready, b))
                dve.wait_ge(lat_hi, n(lat_hi, b))
                nc.vector.tensor_tensor(LTlo[:, :], LT[:, :], LThi[:, :].bitcast(f32), ALU.subtract
                                        ).then_inc(lat_split, made(lat_split, b))
                bk = full(("kb", b))
                dve.wait_ge(k_hi, n(k_hi, (b, "kb", 0)))
                nc.vector.tensor_tensor(KBlo[:, rows], bk[:, :], KBhi[:, rows].bitcast(f32), ALU.subtract
                                        ).then_inc(k_ready, made(k_ready, (b, "kb", 0)))
                bk = full(("vb", b))
                dve.wait_ge(v_hi, n(v_hi, (b, "vb", 0)))
                v = VB[:, b * JT:(b + 1) * JT, :]
                nc.vector.tensor_tensor(v[:, :, HD:P], bk[:, 0:JT * HD].rearrange("p (j d) -> p j d", d=HD),
                                        v[:, :, 0:HD].bitcast(f32), ALU.subtract).then_inc(v_ready, made(v_ready, (b, "vb", 0)))
                dve.wait_ge(iw_ready, n(iw_ready, b))
                for j in searched(b):
                    for h in range(HEADS):
                        for c, w in chunks((b * JT + j + 1) * P):
                            key = (b, j, h, c)
                            g = n(relu_ready, key) - 1
                            dve.wait_ge(relu_ready, g + 1)
                            r, s, iw = RB[:, g % 2, 0:w], SC[:, j, c:c + w], IW[:, j, h:h + 1]
                            if h == 0:
                                ins = nc.vector.tensor_scalar(s, r, iw, None, ALU.mult)
                            else:
                                dve.wait_ge(score_added, n(score_added, (b, j, h - 1, c)))
                                ins = nc.vector.scalar_tensor_tensor(s, r, iw, s, ALU.mult, ALU.add)
                            ins.then_inc(score_added, made(score_added, key))
                    w = (b * JT + j + 1) * P
                    dve.wait_ge(score_added, n(score_added, (b, j, HEADS - 1, chunks(w)[-1][0])))
                    nc.vector.memset(SC[0:HD, j, w - HD:w], NEG).then_inc(score_ready, made(score_ready, (b, j)))
                if searched(b):
                    dve.wait_ge(score_ready, n(score_ready, (b, searched(b)[-1])))
                    dve.wait_ge(logits_full, n(logits_full, ("idx", b, JT - 1, HEADS - 1, chunks((b + 1) * ROWS)[-1][0])))
                for j in range(JT):
                    if j not in searched(b):
                        w = (b * JT + j + 1) * P
                        step[0] += 1
                        nc.vector.memset(MASK[:, j, 0:w], 0.0).then_inc(topk_step, 1)
                        dve.wait_ge(topk_step, step[0])
                        nc.vector.memset(MASK[0:HD, j, w - HD:w], NEG).then_inc(mask_ready, made(mask_ready, (b, j)))
                if searched(b):
                    topk(b)
                for m in range(ET):
                    q_heads(b, "aq", m)
                for g in range(KVH):
                    for s in range(2):
                        dve.wait_ge(k_hi, n(k_hi, (b, "ak", 2 * KVH - 1)))
                        hi = AKhi[s * HD:(s + 1) * HD, g, P:(JT + 1) * P]
                        nc.vector.tensor_tensor(AKlo[s * HD:(s + 1) * HD, g, P:(JT + 1) * P], KAT[g * HD:(g + 1) * HD, :],
                                                hi.bitcast(f32), ALU.subtract
                                                ).then_inc(k_ready, made(k_ready, (b, "ak", 2 * g + s)))
                bk = full(("va", b))
                dve.wait_ge(v_hi, n(v_hi, (b, "va", 0)))
                v = VA[:, 1:JT + 1, :, :]
                nc.vector.tensor_tensor(v[:, :, :, HD:P], bk[:, :].rearrange("p (j g d) -> p j g d", g=KVH, d=HD),
                                        v[:, :, :, 0:HD].bitcast(f32), ALU.subtract).then_inc(v_ready, made(v_ready, (b, "va", 0)))
                dve.wait_ge(taba_ready, HEADS)
                attend(b, "a")
                dve.wait_ge(mask_ready, n(mask_ready, (b, JT - 1)))
                attend(b, "b")
                for s, ot in enumerate((OTA, OTB)):
                    dve.wait_ge(oh_ready, n(oh_ready, (b, s)))
                    nc.vector.tensor_tensor(OTlo[s][:, :, :], ot[:, :, :], OThi[s][:, :, :].bitcast(f32), ALU.subtract
                                            ).then_inc(os_ready, made(os_ready, (b, s)))
                dve.wait_ge(os_ready, n(os_ready, (b, 1)))

                def split_m(m):
                    dve.wait_ge(m_hi, n(m_hi, (b, m)))
                    nc.vector.tensor_tensor(MGlo[:, m, :], M1[:, m % 2, :], MGhi[:, m, :].bitcast(f32), ALU.subtract
                                            ).then_inc(m_split, made(m_split, (b, m)))

                for m in range(KT):
                    dve.wait_ge(gate_in[m % 2], n(gate_in[m % 2], (b, m)))
                    if m >= 2:
                        dve.wait_ge(m_split, n(m_split, (b, m - 2)))
                    for s, dst in enumerate((M1, M2)):
                        bk = full(("br", b, m, s))
                        nc.vector.tensor_tensor(dst[:, m % 2, :], bk[:, :], GL[:, m % 2, s, :], ALU.mult
                                                ).then_inc(gated, made(gated, (b, m, s)))
                    dve.wait_ge(gated, n(gated, (b, m, 1)))
                    nc.vector.tensor_tensor(M1[:, m % 2, :], M1[:, m % 2, :], M2[:, m % 2, :], ALU.add
                                            ).then_inc(merged, made(merged, (b, m)))
                    if m:
                        split_m(m - 1)
                split_m(KT - 1)
                normed(b, 1, X1T, H2F, G2, H2hi, H2lo)
                for part in PARTS:
                    for i in part:
                        bk = full(("fu", b, i))
                        dve.wait_ge(silu_ready, n(silu_ready, (b, i)))
                        if i >= 2:
                            dve.wait_ge(ff_split, n(ff_split, (b, i - 2)))
                        nc.vector.tensor_tensor(FF[:, i % 2, :], bk[:, :], SL[:, i % 2, :], ALU.mult
                                                ).then_inc(ff_ready, made(ff_ready, (b, i)))
                        dve.wait_ge(ff_hi, n(ff_hi, (b, i)))
                        nc.vector.tensor_tensor(FFlo[:, i - part[0], :], FF[:, i % 2, :], FFhi[:, i - part[0], :].bitcast(f32),
                                                ALU.subtract).then_inc(ff_split, made(ff_split, (b, i)))
                    for m in range(KT):
                        bk = full(("fd", b, part[0], m))
                        if part[0]:
                            dve.wait_ge(added, n(added, (b, part[0] - SLOTS, m)))
                        nc.vector.tensor_tensor(X1T[:, m, :], bk[:, :], X1T[:, m, :], ALU.add
                                                ).then_inc(added, made(added, (b, part[0], m)))
                reciprocal_std((b, 2), ("ss", b, 2), D)
                for k in range(KT):
                    nc.vector.scalar_tensor_tensor(X1T[:, k, :], X1T[:, k, :], GF[:, k:k + 1], RV[:, :], ALU.mult,
                                                   ALU.mult).then_inc(y_ready, made(y_ready, (b, k)))
                for j in range(JT):
                    bk = full(("yt", b, j, 1))
                    nc.vector.tensor_copy(OUTN[:, j, ROWS:2 * ROWS], bk[:, :]).then_inc(outn_right, made(outn_right, (b, j, 1)))

    return C.seen


def _bucket(rel):
    starts = [8, 12, 16, 23, 32, 46, 64, 91]
    near = np.abs(rel)
    large = 7 + sum((near >= s).astype(np.int64) for s in starts)
    return np.where(rel > 0, BUCKETS // 2, 0) + np.where(near < 8, near, large)


def _constants():
    hot = np.zeros((BUCKETS, 2 * FTW), np.float32)
    r = np.arange(FTW)
    bucket = _bucket(np.minimum(r - (BAND - 1), P - 1))
    hot[bucket, r] = 1.0
    hot[bucket, FTW + r] = 1.0
    hot[FAR_BUCKET, FTW:] -= 1.0
    band = np.zeros((P, BAND), np.float32)
    half = P // 2
    band[:half, :half] = NEG
    band[:half, 3 * half:] = NEG
    band[half:, :P] = NEG
    return {"hot": hot, "band": band, "ident": np.eye(P, dtype=np.float32)}


_INS = ["x", "norm1_g", "w_in", "rel_bias", "sinks", "kv_norm_g", "w_uk", "w_uv", "w_branch_a", "w_branch_b",
        "w_out", "norm2_g", "w_ffn_gate", "w_ffn_up", "w_ffn_down", "norm_f_g"]


def build(nc, shapes, known):
    f32 = mybir.dt.float32
    io = {name: nc.dram_tensor(f"in_{name}", shape, f32, kind="ExternalInput").ap() for name, shape in shapes.items()}
    io["out"] = nc.dram_tensor("out_0", shapes["x"], f32, kind="ExternalOutput").ap()
    io["ft"] = nc.dram_tensor("ft", (2 * HEADS, P, FTW), f32).ap()
    io["gates"] = nc.dram_tensor("gates", (2 * shapes["x"][2] // P, P, ROWS), f32).ap()
    return trunk_program(nc, io, known)


def kernel(**inputs):
    import concourse.bacc as bacc
    from concourse.bass_utils import run_bass_kernel_spmd

    arrays = {name: np.ascontiguousarray(inputs[name]) for name in _INS}
    arrays.update(_constants())
    shapes = {name: a.shape for name, a in arrays.items()}
    counts = build(bacc.Bacc("TRN2", target_bir_lowering=False, num_devices=1), shapes, {})
    nc = bacc.Bacc("TRN2", target_bir_lowering=False, num_devices=1)
    build(nc, shapes, counts)
    r = run_bass_kernel_spmd(nc, [{f"in_{name}": a for name, a in arrays.items()}], core_ids=[0])
    return r.results[0]["out_0"]
```
